# Optimizing a Trainium2 kernel written in Bass

```python
import math
import jax, jax.numpy as jnp
from jax import lax
import numpy as np

D_MODEL = 1024
BATCH = 1
SEQ = 1024
DEPTH = 2

GRID_W = 64
CTX_LEN = 256
N_MIXERS = 3
BLOCK = 128
ROPE_THETA = 10000.0
LN_EPS = 1e-5
RMS_EPS = 1e-6
DN_ALPHA = (2.0 * DEPTH) ** 0.25
DN_BETA = (8.0 * DEPTH) ** -0.25

A_HEADS = 16
A_KV_HEADS = 4
A_GROUP = A_HEADS // A_KV_HEADS
A_HEAD_DIM = D_MODEL // A_HEADS
A_WINDOW = 128
A_Q_COLS = A_HEADS * A_HEAD_DIM
A_KV_COLS = A_KV_HEADS * A_HEAD_DIM
A_IN_COLS = A_Q_COLS + 2 * A_KV_COLS

B_HEADS = 16
B_NOPE = 64
B_ROPE = 32
B_V = 64
B_Q_RANK = 512
B_KV_RANK = 256
B_IN_COLS = B_Q_RANK + B_KV_RANK + B_ROPE

C_HEADS = 8
C_HEAD_DIM = D_MODEL // (2 * C_HEADS)
C_V_DIM = 2 * C_HEAD_DIM
C_IN_COLS = 3 * C_HEADS * 2 * C_HEAD_DIM

N_GROUPS = 4
EXPERTS_PER_GROUP = 8
N_EXPERTS = N_GROUPS * EXPERTS_PER_GROUP
TOP_K = 2
D_EXPERT = 512
MOE_BLOCK = 128

N_A = len(range(0, DEPTH, N_MIXERS))
N_B = len(range(1, DEPTH, N_MIXERS))
N_C = len(range(2, DEPTH, N_MIXERS))

kernel_name = "hybrid_interleaved_diffusion_block"

def layer_norm(x, g, b):
    xf = x.astype(jnp.float32)
    mu = jnp.mean(xf, -1, keepdims=True)
    var = jnp.mean(jnp.square(xf - mu), -1, keepdims=True)
    y = (xf - mu) * lax.rsqrt(var + LN_EPS)
    return (y * g + b).astype(x.dtype)

def rms_norm(x, g):
    xf = x.astype(jnp.float32)
    y = xf * lax.rsqrt(jnp.mean(xf * xf, -1, keepdims=True) + RMS_EPS)
    return (y * g).astype(x.dtype)

def modulate(x, shift, scale):
    return x * (1 + scale) + shift

def axial_rope_tables(n_tokens, rot_dim):
    rows = n_tokens // GRID_W
    row = jnp.broadcast_to(jnp.arange(rows, dtype=jnp.float32)[:, None], (rows, GRID_W)).reshape(-1)
    col = jnp.broadcast_to(jnp.arange(GRID_W, dtype=jnp.float32)[None, :], (rows, GRID_W)).reshape(-1)
    axis_dim = rot_dim // 2
    inv_freq = ROPE_THETA ** (-jnp.arange(0, axis_dim, 2, dtype=jnp.float32) / axis_dim)
    ang_r = row[:, None] * inv_freq
    ang_c = col[:, None] * inv_freq
    return (jnp.cos(ang_r), jnp.sin(ang_r), jnp.cos(ang_c), jnp.sin(ang_c))

def _rotate(x, cos, sin):
    x1, x2 = jnp.split(x, 2, axis=-1)
    return jnp.concatenate([x1 * cos - x2 * sin, x2 * cos + x1 * sin], axis=-1)

def apply_axial_rope(x, tabs):
    cos_r, sin_r, cos_c, sin_c = [t.reshape((t.shape[0],) + (1,) * (x.ndim - 3) + (t.shape[1],)) for t in tabs]
    xr, xc = jnp.split(x.astype(jnp.float32), 2, axis=-1)
    return jnp.concatenate([_rotate(xr, cos_r, sin_r), _rotate(xc, cos_c, sin_c)], -1).astype(x.dtype)

def softmax_with_sink(s, sink):
    m = jnp.maximum(jnp.max(s, -1, keepdims=True), sink)
    p = jnp.exp(s - m)
    return p / (jnp.sum(p, -1, keepdims=True) + jnp.exp(sink - m))

def sweep_query_blocks(fn, q):
    B, S = q.shape[:2]
    qb = jnp.swapaxes(q.reshape((B, S // BLOCK, BLOCK) + q.shape[2:]), 0, 1)
    o = lax.map(fn, qb)
    return jnp.swapaxes(o, 0, 1).reshape(B, S, -1)

def window_gqa_mixer(h, hc, w_in, w_out, sink, rope, with_ctx_out):
    B, S, _ = h.shape
    L = hc.shape[1]
    scale = A_HEAD_DIM ** -0.5

    def project(t):
        n = t.shape[1]
        q, k, v = jnp.split(t @ w_in, [A_Q_COLS, A_Q_COLS + A_KV_COLS], axis=-1)
        return (q.reshape(B, n, A_KV_HEADS, A_GROUP, A_HEAD_DIM),
                k.reshape(B, n, A_KV_HEADS, A_HEAD_DIM),
                v.reshape(B, n, A_KV_HEADS, A_HEAD_DIM))

    q, k, v = project(h)
    qc, kc, vc = project(hc)
    q = apply_axial_rope(q, rope)
    k = apply_axial_rope(k, rope)
    sink_b = sink.astype(jnp.float32).reshape(1, A_KV_HEADS, A_GROUP, 1, 1)
    pad = ((0, 0), (BLOCK, BLOCK), (0, 0), (0, 0))
    k_pad = jnp.pad(k, pad)
    v_pad = jnp.pad(v, pad)
    q_off = jnp.arange(BLOCK)
    k_off = jnp.arange(3 * BLOCK)

    def attend_block(blk):
        start = blk * BLOCK
        qb = lax.dynamic_slice_in_dim(q, start, BLOCK, axis=1)
        kb = lax.dynamic_slice_in_dim(k_pad, start, 3 * BLOCK, axis=1)
        vb = lax.dynamic_slice_in_dim(v_pad, start, 3 * BLOCK, axis=1)
        q_pos = start + q_off
        k_pos = start - BLOCK + k_off
        valid = (jnp.abs(q_pos[:, None] - k_pos[None, :]) <= A_WINDOW) & (k_pos >= 0) & (k_pos < S)
        s_win = jnp.einsum('bqhgd,bkhd->bhgqk', qb, kb).astype(jnp.float32) * scale
        s_win = jnp.where(valid, s_win, -jnp.inf)
        s_ctx = jnp.einsum('bqhgd,bkhd->bhgqk', qb, kc).astype(jnp.float32) * scale
        p = softmax_with_sink(jnp.concatenate([s_win, s_ctx], -1), sink_b).astype(v.dtype)
        o = (jnp.einsum('bhgqk,bkhd->bqhgd', p[..., :3 * BLOCK], vb)
             + jnp.einsum('bhgqk,bkhd->bqhgd', p[..., 3 * BLOCK:], vc))
        return o.reshape(B, BLOCK, A_Q_COLS)

    o = lax.map(attend_block, jnp.arange(S // BLOCK))
    y = jnp.swapaxes(o, 0, 1).reshape(B, S, A_Q_COLS) @ w_out
    yc = None
    if with_ctx_out:
        s = jnp.einsum('bqhgd,bkhd->bhgqk', qc, kc).astype(jnp.float32) * scale
        p = softmax_with_sink(s, sink_b).astype(vc.dtype)
        yc = jnp.einsum('bhgqk,bkhd->bqhgd', p, vc).reshape(B, L, A_Q_COLS) @ w_out
    return y, yc

def mla_mixer(h, hc, w_in, q_norm, kv_norm, w_uq, w_ukv, w_out, rope, with_ctx_out):
    B = h.shape[0]
    scale = (B_NOPE + B_ROPE) ** -0.5

    def project(t, tabs):
        n = t.shape[1]
        c_q, c_kv, k_rope = jnp.split(t @ w_in, [B_Q_RANK, B_Q_RANK + B_KV_RANK], axis=-1)
        q = (rms_norm(c_q, q_norm) @ w_uq).reshape(B, n, B_HEADS, B_NOPE + B_ROPE)
        kv = (rms_norm(c_kv, kv_norm) @ w_ukv).reshape(B, n, B_HEADS, B_NOPE + B_V)
        q_nope, q_rope = jnp.split(q, [B_NOPE], axis=-1)
        k_nope, v = jnp.split(kv, [B_NOPE], axis=-1)
        k_rope = k_rope[:, :, None, :]
        if tabs is not None:
            q_rope = apply_axial_rope(q_rope, tabs)
            k_rope = apply_axial_rope(k_rope, tabs)
        k_rope = jnp.broadcast_to(k_rope, (B, n, B_HEADS, B_ROPE))
        return (jnp.concatenate([q_nope, q_rope], -1), jnp.concatenate([k_nope, k_rope], -1), v)

    def attend(qb, kk, vv):
        s = jnp.einsum('bqhd,bkhd->bhqk', qb, kk).astype(jnp.float32) * scale
        p = jax.nn.softmax(s, axis=-1).astype(vv.dtype)
        o = jnp.einsum('bhqk,bkhd->bqhd', p, vv)
        return o.reshape(o.shape[0], o.shape[1], B_HEADS * B_V)

    q, k, v = project(h, rope)
    qc, kc, vc = project(hc, None)
    k_all = jnp.concatenate([k, kc], axis=1)
    v_all = jnp.concatenate([v, vc], axis=1)
    y = sweep_query_blocks(lambda qb: attend(qb, k_all, v_all), q) @ w_out
    yc = attend(qc, kc, vc) @ w_out if with_ctx_out else None
    return y, yc

def diff_mixer(h, hc, w_in, lam_params, subln, w_out, rope, lambda_init, with_ctx_out):
    B = h.shape[0]
    scale = C_HEAD_DIM ** -0.5

    def project(t):
        n = t.shape[1]
        q, k, v = jnp.split(t @ w_in, 3, axis=-1)
        return (q.reshape(B, n, C_HEADS, 2, C_HEAD_DIM),
                k.reshape(B, n, C_HEADS, 2, C_HEAD_DIM),
                v.reshape(B, n, C_HEADS, C_V_DIM))

    q, k, v = project(h)
    qc, kc, vc = project(hc)
    q = apply_axial_rope(q, rope)
    k = apply_axial_rope(k, rope)
    lp = lam_params.astype(jnp.float32)
    lam = jnp.exp(jnp.sum(lp[0] * lp[1])) - jnp.exp(jnp.sum(lp[2] * lp[3])) + lambda_init

    def attend(qb, kk, vv):
        s = jnp.einsum('bqhid,bkhid->bhiqk', qb, kk).astype(jnp.float32) * scale
        p = jax.nn.softmax(s, axis=-1)
        a = (p[:, :, 0] - lam * p[:, :, 1]).astype(vv.dtype)
        o = jnp.einsum('bhqk,bkhe->bqhe', a, vv)
        o = rms_norm(o, subln) * (1.0 - lambda_init)
        return o.reshape(o.shape[0], o.shape[1], C_HEADS * C_V_DIM)

    k_all = jnp.concatenate([k, kc], axis=1)
    v_all = jnp.concatenate([v, vc], axis=1)
    y = sweep_query_blocks(lambda qb: attend(qb, k_all, v_all), q) @ w_out
    yc = attend(qc, kc, vc) @ w_out if with_ctx_out else None
    return y, yc

def hier_moe(h, w_grp, b_grp, w_rt, b_rt, w_gate, w_up, w_down):
    T, D = h.shape
    logits_g = (h @ w_grp).astype(jnp.float32) + b_grp.astype(jnp.float32)
    p_grp = jax.nn.softmax(logits_g, axis=-1)
    g_sel = jnp.argmax(logits_g, axis=-1).astype(jnp.int32)
    p_g = jnp.take_along_axis(p_grp, g_sel[:, None], axis=-1)
    logits_e = ((h @ w_rt).astype(jnp.float32) + b_rt.astype(jnp.float32)).reshape(T, N_GROUPS, EXPERTS_PER_GROUP)
    logits_in = jnp.take_along_axis(logits_e, g_sel[:, None, None], axis=1)[:, 0]
    top_v, top_i = lax.top_k(logits_in, TOP_K)
    weights = p_g * jax.nn.softmax(top_v, axis=-1)
    expert = g_sel[:, None] * EXPERTS_PER_GROUP + top_i.astype(jnp.int32)

    TK = T * TOP_K
    flat_e = expert.reshape(TK)
    flat_w = weights.reshape(TK)
    flat_t = jnp.repeat(jnp.arange(T, dtype=jnp.int32), TOP_K)
    order = jnp.argsort(flat_e)
    se, st, sw = flat_e[order], flat_t[order], flat_w[order]
    counts = jnp.bincount(flat_e, length=N_EXPERTS)
    padded = (counts + MOE_BLOCK - 1) // MOE_BLOCK * MOE_BLOCK
    pad_end = jnp.cumsum(padded)
    pad_start = pad_end - padded
    start = jnp.cumsum(counts) - counts
    dest = pad_start[se] + jnp.arange(TK, dtype=jnp.int32) - start[se]
    n_blocks = -(-TK // MOE_BLOCK) + N_EXPERTS
    buf_len = n_blocks * MOE_BLOCK
    buf_tok = jnp.full((buf_len,), T, jnp.int32).at[dest].set(st)
    buf_w = jnp.zeros((buf_len,), h.dtype).at[dest].set(sw.astype(h.dtype))
    block_e = jnp.minimum(jnp.searchsorted(pad_end, jnp.arange(n_blocks) * MOE_BLOCK, side='right'),
                          N_EXPERTS - 1).astype(jnp.int32)
    h_pad = jnp.concatenate([h, jnp.zeros((1, D), h.dtype)], axis=0)
    xb = h_pad[buf_tok].reshape(n_blocks, MOE_BLOCK, D)

    def expert_block(args):
        xblk, e = args
        return (jax.nn.silu(xblk @ w_gate[e]) * (xblk @ w_up[e])) @ w_down[e]

    yb = lax.map(expert_block, (xb, block_e)).reshape(buf_len, D)
    out = jnp.zeros((T + 1, D), h.dtype).at[buf_tok].add(yb * buf_w[:, None])
    return out[:T]

def setup_inputs(seed: int = 0) -> dict:
    key = jax.random.key(seed)
    counter = [0]

    def nrm(shape, scale):
        counter[0] += 1
        return jax.random.normal(jax.random.fold_in(key, counter[0]), shape, jnp.float32) * scale

    D = D_MODEL
    return {
        "x": nrm((BATCH, SEQ, D), 1.0),
        "c": nrm((BATCH, D), 1.0),
        "ctx": nrm((BATCH, CTX_LEN, D), 1.0),
        "c_ctx": nrm((D,), 1.0),
        "ada_w": nrm((DEPTH, D, 6 * D), 0.5 * D ** -0.5),
        "ada_b": nrm((DEPTH, 6 * D), 0.02),
        "ln_mix_g": 1.0 + nrm((DEPTH, D), 0.02),
        "ln_mix_b": nrm((DEPTH, D), 0.02),
        "ln_ffn_g": 1.0 + nrm((DEPTH, D), 0.02),
        "ln_ffn_b": nrm((DEPTH, D), 0.02),
        "win_w_in": nrm((N_A, D, A_IN_COLS), D ** -0.5),
        "win_w_out": nrm((N_A, A_Q_COLS, D), A_Q_COLS ** -0.5 * DN_BETA),
        "win_sink": nrm((N_A, A_HEADS), 0.5),
        "mla_w_in": nrm((N_B, D, B_IN_COLS), D ** -0.5),
        "mla_q_norm": 1.0 + nrm((N_B, B_Q_RANK), 0.02),
        "mla_kv_norm": 1.0 + nrm((N_B, B_KV_RANK), 0.02),
        "mla_w_uq": nrm((N_B, B_Q_RANK, B_HEADS * (B_NOPE + B_ROPE)), B_Q_RANK ** -0.5),
        "mla_w_ukv": nrm((N_B, B_KV_RANK, B_HEADS * (B_NOPE + B_V)), B_KV_RANK ** -0.5),
        "mla_w_out": nrm((N_B, B_HEADS * B_V, D), (B_HEADS * B_V) ** -0.5 * DN_BETA),
        "dif_w_in": nrm((N_C, D, C_IN_COLS), D ** -0.5),
        "dif_lambda": nrm((N_C, 4, C_HEAD_DIM), 0.1),
        "dif_subln": 1.0 + nrm((N_C, C_V_DIM), 0.02),
        "dif_w_out": nrm((N_C, C_HEADS * C_V_DIM, D), (C_HEADS * C_V_DIM) ** -0.5 * DN_BETA),
        "moe_w_grp": nrm((DEPTH, D, N_GROUPS), D ** -0.5),
        "moe_b_grp": nrm((DEPTH, N_GROUPS), 0.01),
        "moe_w_rt": nrm((DEPTH, D, N_EXPERTS), D ** -0.5),
        "moe_b_rt": nrm((DEPTH, N_EXPERTS), 0.01),
        "moe_w_gate": nrm((DEPTH, N_EXPERTS, D, D_EXPERT), D ** -0.5),
        "moe_w_up": nrm((DEPTH, N_EXPERTS, D, D_EXPERT), D ** -0.5),
        "moe_w_down": nrm((DEPTH, N_EXPERTS, D_EXPERT, D), D_EXPERT ** -0.5 * DN_BETA),
    }

def reference(x, c, ctx, c_ctx, ada_w, ada_b, ln_mix_g, ln_mix_b, ln_ffn_g, ln_ffn_b,
              win_w_in, win_w_out, win_sink,
              mla_w_in, mla_q_norm, mla_kv_norm, mla_w_uq, mla_w_ukv, mla_w_out,
              dif_w_in, dif_lambda, dif_subln, dif_w_out,
              moe_w_grp, moe_b_grp, moe_w_rt, moe_b_rt, moe_w_gate, moe_w_up, moe_w_down):
    B, S, D = x.shape
    L = ctx.shape[1]
    rope64 = axial_rope_tables(S, A_HEAD_DIM)
    rope32 = axial_rope_tables(S, B_ROPE)
    xc = ctx
    silu_c = jax.nn.silu(c)
    silu_cc = jax.nn.silu(c_ctx)
    for i in range(DEPTH):
        last = i == DEPTH - 1
        kind = i % N_MIXERS
        slot = i // N_MIXERS
        mod = silu_c @ ada_w[i] + ada_b[i]
        mod_c = silu_cc @ ada_w[i] + ada_b[i]
        sh_m, sc_m, g_m, sh_f, sc_f, g_f = jnp.split(mod[:, None, :], 6, axis=-1)
        csh_m, csc_m, cg_m, csh_f, csc_f, cg_f = jnp.split(mod_c, 6, axis=-1)

        h = modulate(x, sh_m, sc_m)
        hc = modulate(xc, csh_m, csc_m)
        if kind == 0:
            y, yc = window_gqa_mixer(h, hc, win_w_in[slot], win_w_out[slot], win_sink[slot], rope64, not last)
        elif kind == 1:
            y, yc = mla_mixer(h, hc, mla_w_in[slot], mla_q_norm[slot], mla_kv_norm[slot], mla_w_uq[slot],
                              mla_w_ukv[slot], mla_w_out[slot], rope32, not last)
        else:
            lambda_init = 0.8 - 0.6 * math.exp(-0.3 * i)
            y, yc = diff_mixer(h, hc, dif_w_in[slot], dif_lambda[slot], dif_subln[slot], dif_w_out[slot],
                               rope64, lambda_init, not last)
        x = layer_norm(DN_ALPHA * x + g_m * y, ln_mix_g[i], ln_mix_b[i])

        h = modulate(x, sh_f, sc_f)
        moe_args = (moe_w_grp[i], moe_b_grp[i], moe_w_rt[i], moe_b_rt[i], moe_w_gate[i], moe_w_up[i], moe_w_down[i])
        if not last:
            xc = layer_norm(DN_ALPHA * xc + cg_m * yc, ln_mix_g[i], ln_mix_b[i])
            hc = modulate(xc, csh_f, csc_f)
            y_all = hier_moe(jnp.concatenate([h.reshape(B * S, D), hc.reshape(B * L, D)], axis=0), *moe_args)
            y = y_all[:B * S].reshape(B, S, D)
            yc = y_all[B * S:].reshape(B, L, D)
            xc = layer_norm(DN_ALPHA * xc + cg_f * yc, ln_ffn_g[i], ln_ffn_b[i])
        else:
            y = hier_moe(h.reshape(B * S, D), *moe_args).reshape(B, S, D)
        x = layer_norm(DN_ALPHA * x + g_f * y, ln_ffn_g[i], ln_ffn_b[i])
    return x


_drawn_inputs = setup_inputs


def setup_inputs(seed=0):
    import zlib

    import numpy as np

    out = dict(_drawn_inputs(seed))
    spreads = {}
    factors = {'ctx': 6.214,
     'c_ctx': 2.958,
     'ada_b': 6.921,
     'win_sink': 64.0,
     'mla_q_norm': 8.0,
     'mla_kv_norm': 8.0,
     'mla_w_uq': 6.668,
     'moe_b_grp': 8.0,
     'moe_b_rt': 8.0}
    for name, (base, spread) in spreads.items():
        noise = np.random.default_rng([zlib.crc32(name.encode()), seed]).standard_normal(out[name].shape)
        drawn = base * np.exp(spread * noise) if base else spread * noise
        out[name] = __import__('jax').numpy.asarray(drawn.astype(out[name].dtype))
    for name, factor in factors.items():
        out[name] = (out[name] * factor).astype(out[name].dtype)
    return out
```

```python
from contextlib import ExitStack

import numpy as np

import concourse.bass as bass
from concourse import mybir
from concourse.alu_op_type import AluOpType as ALU

F32 = mybir.dt.float32
BF16 = mybir.dt.bfloat16
I32 = mybir.dt.int32
ACT = mybir.ActivationFunctionType
AX = mybir.AxisListType.X

P = 128
D = 1024
KD = D // P
SEQ, CTX = 1024, 256
TALL = SEQ + CTX
NT_X, NT_C = SEQ // P, CTX // P
NT_ALL = NT_X + NT_C
BANK = 512
GRID_W = 64
ALPHA = 4.0 ** 0.25
LN_EPS, RMS_EPS = 1e-5, 1e-6

A_HEADS, A_KV, A_GROUP, A_HD = 16, 4, 4, 64
A_QK_CHUNKS = (A_HEADS + A_KV) * A_HD // P
A_SCALE = A_HD ** -0.5

B_HEADS, B_NOPE, B_ROPE, B_V = 16, 64, 32, 64
B_QR, B_KVR = 512, 256
B_QD = B_NOPE + B_ROPE
B_IN = B_QR + B_KVR + B_ROPE
B_SCALE = B_QD ** -0.5

NG, EPG = 4, 8
NE = NG * EPG
DE = 512
KE = DE // P
BIG = 1.0e30
ROUTE = NG + NE


def n_blocks(tiles):
    return tiles * 2 + NE


def rope_angles(rot_dim):
    axis = rot_dim // 2
    inv = (np.float32(10000.0) ** (-np.arange(0, axis, 2, dtype=np.float32) / np.float32(axis))).astype(np.float32)
    pos = np.arange(SEQ)
    row = (pos // GRID_W).astype(np.float32)
    col = (pos % GRID_W).astype(np.float32)
    ang = np.zeros((rot_dim, SEQ), np.float32)
    partner = np.zeros(rot_dim, int)
    sign = np.zeros(rot_dim, np.float32)
    half = axis // 2
    for a, where in enumerate((row, col)):
        for j in range(axis):
            d = a * axis + j
            ang[d] = where * inv[j % half]
            partner[d] = d + half if j < half else d - half
            sign[d] = -1.0 if j < half else 1.0
    return ang, partner, sign


def constant_arrays():
    cols, parts = {}, []

    def add(name, a):
        full = np.zeros((P, a.shape[1]), np.float32)
        full[: a.shape[0]] = a
        at = sum(x.shape[1] for x in parts)
        cols[name] = (at, a.shape[1])
        parts.append(full)

    add("ident", np.eye(P, dtype=np.float32))
    add("ones", np.ones((P, P), np.float32))
    r, c = np.arange(P)[:, None], np.arange(P)[None, :]
    add("before", (r < c).astype(np.float32))
    add("mask", np.concatenate([np.where(c >= r, 0.0, -BIG), np.where(c <= r, 0.0, -BIG)], 1))
    ang, partner, sign = rope_angles(A_HD)
    rot = np.zeros((A_HD, A_HD), np.float32)
    rot[partner, np.arange(A_HD)] = sign
    two = np.zeros((P, P), np.float32)
    two[:A_HD, :A_HD] = rot
    two[A_HD:, A_HD:] = rot
    add("rot_a", two)
    add("cos_a", np.concatenate([np.cos(ang)] * 2, 0))
    add("sin_a", np.concatenate([np.sin(ang)] * 2, 0))
    ang, partner, sign = rope_angles(B_ROPE)
    rot = np.zeros((B_QD, B_QD), np.float32)
    rot[B_NOPE + partner, B_NOPE + np.arange(B_ROPE)] = sign
    add("rot_b", rot)
    add("cos_b", np.concatenate([np.ones((B_NOPE, SEQ)), np.cos(ang)], 0))
    add("sin_b", np.concatenate([np.zeros((B_NOPE, SEQ)), np.sin(ang)], 0))
    add("cos_k", np.cos(ang).T.reshape(NT_X, P, B_ROPE).transpose(1, 0, 2).reshape(P, -1))
    add("sin_k", (np.sin(ang) * sign[:, None]).T.reshape(NT_X, P, B_ROPE).transpose(1, 0, 2).reshape(P, -1))
    add("iota_e", np.broadcast_to(np.arange(NE) - 64.0, (P, NE)))
    add("iota_g", np.broadcast_to(np.arange(NG) - 64.0, (P, NG)))
    add("steps", np.broadcast_to(np.arange(NT_ALL) * float(P), (P, NT_ALL)))
    nb = n_blocks(NT_ALL)
    add("iota_b", np.broadcast_to(np.arange(nb) * 1.0, (P, nb)))
    add("token", np.arange(P)[:, None] + np.arange(NT_ALL)[None, :] * float(P))
    return np.ascontiguousarray(np.concatenate(parts, 1), np.float32), cols


def bcast_last(ap, n):
    return ap.unsqueeze(2).broadcast_to([ap.shape[0], ap.shape[1], n])


def bcast_mid(ap, n):
    return ap.unsqueeze(1).broadcast_to([ap.shape[0], n, ap.shape[1]])


class Chain:

    def __init__(self, eng, sem, base=0):
        self.eng, self.sem, self.base, self.n = eng, sem, base, 0

    def inc(self, instruction):
        self.n += 1
        instruction.then_inc(self.sem, 1)
        return instruction

    def wait(self):
        self.eng.wait_ge(self.sem, self.base + self.n)

    def link(self, instruction):
        self.inc(instruction)
        self.wait()


class Stage:

    settled = None

    def settle(self, eng):
        eng.sem_inc(Stage.settled, 1)

    def __init__(self, nc, name):
        self.nc, self.name, self.stack, self.used = nc, name, ExitStack(), []

    def __enter__(self):
        self.stack.__enter__()
        return self

    def __exit__(self, *a):
        if self.used and a[0] is None:
            with self.nc.Block() as block:

                @block.sync
                def _(sp):
                    for sem in self.used:
                        sp.sem_clear(sem)

        return self.stack.__exit__(*a)

    def sb(self, name, shape, dt=F32):
        return self.stack.enter_context(self.nc.sbuf_tensor(f"{self.name}_{name}", shape, dt))

    def ps(self, name, shape):
        return self.stack.enter_context(self.nc.psum_tensor(f"{self.name}_ps_{name}", shape, F32))

    def sem(self, name):
        self.used.append(self.stack.enter_context(self.nc.semaphore(f"{self.name}_{name}")))
        return self.used[-1]

    def pool_dma_sem(self, name):
        return Stage.pool_dma.enter_context(self.nc.semaphore(f"{self.name}_{name}"))

    def sems(self, name, n):
        return [self.sem(f"{name}{i}") for i in range(n)]


def stage_mods(nc, io, dr, const):
    PAIRS = 6 * D // BANK // 2
    BUFS = 4
    with Stage(nc, "mods") as st:
        w = [st.sb(f"w{b}", [P, KD, BANK]) for b in range(BUFS)]
        bias = st.sb("bias", [2, 2, 6 * D])
        rows = st.sb("rows", [2, 2, 6 * D])
        c_col = st.sb("c_col", [P, 2, KD])
        s_col = st.sb("s_col", [P, 2, KD])
        ps = [st.ps(f"ps{b}", [P, BANK]) for b in range(BUFS)]
        w_in, ps_full, ps_free = (st.sems(n, BUFS) for n in ("w_in", "ps_full", "ps_free"))
        c_in, bias_in, s_ready, copied, stored = (st.sem(n) for n in ("c_in", "bias_in", "s_ready", "copied", "stored"))
        with nc.Block() as block:

            @block.sync
            def _(sp):
                sp.dma_start(c_col[:, 0, :], io["c"][0].rearrange("(p k) -> p k", k=KD)).then_inc(c_in, 16)
                sp.dma_start(c_col[:, 1, :], io["c_ctx"].rearrange("(p k) -> p k", k=KD)).then_inc(c_in, 16)

                def load(i, b):
                    src = io["ada_w"][b // 2].rearrange("(p k) n -> p k n", k=KD)
                    sp.dma_start(w[b][:, :, :], src[:, :, bass.ds((i * 2 + b % 2) * BANK, BANK)]).then_inc(w_in[b], 16)

                for b in range(BUFS):
                    load(0, b)
                with sp.Fori(1, PAIRS) as i:
                    for b in range(BUFS):
                        sp.wait_ge(ps_full[b], i)
                        load(i, b)
                for b in range(BUFS):
                    sp.wait_ge(ps_free[b], PAIRS + 1)
                for l in range(2):
                    sp.dma_start(dr["mod"][l], rows[:, l, :]).then_inc(stored, 16)
                sp.wait_ge(stored, 32)
                sp.wait_ge(copied, 32)

            @block.scalar
            def _(act):
                for l in range(2):
                    act.dma_start(bias[:, l, :], io["ada_b"][l].partition_broadcast(2)).then_inc(bias_in, 16)
                act.wait_ge(c_in, 32)
                nc.scalar.activation(s_col[:, :, :], c_col[:, :, :], ACT.Silu).then_inc(s_ready, 1)
                act.dma_start(dr["x"][0:SEQ, :], io["x"][0]).then_inc(copied, 16)
                act.dma_start(dr["x"][SEQ:TALL, :], io["ctx"][0]).then_inc(copied, 16)

            @block.vector
            def _(dve):
                for b in range(BUFS):
                    dve.sem_inc(ps_free[b], 1)
                dve.wait_ge(bias_in, 32)
                with dve.Fori(0, PAIRS) as i:
                    for b in range(BUFS):
                        at = bass.ds((i * 2 + b % 2) * BANK, BANK)
                        dve.wait_ge(ps_full[b], i + 1)
                        nc.vector.tensor_tensor(rows[:, b // 2, at], ps[b][0:2, :], bias[:, b // 2, at],
                                                ALU.add).then_inc(ps_free[b], 1)

            @block.tensor
            def _(pe):
                pe.wait_ge(s_ready, 1)
                with pe.Fori(0, PAIRS) as i:
                    for b in range(BUFS):
                        pe.wait_ge(ps_free[b], i + 1)
                        pe.wait_ge(w_in[b], 16 * i + 16)
                        for k in range(KD):
                            last = nc.tensor.matmul(ps[b][0:2, :], s_col[:, :, k], w[b][:, k, :],
                                                    start=(k == 0), stop=(k == KD - 1))
                        last.then_inc(ps_full[b], 1)


def stage_transposed(nc, dr, const, hT, layer):
    with Stage(nc, f"tr{layer}") as st:
        x = [st.sb(f"x{b}", [P, D]) for b in range(2)]
        shift = st.sb("shift", [P, 2, KD])
        scale = st.sb("scale", [P, 2, KD])
        scale1 = st.sb("scale1", [P, 2, KD])
        ps = [st.ps(f"ps{b}", [P, 2 * BANK]) for b in range(2)]
        x_in, ps_full, ps_free_a, ps_free_v = (st.sems(n, 2) for n in ("x_in", "ps_full", "ps_free_a", "ps_free_v"))
        m_in, m_ready = st.sem("m_in"), st.sem("m_ready")
        ident = const("ident")

        def halves(eng, per):
            with eng.Fori(0, NT_X // 2) as i:
                for b in range(2):
                    per(i, b, 0)
            for b in range(2):
                per(NT_X // 2, b, 1)

        with nc.Block() as block:

            @block.sync
            def _(sp):
                for s in range(2):
                    for tile, part in ((shift, 0), (scale, 1)):
                        sp.dma_start(tile[:, s, :], dr["mod"][layer, s, part * D:(part + 1) * D].rearrange("(p k) -> p k", k=KD)).then_inc(m_in, 16)

                def load(i, b):
                    sp.dma_start(x[b][:, :], dr["x"][bass.ds((i * 2 + b) * P, P), :]).then_inc(x_in[b], 16)

                for b in range(2):
                    load(0, b)
                with sp.Fori(1, NT_ALL // 2) as i:
                    for b in range(2):
                        sp.wait_ge(ps_full[b], i)
                        load(i, b)

            @block.tensor
            def _(pe):
                def turn(i, b, s):
                    pe.wait_ge(x_in[b], 16 * i + 16)
                    pe.wait_ge(ps_free_a[b], i + 1)
                    pe.wait_ge(ps_free_v[b], i + 1)
                    rows = x[b][:, :].rearrange("t (p k) -> t k p", k=KD)
                    for k in range(KD):
                        last = nc.tensor.transpose(ps[b][:, k * P:(k + 1) * P], rows[:, k, :], ident)
                    last.then_inc(ps_full[b], 1)

                halves(pe, turn)

            @block.scalar
            def _(act):
                for b in range(2):
                    act.sem_inc(ps_free_a[b], 1)
                act.wait_ge(m_ready, 1)

                def out(i, b, s):
                    act.wait_ge(ps_full[b], i + 1)
                    for k in range(0, KD // 2):
                        last = nc.scalar.activation(hT[:, k, bass.ds((i * 2 + b) * P, P)], ps[b][:, k * P:(k + 1) * P],
                                                    ACT.Identity, bias=shift[:, s, k:k + 1], scale=scale1[:, s, k:k + 1])
                    last.then_inc(ps_free_a[b], 1)

                halves(act, out)

            @block.vector
            def _(dve):
                for b in range(2):
                    dve.sem_inc(ps_free_v[b], 1)
                dve.wait_ge(m_in, 64)
                nc.vector.tensor_scalar(scale1[:, :, :], scale[:, :, :], 1.0, None, ALU.add).then_inc(m_ready, 1)
                dve.wait_ge(m_ready, 1)

                def out(i, b, s):
                    dve.wait_ge(ps_full[b], i + 1)
                    for k in range(KD // 2, KD):
                        last = nc.vector.tensor_scalar(hT[:, k, bass.ds((i * 2 + b) * P, P)], ps[b][:, k * P:(k + 1) * P],
                                                       scale1[:, s, k:k + 1], shift[:, s, k:k + 1], ALU.mult, ALU.add)
                    last.then_inc(ps_free_v[b], 1)

                halves(dve, out)


N_CUTS = [(0, BANK), (BANK, BANK), (2 * BANK, CTX)]


def stage_window_qkv(nc, io, dr, const, hT, v_all):
    with Stage(nc, "qkv") as st:
        w = [st.sb(f"w{b}", [P, KD, P]) for b in range(2)]
        wv = st.sb("wv", [P, KD, A_KV * A_HD])
        raw = [st.sb(f"raw{b}", [P, SEQ]) for b in range(2)]
        rawcos = [st.sb(f"rawcos{b}", [P, SEQ]) for b in range(2)]
        rotsin = [st.sb(f"rotsin{b}", [P, SEQ]) for b in range(2)]
        out = [st.sb(f"out{b}", [P, TALL]) for b in range(2)]
        ps = [st.ps(f"ps{n}", [P, BANK]) for n in range(3)]
        ps_rot = [st.ps(f"rot{n}", [P, BANK]) for n in range(2)]
        w_in, cos_ready, out_ready, stored = (st.sems(n, 2) for n in ("w_in", "cos_ready", "out_ready", "stored"))
        ps_full, copied = (st.sems(n, 3) for n in ("ps_full", "copied"))
        rot_full, rotsin_ready = (st.sems(n, 2) for n in ("rot_full", "rotsin_ready"))
        zeros = st.sb("zeros", [P, D])
        wv_in, v_full, v_read, zeros_ready, zeroed = (st.sem(n) for n in ("wv_in", "v_full", "v_read", "zeros_ready", "zeroed"))
        cos, sin, rot = const("cos_a"), const("sin_a"), const("rot_a")
        w_dram = io["win_w_in"][0].rearrange("(p k) n -> p k n", k=KD)
        PAIRS = A_QK_CHUNKS // 2
        with nc.Block() as block:

            @block.sync
            def _(sp):
                def load(i, b):
                    sp.dma_start(w[b][:, :, :], w_dram[:, :, bass.ds((i * 2 + b) * P, P)]).then_inc(w_in[b], 16)

                def store(i, b):
                    sp.wait_ge(out_ready[b], i + 2)
                    st.settle(sp)
                    sp.wait_ge(copied[2], 2 * i + b + 2)
                    st.settle(sp)
                    sp.dma_start(dr["qkT"][bass.ds((i * 2 + b) * P, P), :], out[b][:, :]).then_inc(stored[b], 16)

                for b in range(2):
                    sp.sem_inc(stored[b], 16)
                    load(0, b)
                sp.dma_start(wv[:, :, :], w_dram[:, :, A_QK_CHUNKS * P:]).then_inc(wv_in, 16)
                sp.wait_ge(zeros_ready, 1)
                y_rows = dr["y"].rearrange("(b p) d -> p b d", p=P)
                sp.dma_start(y_rows, zeros[:, :].unsqueeze(1).broadcast_to([P, y_rows.shape[1], D])).then_inc(zeroed, 16)
                with sp.Fori(1, PAIRS) as i:
                    for b in range(2):
                        sp.wait_ge(ps_full[2], 2 * i + b - 1)
                        load(i, b)
                        store(i - 1, b)
                for b in range(2):
                    store(PAIRS - 1, b)
                for b in range(2):
                    sp.wait_ge(stored[b], 16 * PAIRS + 16)
                sp.wait_ge(zeroed, 16)

            @block.tensor
            def _(pe):
                for n in range(2):
                    pe.sem_inc(rot_full[n], 2)
                with pe.Fori(0, PAIRS) as i:
                    for b in range(2):
                        pe.wait_ge(w_in[b], 16 * i + 16)
                        for n, (at, size) in enumerate(N_CUTS):
                            pe.wait_ge(copied[n], 2 * i + b + 1)
                            for k in range(KD):
                                last = nc.tensor.matmul(ps[n][:, 0:size], w[b][:, k, :], hT[:, k, at:at + size],
                                                        start=(k == 0), stop=(k == KD - 1))
                            last.then_inc(ps_full[n], 1)
                        for n in range(2):
                            pe.wait_ge(copied[n], 2 * i + b + 2)
                            pe.wait_ge(rotsin_ready[n], 2 * i + b + 1)
                            nc.tensor.matmul(ps_rot[n][:, :], rot, raw[b][:, n * BANK:(n + 1) * BANK],
                                             start=True, stop=True).then_inc(rot_full[n], 1)
                pe.wait_ge(wv_in, 16)
                for t in range(NT_ALL):
                    if t < 3:
                        pe.wait_ge(copied[t], 2 * PAIRS + 1)
                    else:
                        pe.wait_ge(v_read, t - 2)
                    for k in range(KD):
                        last = nc.tensor.matmul(ps[t % 3][:, 0:A_KV * A_HD], hT[:, k, t * P:(t + 1) * P], wv[:, k, :],
                                                start=(k == 0), stop=(k == KD - 1))
                    last.then_inc(v_full, 1)

            @block.scalar
            def _(act):
                for n in range(3):
                    act.sem_inc(copied[n], 1)
                with act.Fori(0, PAIRS) as i:
                    for b in range(2):
                        act.wait_ge(cos_ready[b], i + 1)
                        for n in range(2):
                            act.wait_ge(rot_full[n], 2 * i + b + 1)
                            act.wait_ge(ps_full[n], 2 * i + b + 1)
                            nc.scalar.activation(raw[b][:, n * BANK:(n + 1) * BANK], ps[n][:, :], ACT.Copy).then_inc(copied[n], 1)
                        act.wait_ge(ps_full[2], 2 * i + b + 1)
                        act.wait_ge(stored[b], 16 * i + 16)
                        nc.scalar.activation(out[b][:, SEQ:TALL], ps[2][:, 0:CTX], ACT.Copy).then_inc(copied[2], 1)
                for t in range(NT_ALL):
                    act.wait_ge(v_full, t + 1)
                    nc.scalar.activation(v_all[:, t, :], ps[t % 3][:, 0:A_KV * A_HD], ACT.Copy).then_inc(v_read, 1)

            @block.gpsimd
            def _(pool):
                nc.gpsimd.memset(zeros[:, :], 0.0).then_inc(zeros_ready, 1)
                for b in range(2):
                    pool.sem_inc(cos_ready[b], 1)
                with pool.Fori(0, PAIRS) as i:
                    for b in range(2):
                        for n in range(2):
                            pool.wait_ge(copied[n], 2 * i + b + 2)
                        pool.wait_ge(out_ready[b], i + 1)
                        nc.gpsimd.tensor_tensor(rawcos[b][:, :], raw[b][:, :], cos, ALU.mult).then_inc(cos_ready[b], 1)

            @block.vector
            def _(dve):
                for n in range(2):
                    dve.sem_inc(rotsin_ready[n], 1)
                    dve.sem_inc(out_ready[n], 1)
                with dve.Fori(0, PAIRS) as i:
                    for b in range(2):
                        dve.wait_ge(out_ready[b], i + 1)
                        for n in range(2):
                            dve.wait_ge(rot_full[n], 2 * i + b + 3)
                            nc.vector.tensor_tensor(rotsin[b][:, n * BANK:(n + 1) * BANK], ps_rot[n][:, :],
                                                    sin[:, n * BANK:(n + 1) * BANK], ALU.mult).then_inc(rotsin_ready[n], 1)
                        for n in range(2):
                            dve.wait_ge(rotsin_ready[n], 2 * i + b + 2)
                        dve.wait_ge(cos_ready[b], i + 2)
                        dve.wait_ge(stored[b], 16 * i + 16)
                        nc.vector.tensor_tensor(out[b][:, 0:SEQ], rawcos[b][:, :], rotsin[b][:, :], ALU.add).then_inc(out_ready[b], 1)


def stage_window_attention(nc, io, dr, const, v_all):
    BLOCKS = NT_ALL
    STEPS = BLOCKS * A_GROUP
    W3 = 3 * P
    with Stage(nc, "wat") as st:
        q = st.sb("q", [A_HD, A_GROUP, TALL])
        k = st.sb("k", [A_HD, TALL])
        ident_h, mask_h = st.sb("ident_h", [P, P], BF16), st.sb("mask_h", [P, 2 * P], BF16)
        sinks, sink, neg_sink = st.sb("sinks", [P, A_HEADS]), st.sb("sink", [P, A_GROUP]), st.sb("neg_sink", [P, A_GROUP])
        probs = [st.sb(f"probs{b}", [P, W3 + CTX]) for b in range(2)]
        probsT = [st.sb(f"probsT{b}", [P, W3 + CTX]) for b in range(2)]
        outs = [st.sb(f"outs{b}", [P, A_GROUP * A_HD]) for b in range(2)]
        top, neg_max, total, sink_exp, denom, inv = (st.sb(n, [P, 4]) for n in ("top", "neg_max", "total", "sink_exp", "denom", "inv"))
        ps_s = [st.ps(f"s{b}", [P, 2 * BANK]) for b in range(2)]
        ps_t = [st.ps(f"t{b}", [P, BANK]) for b in range(2)]
        ps_o = [st.ps(f"o{b}", [P, BANK]) for b in range(2)]
        q_in, k_in, sinks_in, sink_ready, const_ready = (st.sem(n) for n in ("q_in", "k_in", "sinks_in", "sink_ready", "const_ready"))
        scored, top_ready, max_ready, exp_done, sink_exp_done, pv_full, inv_step, out_done = (
            st.sem(n) for n in ("scored", "top_ready", "max_ready", "exp_done", "sink_exp_done", "pv_full", "inv_step", "out_done"))
        turned, turned_read = st.sems("turned", 2), st.sems("turned_read", 2)
        stored = st.sems("stored", 2)
        ident = const("ident")

        def shape_of(u):
            blk = u // A_GROUP
            tiles = [t for t in (blk - 1, blk, blk + 1) if 0 <= t < NT_X] if blk < NT_X else []
            keys = tiles + [NT_X, NT_X + 1]
            return blk, tiles, keys, BANK - P * len(tiles), (len(keys) + 1) // 2

        with nc.Block() as block:

            @block.sync
            def _(sp):
                sp.dma_start(sinks[:, :], io["win_sink"][0].partition_broadcast(P)).then_inc(sinks_in, 16)
                for b in range(2):
                    sp.sem_inc(stored[b], 16)

                def load(g):
                    sp.dma_start(q[:, :, :], dr["qkT"][bass.ds(g * A_GROUP * A_HD, A_GROUP * A_HD), :]
                                 .rearrange("(h d) t -> d h t", d=A_HD)).then_inc(q_in, 16)
                    sp.dma_start(k[:, :], dr["qkT"][bass.ds(g * A_HD + A_HEADS * A_HD, A_HD), :]).then_inc(k_in, 16)

                def store(g):
                    for blk in range(BLOCKS):
                        sp.wait_ge(out_done, g * STEPS + A_GROUP * (blk + 1) + 2)
                        st.settle(sp)
                        sp.dma_start(dr["o"][blk * P:(blk + 1) * P, bass.ds(g * A_GROUP * A_HD, A_GROUP * A_HD)],
                                     outs[blk % 2][:, :]).then_inc(stored[blk % 2], 16)

                load(0)
                store(0)
                with sp.Fori(1, A_KV) as g:
                    sp.wait_ge(scored, g * STEPS)
                    load(g)
                    store(g)
                for b in range(2):
                    sp.wait_ge(stored[b], 16 * (A_KV * BLOCKS // 2 + 1))

            @block.gpsimd
            def _(pool):
                nc.gpsimd.tensor_copy(ident_h[:, :], ident).then_inc(const_ready, 1)
                nc.gpsimd.tensor_copy(mask_h[:, :], const("mask")).then_inc(const_ready, 1)

            @block.tensor
            def _(pe):
                pe.sem_inc(pv_full, 2)
                pe.sem_inc(turned[0], 2)
                pe.sem_inc(turned[1], 2)
                pe.wait_ge(const_ready, 2)
                with pe.Fori(0, A_KV) as g:

                    def scores(u):
                        blk, tiles, keys, at, _ = shape_of(u)
                        s = ps_s[u % 2]
                        qb = q[:, u % A_GROUP, blk * P:(blk + 1) * P]
                        pe.wait_ge(exp_done, g * STEPS + u + 1)
                        if tiles:
                            nc.tensor.matmul(s[:, at:BANK], qb, k[:, tiles[0] * P:(tiles[-1] + 1) * P], start=True, stop=False)
                            for t, m in ((blk - 1, 0), (blk + 1, 1)):
                                if t in tiles:
                                    c = at + (t - tiles[0]) * P
                                    nc.tensor.matmul(s[:, c:c + P], ident_h[:, :], mask_h[:, m * P:(m + 1) * P],
                                                     start=False, stop=(t == tiles[-1]) or blk == NT_X - 1)
                        nc.tensor.matmul(s[:, BANK:BANK + CTX], qb, k[:, SEQ:TALL], start=True, stop=True).then_inc(scored, 1)

                    def turn(u):
                        _, _, keys, _, cut = shape_of(u)
                        pe.wait_ge(exp_done, g * STEPS + u + 3)
                        for half, cs in ((0, range(0, cut)), (1, range(cut, len(keys)))):
                            pe.wait_ge(turned_read[half], g * STEPS + u + 1)
                            for c in cs:
                                last = nc.tensor.transpose(ps_t[half][:, (c - cs[0]) * P:(c - cs[0] + 1) * P],
                                                           probs[u % 2][:, c * P:(c + 1) * P], ident)
                            last.then_inc(turned[half], 1)

                    def mix(u):
                        _, _, keys, _, _ = shape_of(u)
                        for half in range(2):
                            pe.wait_ge(turned_read[half], g * STEPS + u + 2)
                        pe.wait_ge(out_done, g * STEPS + u + 1)
                        for c, t in enumerate(keys):
                            last = nc.tensor.matmul(ps_o[u % 2][:, 0:A_HD], probsT[u % 2][:, c * P:(c + 1) * P],
                                                    v_all[:, t, bass.ds(g * A_HD, A_HD)], start=(c == 0), stop=(c == len(keys) - 1))
                        last.then_inc(pv_full, 1)

                    pe.wait_ge(q_in, 16 * g + 16)
                    pe.wait_ge(k_in, 16 * g + 16)
                    scores(0)
                    for u in range(STEPS):
                        if u + 1 < STEPS:
                            scores(u + 1)
                        if u:
                            mix(u - 1)
                        turn(u)
                    mix(STEPS - 1)

            @block.scalar
            def _(act):
                act.sem_inc(exp_done, 2)
                act.sem_inc(turned_read[0], 1)
                act.wait_ge(sinks_in, 16)
                with act.Fori(0, A_KV) as g:
                    act.wait_ge(out_done, g * STEPS + 2)
                    nc.scalar.activation(sink[:, :], sinks[:, bass.ds(g * A_GROUP, A_GROUP)], ACT.Copy).then_inc(sink_ready, 1)
                    nc.scalar.activation(neg_sink[:, :], sinks[:, bass.ds(g * A_GROUP, A_GROUP)], ACT.Copy, scale=-1.0).then_inc(sink_ready, 1)
                    act.wait_ge(sink_ready, 2 * g + 2)

                    def exps(u):
                        blk, tiles, keys, at, _ = shape_of(u)
                        j = u % 4
                        act.wait_ge(turned[1], g * STEPS + u + 1)
                        act.wait_ge(max_ready, g * STEPS + u + 1)
                        nc.scalar.activation(probs[u % 2][:, 0:len(keys) * P], ps_s[u % 2][:, at:BANK + CTX], ACT.Exp,
                                             bias=neg_max[:, j:j + 1], scale=A_SCALE, accum_out=total[:, j:j + 1]).then_inc(exp_done, 1)
                        nc.scalar.activation(sink_exp[:, j:j + 1], sink[:, u % A_GROUP:u % A_GROUP + 1], ACT.Exp,
                                             bias=neg_max[:, j:j + 1]).then_inc(sink_exp_done, 1)

                    def read(u):
                        cut = shape_of(u)[4]
                        act.wait_ge(turned[0], g * STEPS + u + 3)
                        act.wait_ge(pv_full, g * STEPS + u + 1)
                        nc.scalar.activation(probsT[u % 2][:, 0:cut * P], ps_t[0][:, 0:cut * P], ACT.Copy).then_inc(turned_read[0], 1)

                    exps(0)
                    for u in range(STEPS):
                        if u + 1 < STEPS:
                            exps(u + 1)
                        read(u)

            @block.vector
            def _(dve):
                dve.sem_inc(out_done, 2)
                dve.sem_inc(turned_read[1], 1)
                with dve.Fori(0, A_KV) as g:
                    dve.wait_ge(sink_ready, 2 * g + 2)

                    def maxima(u):
                        _, _, _, at, _ = shape_of(u)
                        j = u % 4
                        dve.wait_ge(scored, g * STEPS + u + 1)
                        nc.vector.tensor_reduce(top[:, j:j + 1], ps_s[u % 2][:, at:BANK + CTX], AX, ALU.max).then_inc(top_ready, 1)
                        dve.wait_ge(top_ready, g * STEPS + u + 1)
                        nc.vector.tensor_scalar(neg_max[:, j:j + 1], top[:, j:j + 1], -A_SCALE,
                                                neg_sink[:, u % A_GROUP:u % A_GROUP + 1], ALU.mult, ALU.min).then_inc(max_ready, 1)

                    def read(u):
                        _, _, keys, _, cut = shape_of(u)
                        dve.wait_ge(turned[1], g * STEPS + u + 3)
                        dve.wait_ge(pv_full, g * STEPS + u + 1)
                        nc.vector.tensor_copy(probsT[u % 2][:, cut * P:len(keys) * P],
                                              ps_t[1][:, 0:(len(keys) - cut) * P]).then_inc(turned_read[1], 1)

                    def finish(u):
                        blk, h, j = u // A_GROUP, u % A_GROUP, u % 4
                        n = 2 * (g * STEPS + u)
                        dve.wait_ge(sink_exp_done, g * STEPS + u + 1)
                        nc.vector.tensor_tensor(denom[:, j:j + 1], total[:, j:j + 1], sink_exp[:, j:j + 1], ALU.add).then_inc(inv_step, 1)
                        dve.wait_ge(inv_step, n + 1)
                        nc.vector.reciprocal(inv[:, j:j + 1], denom[:, j:j + 1]).then_inc(inv_step, 1)
                        dve.wait_ge(inv_step, n + 2)
                        dve.wait_ge(pv_full, g * STEPS + u + 3)
                        if h == 0:
                            dve.wait_ge(stored[blk % 2], 16 * (g * (BLOCKS // 2) + blk // 2) + 16)
                        nc.vector.tensor_scalar(outs[blk % 2][:, h * A_HD:(h + 1) * A_HD], ps_o[u % 2][:, 0:A_HD],
                                                inv[:, j:j + 1], None, ALU.mult).then_inc(out_done, 1)

                    maxima(0)
                    for u in range(STEPS):
                        if u + 1 < STEPS:
                            maxima(u + 1)
                        read(u)
                        if u:
                            finish(u - 1)
                    finish(STEPS - 1)


def stage_latents(nc, io, dr, const, cqT, ckvT, kT):
    with Stage(nc, "lat") as st:
        w = st.sb("w", [P, KD, B_IN])
        x = [st.sb(f"x{b}", [P, D]) for b in range(2)]
        xT = [st.sb(f"xT{b}", [P, KD, P]) for b in range(2)]
        lat = [st.sb(f"lat{b}", [P, B_IN]) for b in range(2)]
        shift, scale, scale1 = (st.sb(n, [P, 2, KD]) for n in ("shift", "scale", "scale1"))
        q_gain, kv_gain = st.sb("q_gain", [P, B_QR // P]), st.sb("kv_gain", [P, B_KVR // P])
        squares = [st.sb(f"squares{n}", [P, BANK]) for n in range(2)]
        sums, mean, root, rstd = (st.sb(n, [P, 2, 2]) for n in ("sums", "mean", "root", "rstd"))
        kcos, ksin = st.sb("kcos", [P, B_ROPE]), st.sb("ksin", [P, B_ROPE])
        ps_x = [st.ps(f"x{b}", [P, 2 * BANK]) for b in range(2)]
        ps_c = st.ps("c", [P, 2 * BANK])
        ps_z = st.ps("z", [P, 2 * BANK])
        x_in = st.sems("x_in", 2)
        w_in, m_in, m_ready = st.sem("w_in"), st.sem("m_in"), st.sem("m_ready")
        turned, xT_a, xT_v, projected, squared, rooted, chain, c_read, c_scaled, lat_full, z_read_a, z_read_v = (
            st.sem(n) for n in ("turned", "xT_a", "xT_v", "projected", "squared", "rooted", "chain", "c_read", "c_scaled", "lat_full", "z_read_a", "z_read_v"))
        ident = const("ident")
        KQ, KV = B_QR // P, B_KVR // P
        ROPE_AT = B_QR + B_KVR
        CHAIN = 4

        def skewed(eng, first, second):
            first(0, 0, 0)
            first(0, 1, 0)
            second(0, 0, 0)
            with eng.Fori(1, NT_X // 2) as i:
                first(i, 0, 0)
                second(i - 1, 1, 0)
                first(i, 1, 0)
                second(i, 0, 0)
            first(NT_X // 2, 0, 1)
            second(NT_X // 2 - 1, 1, 0)
            first(NT_X // 2, 1, 1)
            second(NT_X // 2, 0, 1)
            second(NT_X // 2, 1, 1)

        with nc.Block() as block:

            @block.sync
            def _(sp):
                for s in range(2):
                    for tile, part in ((shift, 0), (scale, 1)):
                        sp.dma_start(tile[:, s, :], dr["mod"][1, s, part * D:(part + 1) * D].rearrange("(p k) -> p k", k=KD)).then_inc(m_in, 16)
                sp.dma_start(q_gain[:, :], io["mla_q_norm"][0].rearrange("(p k) -> p k", k=KQ)).then_inc(m_in, 16)
                sp.dma_start(kv_gain[:, :], io["mla_kv_norm"][0].rearrange("(p k) -> p k", k=KV)).then_inc(m_in, 16)

                def load(i, b):
                    sp.dma_start(x[b][:, :], dr["x"][bass.ds((i * 2 + b) * P, P), :]).then_inc(x_in[b], 16)

                for b in range(2):
                    load(0, b)
                sp.dma_start(w[:, :, :], io["mla_w_in"][0].rearrange("(p k) n -> p k n", k=KD)).then_inc(w_in, 16)
                with sp.Fori(1, NT_ALL // 2) as i:
                    for b in range(2):
                        sp.wait_ge(turned, 2 * i + b - 1)
                        load(i, b)

            @block.tensor
            def _(pe):
                def turn_and_project(i, b, s):
                    t = 2 * i + b
                    rows = x[b][:, :].rearrange("t (p k) -> t k p", k=KD)
                    pe.wait_ge(x_in[b], 16 * i + 16)
                    pe.wait_ge(xT_a, t + 1)
                    pe.wait_ge(xT_v, t + 1)
                    for k in range(KD):
                        last = nc.tensor.transpose(ps_x[b][:, k * P:(k + 1) * P], rows[:, k, :], ident)
                    last.then_inc(turned, 1)
                    pe.wait_ge(xT_a, t + 3)
                    pe.wait_ge(xT_v, t + 3)
                    pe.wait_ge(c_read, t + 1)
                    pe.wait_ge(c_scaled, t + 1)
                    cuts = ((0, B_QR), (B_QR, B_IN)) if s == 0 else ((B_QR, B_IN),)
                    for lo, hi in cuts:
                        for k in range(KD):
                            last = nc.tensor.matmul(ps_c[:, lo:hi], xT[b][:, k, :], w[:, k, lo:hi],
                                                    start=(k == 0), stop=(k == KD - 1))
                    last.then_inc(projected, 1)

                def turn_latents(i, b, s):
                    t = 2 * i + b
                    pe.wait_ge(c_read, t + 2)
                    pe.wait_ge(c_scaled, t + 2)
                    pe.wait_ge(z_read_a, t + 1)
                    pe.wait_ge(z_read_v, t + 1)
                    if s == 0:
                        cq = lat[b][:, 0:B_QR].rearrange("t (p k) -> t k p", k=KQ)
                        for k in range(KQ):
                            nc.tensor.transpose(ps_z[:, k * P:(k + 1) * P], cq[:, k, :], ident)
                    kv = lat[b][:, B_QR:ROPE_AT].rearrange("t (p k) -> t k p", k=KV)
                    for k in range(KV):
                        nc.tensor.transpose(ps_z[:, BANK + k * P:BANK + (k + 1) * P], kv[:, k, :], ident)
                    nc.tensor.transpose(ps_z[0:B_ROPE, BANK + KV * P:BANK + (KV + 1) * P], lat[b][:, ROPE_AT:B_IN],
                                        ident).then_inc(lat_full, 1)

                pe.sem_inc(projected, 2)
                pe.sem_inc(lat_full, 2)
                pe.wait_ge(w_in, 16)
                skewed(pe, turn_and_project, turn_latents)

            @block.scalar
            def _(act):
                act.sem_inc(xT_a, 2)
                act.sem_inc(c_scaled, 1)
                act.sem_inc(z_read_a, 1)
                act.wait_ge(m_ready, 1)

                def scale_latents(i, b, s):
                    t = 2 * i + b
                    act.wait_ge(turned, t + 1)
                    act.wait_ge(projected, t + 1)
                    for k in range(KD // 2):
                        last = nc.scalar.activation(xT[b][:, k, :], ps_x[b][:, k * P:(k + 1) * P], ACT.Identity,
                                                    bias=shift[:, s, k:k + 1], scale=scale1[:, s, k:k + 1])
                    last.then_inc(xT_a, 1)
                    act.wait_ge(projected, t + 3)
                    act.wait_ge(c_read, t + 1)
                    if s == 0:
                        nc.scalar.activation(squares[0][:, 0:B_QR], ps_c[:, 0:B_QR], ACT.Square, accum_out=sums[:, b, 0:1])
                    act.wait_ge(chain, CHAIN * t + 1)
                    nc.scalar.activation(squares[1][:, 0:B_KVR], ps_c[:, B_QR:ROPE_AT], ACT.Square,
                                         accum_out=sums[:, b, 1:2]).then_inc(squared, 1)
                    act.wait_ge(chain, CHAIN * t + 3)
                    nc.scalar.activation(root[:, b, s:2], mean[:, b, s:2], ACT.Sqrt).then_inc(rooted, 1)
                    act.wait_ge(chain, CHAIN * t + 4)
                    act.wait_ge(lat_full, t + 1)
                    nc.scalar.activation(lat[b][:, B_QR:ROPE_AT], ps_c[:, B_QR:ROPE_AT], ACT.Copy,
                                         scale=rstd[:, b, 1:2]).then_inc(c_scaled, 1)

                def gain(i, b, s):
                    t = 2 * i + b
                    act.wait_ge(lat_full, t + 3)
                    if s == 0:
                        for k in range(KQ):
                            last = nc.scalar.activation(cqT[:, k, bass.ds(t * P, P)], ps_z[:, k * P:(k + 1) * P], ACT.Copy,
                                                        scale=q_gain[:, k:k + 1])
                        last.then_inc(z_read_a, 1)
                    else:
                        act.sem_inc(z_read_a, 1)

                skewed(act, scale_latents, gain)

            @block.vector
            def _(dve):
                dve.sem_inc(xT_v, 2)
                dve.sem_inc(c_read, 1)
                dve.sem_inc(z_read_v, 1)
                dve.wait_ge(m_in, 96)
                nc.vector.tensor_scalar(scale1[:, :, :], scale[:, :, :], 1.0, None, ALU.add).then_inc(m_ready, 1)
                dve.wait_ge(m_ready, 1)

                def scale_latents(i, b, s):
                    t = 2 * i + b
                    dve.wait_ge(turned, t + 1)
                    dve.wait_ge(projected, t + 1)
                    for k in range(KD // 2, KD):
                        last = nc.vector.tensor_scalar(xT[b][:, k, :], ps_x[b][:, k * P:(k + 1) * P],
                                                       scale1[:, s, k:k + 1], shift[:, s, k:k + 1], ALU.mult, ALU.add)
                    last.then_inc(xT_v, 1)
                    own = Chain(dve, chain, CHAIN * t)
                    rope = ps_c[:, ROPE_AT:B_IN]
                    dve.wait_ge(projected, t + 3)
                    dve.wait_ge(lat_full, t + 1)
                    if s == 0:
                        halves = lambda ap: ap.rearrange("p (a h j) -> p a h j", a=2, h=2)
                        tk = bass.ds(t * B_ROPE, B_ROPE)
                        r, sn, o = halves(rope), halves(const("sin_k")[:, tk]), halves(ksin[:, :])
                        nc.vector.tensor_tensor(o[:, :, 0, :], r[:, :, 1, :], sn[:, :, 0, :], ALU.mult)
                        nc.vector.tensor_tensor(o[:, :, 1, :], r[:, :, 0, :], sn[:, :, 1, :], ALU.mult)
                        own.link(nc.vector.tensor_tensor(kcos[:, :], rope, const("cos_k")[:, tk], ALU.mult))
                        own.link(nc.vector.tensor_tensor(lat[b][:, ROPE_AT:B_IN], kcos[:, :], ksin[:, :], ALU.add))
                    else:
                        own.link(nc.vector.tensor_copy(lat[b][:, ROPE_AT:B_IN], rope))
                        dve.sem_inc(chain, 1)
                        own.n += 1
                    dve.wait_ge(squared, t + 1)
                    if s == 0:
                        nc.vector.tensor_scalar(mean[:, b, 0:1], sums[:, b, 0:1], 1.0 / B_QR, RMS_EPS, ALU.mult, ALU.add)
                    own.link(nc.vector.tensor_scalar(mean[:, b, 1:2], sums[:, b, 1:2], 1.0 / B_KVR, RMS_EPS, ALU.mult, ALU.add))
                    lo = 0 if s == 0 else 1
                    dve.wait_ge(rooted, t + 1)
                    own.link(nc.vector.reciprocal(rstd[:, b, lo:2], root[:, b, lo:2]))
                    if s == 0:
                        nc.vector.tensor_scalar(lat[b][:, 0:B_QR], ps_c[:, 0:B_QR], rstd[:, b, 0:1], None, ALU.mult).then_inc(c_read, 1)
                    else:
                        dve.sem_inc(c_read, 1)
                    assert own.n == CHAIN

                def gain(i, b, s):
                    t = 2 * i + b
                    dve.wait_ge(lat_full, t + 3)
                    for k in range(KV):
                        nc.vector.tensor_scalar(ckvT[:, k, bass.ds(t * P, P)], ps_z[:, BANK + k * P:BANK + (k + 1) * P],
                                                kv_gain[:, k:k + 1], None, ALU.mult)
                    nc.vector.tensor_copy(kT[B_NOPE:B_QD, bass.ds(t * P, P)],
                                          ps_z[0:B_ROPE, BANK + KV * P:BANK + (KV + 1) * P]).then_inc(z_read_v, 1)

                skewed(dve, scale_latents, gain)


def stage_latent_attention(nc, io, dr, const, cqT, ckvT, kT):
    UN = NT_X
    GROUPS = [(0, 4), (4, 8), (8, 10)]
    PER_BANK = UN * len(GROUPS) // 2
    KQ, KV = B_QR // P, B_KVR // P
    with Stage(nc, "mla") as st:
        wq = [st.sb(f"wq{b}", [P, KQ, B_QD]) for b in range(2)]
        wk = [st.sb(f"wk{b}", [P, KV, B_NOPE]) for b in range(2)]
        wv = st.sb("wv", [P, KV, B_HEADS * B_V])
        v_all = st.sb("v_all", [P, NT_ALL, B_HEADS * B_V])
        o_all = st.sb("o_all", [P, NT_X, B_HEADS * B_V])
        q_raw, q_cos, q_sin, qT = (st.sb(n, [B_QD, SEQ]) for n in ("q_raw", "q_cos", "q_sin", "qT"))
        probs = [st.sb(f"probs{b}", [P, TALL]) for b in range(2)]
        probsT = [st.sb(f"probsT{b}", [P, TALL]) for b in range(2)]
        top, neg_max, total, inv = (st.sb(n, [P, 4]) for n in ("top", "neg_max", "total", "inv"))
        ps_s = [st.ps(f"s{b}", [P, 3 * BANK]) for b in range(2)]
        ps_t = [st.ps(f"t{b}", [P, BANK]) for b in range(2)]
        wq_in, wk_in = st.sems("wq_in", 2), st.sems("wk_in", 2)
        turned, turned_read = st.sems("turned", 2), st.sems("turned_read", 2)
        wv_in, v_full, v_read, q_full, k_full, q_copied, k_copied, rot_full, sin_ready, cos_ready, q_ready = (
            st.sem(n) for n in ("wv_in", "v_full", "v_read", "q_full", "k_full", "q_copied", "k_copied", "rot_full", "sin_ready", "cos_ready", "q_ready"))
        scored, top_ready, max_ready, exp_done, pv_full, inv_ready, out_done, stored = (
            st.sem(n) for n in ("scored", "top_ready", "max_ready", "exp_done", "pv_full", "inv_ready", "out_done", "stored"))
        ident = const("ident")
        cos, sin, rot = const("cos_b")[0:B_QD, :], const("sin_b")[0:B_QD, :], const("rot_b")[0:B_QD, :]
        O_AT = TALL
        ukv = io["mla_w_ukv"][0].rearrange("(p k) (h e) -> p k h e", k=KV, e=B_NOPE + B_V)
        uq = io["mla_w_uq"][0].rearrange("(p k) n -> p k n", k=KQ)
        V_BANKS = 6

        def v_bank(n):
            return ps_s[n // 3][:, (n % 3) * BANK:(n % 3 + 1) * BANK]

        with nc.Block() as block:

            @block.sync
            def _(sp):
                for k in range(KV):
                    sp.dma_start(wv[:, k, :].rearrange("p (h e) -> p h e", e=B_V), ukv[:, k, :, B_NOPE:]).then_inc(wv_in, 16)

                def load(i, b):
                    h = 2 * i + b
                    sp.dma_start(wq[b][:, :, :], uq[:, :, bass.ds(h * B_QD, B_QD)]).then_inc(wq_in[b], 16)
                    sp.dma_start(wk[b][:, :, :], io["mla_w_ukv"][0].rearrange("(p k) n -> p k n", k=KV)[
                        :, :, bass.ds(h * (B_NOPE + B_V), B_NOPE)]).then_inc(wk_in[b], 16)

                for b in range(2):
                    load(0, b)
                with sp.Fori(1, B_HEADS // 2) as i:
                    for b in range(2):
                        sp.wait_ge(k_full, 3 * (2 * i + b - 1))
                        load(i, b)
                for t in range(NT_X):
                    sp.wait_ge(out_done, B_HEADS * UN + 2)
                    sp.dma_start(dr["o"][t * P:(t + 1) * P, :], o_all[:, t, :]).then_inc(stored, 16)
                sp.wait_ge(stored, 16 * NT_X)

            @block.tensor
            def _(pe):
                pe.sem_inc(pv_full, 2)
                for n in range(2):
                    pe.sem_inc(turned[n], 2)
                pe.wait_ge(wv_in, 32)
                for t in range(NT_ALL):
                    for n in range(2):
                        u = 2 * t + n
                        if u >= V_BANKS:
                            pe.wait_ge(v_read, u - V_BANKS + 1)
                        for k in range(KV):
                            last = nc.tensor.matmul(v_bank(u % V_BANKS), ckvT[:, k, t * P:(t + 1) * P],
                                                    wv[:, k, n * BANK:(n + 1) * BANK], start=(k == 0), stop=(k == KV - 1))
                        last.then_inc(v_full, 1)
                pe.wait_ge(v_read, 2 * NT_ALL)

                with pe.Fori(0, B_HEADS // 2) as i:
                    for hb in range(2):
                        h = 2 * i + hb

                        def project():
                            pe.wait_ge(out_done, h * UN + 2)
                            pe.wait_ge(wq_in[hb], 16 * i + 16)
                            pe.wait_ge(wk_in[hb], 16 * i + 16)
                            for n in range(2):
                                for k in range(KQ):
                                    last = nc.tensor.matmul(ps_s[0][0:B_QD, n * BANK:(n + 1) * BANK], wq[hb][:, k, :],
                                                            cqT[:, k, n * BANK:(n + 1) * BANK], start=(k == 0), stop=(k == KQ - 1))
                                last.then_inc(q_full, 1)
                            for n, (at, size) in enumerate(N_CUTS):
                                for k in range(KV):
                                    last = nc.tensor.matmul(ps_s[1][0:B_NOPE, at:at + size], wk[hb][:, k, :],
                                                            ckvT[:, k, at:at + size], start=(k == 0), stop=(k == KV - 1))
                                last.then_inc(k_full, 1)
                            for n in range(2):
                                pe.wait_ge(q_copied, 2 * h + n + 1)
                                pe.wait_ge(turned_read[n], PER_BANK * h + 1)
                                nc.tensor.matmul(ps_t[n][0:B_QD, :], rot, q_raw[:, n * BANK:(n + 1) * BANK],
                                                 start=True, stop=True).then_inc(rot_full, 1)

                        def scores(u):
                            pe.wait_ge(exp_done, h * UN + u + 1)
                            pe.wait_ge(out_done, h * UN + u + 1)
                            if u == 0:
                                pe.wait_ge(q_ready, h + 1)
                                pe.wait_ge(k_copied, 3 * h + 3)
                            for at, size in N_CUTS:
                                last = nc.tensor.matmul(ps_s[u % 2][:, at:at + size], qT[:, u * P:(u + 1) * P], kT[:, at:at + size],
                                                        start=True, stop=True)
                            last.then_inc(scored, 1)

                        def turn(u):
                            pe.wait_ge(exp_done, h * UN + u + 3)
                            for n, (lo, hi) in enumerate(GROUPS):
                                bank, nth = (3 * u + n) % 2, (3 * u + n) // 2
                                if u == 0:
                                    pe.wait_ge(sin_ready, 2 * h + 2)
                                pe.wait_ge(turned_read[bank], PER_BANK * h + nth + 1)
                                for c in range(lo, hi):
                                    last = nc.tensor.transpose(ps_t[bank][:, (c - lo) * P:(c - lo + 1) * P],
                                                               probs[u % 2][:, c * P:(c + 1) * P], ident)
                                last.then_inc(turned[bank], 1)

                        def mix(u):
                            for bank in range(2):
                                nth = max((3 * u + n) // 2 for n in range(3) if (3 * u + n) % 2 == bank)
                                pe.wait_ge(turned_read[bank], PER_BANK * h + nth + 2)
                            for c in range(NT_ALL):
                                last = nc.tensor.matmul(ps_s[u % 2][:, O_AT:O_AT + B_V], probsT[u % 2][:, c * P:(c + 1) * P],
                                                        v_all[:, c, bass.ds(h * B_V, B_V)], start=(c == 0), stop=(c == NT_ALL - 1))
                            last.then_inc(pv_full, 1)

                        project()
                        scores(0)
                        for u in range(UN):
                            if u + 1 < UN:
                                if u:
                                    mix(u - 1)
                                scores(u + 1)
                            elif u:
                                mix(u - 1)
                            turn(u)
                        mix(UN - 1)

            @block.scalar
            def _(act):
                act.sem_inc(exp_done, 2)
                act.sem_inc(turned_read[0], 1)
                for u in range(0, 2 * NT_ALL, 2):
                    act.wait_ge(v_full, u + 2)
                    nc.scalar.activation(v_all[:, u // 2, 0:BANK], v_bank(u % V_BANKS), ACT.Copy).then_inc(v_read, 1)
                    nc.scalar.activation(v_all[:, u // 2, BANK:], v_bank((u + 1) % V_BANKS), ACT.Copy).then_inc(v_read, 1)
                with act.Fori(0, B_HEADS // 2) as i:
                    for hb in range(2):
                        h = 2 * i + hb
                        for n in range(2):
                            act.wait_ge(q_full, 2 * h + n + 1)
                            nc.scalar.activation(q_raw[:, n * BANK:(n + 1) * BANK], ps_s[0][0:B_QD, n * BANK:(n + 1) * BANK],
                                                 ACT.Copy).then_inc(q_copied, 1)

                        def exps(u):
                            j = u % 4
                            act.wait_ge(max_ready, h * UN + u + 1)
                            for bank in range(2):
                                done = [(3 * v + n) // 2 + 1 for v in range(u - 1) for n in range(3) if (3 * v + n) % 2 == bank]
                                act.wait_ge(turned[bank], PER_BANK * h + max(done, default=0) + 2)
                            nc.scalar.activation(probs[u % 2][:, :], ps_s[u % 2][:, 0:TALL], ACT.Exp, bias=neg_max[:, j:j + 1],
                                                 scale=B_SCALE, accum_out=total[:, j:j + 1]).then_inc(exp_done, 1)

                        def read(u):
                            act.wait_ge(pv_full, h * UN + u + 1)
                            for n, (lo, hi) in enumerate(GROUPS):
                                bank, nth = (3 * u + n) % 2, (3 * u + n) // 2
                                if bank == 0:
                                    act.wait_ge(turned[0], PER_BANK * h + nth + 3)
                                    nc.scalar.activation(probsT[u % 2][:, lo * P:hi * P], ps_t[0][:, 0:(hi - lo) * P],
                                                         ACT.Copy).then_inc(turned_read[0], 1)

                        exps(0)
                        for u in range(UN):
                            if u + 1 < UN:
                                exps(u + 1)
                            read(u)

            @block.gpsimd
            def _(pool):
                with pool.Fori(0, B_HEADS) as h:
                    pool.wait_ge(q_copied, 2 * h + 2)
                    nc.gpsimd.tensor_tensor(q_cos[:, :], q_raw[:, :], cos, ALU.mult).then_inc(cos_ready, 1)

            @block.vector
            def _(dve):
                dve.sem_inc(out_done, 2)
                dve.sem_inc(turned_read[1], 1)
                with dve.Fori(0, B_HEADS // 2) as i:
                    for hb in range(2):
                        h = 2 * i + hb
                        for n, (at, size) in enumerate(N_CUTS):
                            dve.wait_ge(k_full, 3 * h + n + 1)
                            nc.vector.tensor_copy(kT[0:B_NOPE, at:at + size], ps_s[1][0:B_NOPE, at:at + size]).then_inc(k_copied, 1)
                        for n in range(2):
                            dve.wait_ge(rot_full, 2 * h + n + 1)
                            nc.vector.tensor_tensor(q_sin[:, n * BANK:(n + 1) * BANK], ps_t[n][0:B_QD, :],
                                                    sin[:, n * BANK:(n + 1) * BANK], ALU.mult).then_inc(sin_ready, 1)
                        dve.wait_ge(sin_ready, 2 * h + 2)
                        dve.wait_ge(cos_ready, h + 1)
                        nc.vector.tensor_tensor(qT[:, :], q_cos[:, :], q_sin[:, :], ALU.add).then_inc(q_ready, 1)

                        def maxima(u):
                            j = u % 4
                            dve.wait_ge(scored, h * UN + u + 1)
                            nc.vector.tensor_reduce(top[:, j:j + 1], ps_s[u % 2][:, 0:TALL], AX, ALU.max).then_inc(top_ready, 1)
                            dve.wait_ge(top_ready, h * UN + u + 1)
                            nc.vector.tensor_scalar(neg_max[:, j:j + 1], top[:, j:j + 1], -B_SCALE, None, ALU.mult).then_inc(max_ready, 1)

                        def read(u):
                            dve.wait_ge(pv_full, h * UN + u + 1)
                            for n, (lo, hi) in enumerate(GROUPS):
                                bank, nth = (3 * u + n) % 2, (3 * u + n) // 2
                                if bank == 1:
                                    dve.wait_ge(turned[1], PER_BANK * h + nth + 3)
                                    nc.vector.tensor_copy(probsT[u % 2][:, lo * P:hi * P], ps_t[1][:, 0:(hi - lo) * P]).then_inc(turned_read[1], 1)

                        def finish(u):
                            j = u % 4
                            dve.wait_ge(exp_done, h * UN + u + 3)
                            nc.vector.reciprocal(inv[:, j:j + 1], total[:, j:j + 1]).then_inc(inv_ready, 1)
                            dve.wait_ge(inv_ready, h * UN + u + 1)
                            dve.wait_ge(pv_full, h * UN + u + 3)
                            nc.vector.tensor_scalar(o_all[:, u, bass.ds(h * B_V, B_V)], ps_s[u % 2][:, O_AT:O_AT + B_V],
                                                    inv[:, j:j + 1], None, ALU.mult).then_inc(out_done, 1)

                        maxima(0)
                        for u in range(UN):
                            if u:
                                finish(u - 1)
                            if u + 1 < UN:
                                maxima(u + 1)
                            read(u)
                        finish(UN - 1)


def load_rows(sp, sem, pairs):
    for tile, row in pairs:
        sp.dma_start(tile, row.partition_broadcast(P)).then_inc(sem, 16)
    return 16 * len(pairs)


def stage_project_out(nc, io, dr, const, layer, w_out, tiles, logits):
    with Stage(nc, f"out{layer}") as st:
        w, wr = st.sb("w", [P, KD, D]), st.sb("wr", [P, KD, ROUTE])
        r_bias = st.sb("r_bias", [P, ROUTE])
        kinds = 2 if tiles > NT_X else 1
        gate, scale, shift = ([st.sb(f"{n}{s}", [P, D]) for s in range(kinds)] for n in ("gate", "scale", "shift"))
        ln_g, ln_b = st.sb("ln_g", [P, D]), st.sb("ln_b", [P, D])
        o, x = ([st.sb(f"{n}{b}", [P, D]) for b in range(2)] for n in ("o", "x"))
        oT, hT = st.sb("oT", [P, KD, P]), st.sb("hT", [P, KD, P])
        gated, res, xn, xg, hs = (st.sb(n, [P, D]) for n in ("gated", "res", "xn", "xg", "hs"))
        xo, h = ([st.sb(f"{n}{b}", [P, D]) for b in range(2)] for n in ("xo", "h"))
        stats, mv, var, rstd, bias = st.sb("stats", [P, 2, 6]), st.sb("mv", [P, 2]), st.sb("var", [P, 1]), st.sb("rstd", [P, 1]), st.sb("bias", [P, 1])
        root = st.sb("root", [P, 1])
        ps_o, ps_y, ps_h = (st.ps(n, [P, 2 * BANK]) for n in ("o", "y", "h"))
        ps_r = st.ps("r", [P, BANK])
        o_in, x_in, x_stored, h_stored = (st.sems(n, 2) for n in ("o_in", "x_in", "x_stored", "h_stored"))
        w_in, rows_in, scale_ready, o_turned, o_read, y_full, h_turned, h_read, routed = (
            st.sem(n) for n in ("w_in", "rows_in", "scale_ready", "o_turned", "o_read", "y_full", "h_turned", "h_read", "routed"))
        chain, rooted, normed, x_ready, hs_ready, h_ready, logit_done = (
            st.sem(n) for n in ("chain", "rooted", "normed", "x_ready", "hs_ready", "h_ready", "logit_done"))
        ident = const("ident")
        STEPS = 9
        mod = lambda s, part: dr["mod"][layer, s, part * D:(part + 1) * D]

        def each(eng, first, second=None):
            pairs = NT_X // 2
            seq = lambda i, b, s: first(i, b, s)
            sec = second or (lambda i, b, s: None)
            seq(0, 0, 0)
            seq(0, 1, 0)
            sec(0, 0, 0)
            with eng.Fori(1, pairs) as i:
                seq(i, 0, 0)
                sec(i - 1, 1, 0)
                seq(i, 1, 0)
                sec(i, 0, 0)
            if kinds == 2:
                seq(pairs, 0, 1)
                sec(pairs - 1, 1, 0)
                seq(pairs, 1, 1)
                sec(pairs, 0, 1)
                sec(pairs, 1, 1)
            else:
                sec(pairs - 1, 1, 0)

        with nc.Block() as block:

            @block.sync
            def _(sp):
                def load(i, b):
                    t = bass.ds((i * 2 + b) * P, P)
                    sp.dma_start(o[b][:, :], dr["o"][t, :]).then_inc(o_in[b], 16)
                    sp.dma_start(x[b][:, :], dr["x"][t, :]).then_inc(x_in[b], 16)

                def store(i, b):
                    t = bass.ds((i * 2 + b) * P, P)
                    sp.wait_ge(x_ready, 2 * i + b + 1)
                    sp.dma_start(dr["x"][t, :], xo[b][:, :]).then_inc(x_stored[b], 16)
                    sp.wait_ge(h_ready, 2 * i + b + 1)
                    sp.dma_start(dr["h"][t, :], h[b][:, :]).then_inc(h_stored[b], 16)

                for b in range(2):
                    sp.sem_inc(x_stored[b], 16)
                    sp.sem_inc(h_stored[b], 16)
                    load(0, b)
                sp.dma_start(w[:, :, :], w_out.rearrange("(p k) n -> p k n", k=KD)).then_inc(w_in, 16)
                pairs = [(ln_g[:, :], io["ln_mix_g"][layer]), (ln_b[:, :], io["ln_mix_b"][layer]),
                         (r_bias[:, 0:NG], io["moe_b_grp"][layer]), (r_bias[:, NG:], io["moe_b_rt"][layer])]
                for s in range(kinds):
                    pairs += [(gate[s][:, :], mod(s, 2)), (shift[s][:, :], mod(s, 3)), (scale[s][:, :], mod(s, 4))]
                load_rows(sp, rows_in, pairs)
                sp.dma_start(wr[:, :, 0:NG], io["moe_w_grp"][layer].rearrange("(p k) n -> p k n", k=KD)).then_inc(rows_in, 16)
                sp.dma_start(wr[:, :, NG:], io["moe_w_rt"][layer].rearrange("(p k) n -> p k n", k=KD)).then_inc(rows_in, 16)
                with sp.Fori(1, tiles // 2) as i:
                    for b in range(2):
                        sp.wait_ge(chain, STEPS * (2 * i + b - 2) + 2)
                        load(i, b)
                        store(i - 1, b)
                for b in range(2):
                    store(tiles // 2 - 1, b)
                for b in range(2):
                    sp.wait_ge(x_stored[b], 16 * (tiles // 2) + 16)
                    sp.wait_ge(h_stored[b], 16 * (tiles // 2) + 16)

            ROWS_IN = 16 * (4 + 3 * kinds + 2)

            @block.tensor
            def _(pe):
                pe.sem_inc(y_full, 1)
                pe.sem_inc(routed, 1)
                pe.wait_ge(rows_in, ROWS_IN)
                pe.wait_ge(w_in, 16)

                def project(i, b, s):
                    t = 2 * i + b
                    pe.wait_ge(o_in[b], 16 * i + 16)
                    pe.wait_ge(o_read, t + 1)
                    rows = o[b][:, :].rearrange("t (p k) -> t k p", k=KD)
                    for k in range(KD):
                        last = nc.tensor.transpose(ps_o[:, k * P:(k + 1) * P], rows[:, k, :], ident)
                    last.then_inc(o_turned, 1)
                    pe.wait_ge(o_read, t + 2)
                    if not (isinstance(i, int) and t == 0):
                        pe.wait_ge(chain, STEPS * t - (STEPS - 1))
                    for n in range(2):
                        for k in range(KD):
                            last = nc.tensor.matmul(ps_y[:, n * BANK:(n + 1) * BANK], oT[:, k, :], w[:, k, n * BANK:(n + 1) * BANK],
                                                    start=(k == 0), stop=(k == KD - 1))
                    last.then_inc(y_full, 1)

                def route(i, b, s):
                    t = 2 * i + b
                    pe.wait_ge(h_ready, t + 1)
                    pe.wait_ge(h_read, t + 1)
                    rows = h[b][:, :].rearrange("t (p k) -> t k p", k=KD)
                    for k in range(KD):
                        last = nc.tensor.transpose(ps_h[:, k * P:(k + 1) * P], rows[:, k, :], ident)
                    last.then_inc(h_turned, 1)
                    pe.wait_ge(h_read, t + 2)
                    pe.wait_ge(logit_done, t + 1)
                    for k in range(KD):
                        last = nc.tensor.matmul(ps_r[:, 0:ROUTE], hT[:, k, :], wr[:, k, :], start=(k == 0), stop=(k == KD - 1))
                    last.then_inc(routed, 1)

                each(pe, project, route)

            @block.scalar
            def _(act):
                act.sem_inc(o_read, 1)
                act.sem_inc(h_read, 1)

                def first(i, b, s):
                    t = 2 * i + b
                    act.wait_ge(o_turned, t + 1)
                    act.wait_ge(y_full, t + 1)
                    nc.scalar.activation(oT[:, :, :].rearrange("p k t -> p (k t)"), ps_o[:, :], ACT.Copy).then_inc(o_read, 1)

                def norm(i, b, s):
                    t = 2 * i + b
                    act.wait_ge(chain, STEPS * t + 6)
                    nc.scalar.activation(root[:, :], var[:, :], ACT.Sqrt).then_inc(rooted, 1)
                    act.wait_ge(chain, STEPS * t + 8)
                    nc.scalar.activation(xn[:, :], res[:, :], ACT.Identity, bias=bias[:, :], scale=rstd[:, :]).then_inc(normed, 1)
                    act.wait_ge(h_turned, t + 1)
                    act.wait_ge(routed, t + 1)
                    nc.scalar.activation(hT[:, :, :].rearrange("p k t -> p (k t)"), ps_h[:, :], ACT.Copy).then_inc(h_read, 1)

                each(act, first, norm)

            @block.vector
            def _(dve):
                dve.sem_inc(logit_done, 1)
                dve.wait_ge(rows_in, ROWS_IN)
                for s in range(kinds):
                    last = nc.vector.tensor_scalar(scale[s][:, :], scale[s][:, :], 1.0, None, ALU.add)
                last.then_inc(scale_ready, 1)
                dve.wait_ge(scale_ready, 1)

                def update(i, b, s):
                    t = 2 * i + b
                    own = Chain(dve, chain, STEPS * t)
                    dve.wait_ge(y_full, t + 2)
                    own.link(nc.vector.tensor_tensor(gated[:, :], ps_y[:, :], gate[s][:, :], ALU.mult))
                    dve.wait_ge(x_in[b], 16 * i + 16)
                    own.link(nc.vector.scalar_tensor_tensor(res[:, :], x[b][:, :], ALPHA, gated[:, :], ALU.mult, ALU.add))
                    for n in range(2):
                        own.inc(nc.vector.bn_stats(stats[:, n, :], res[:, n * BANK:(n + 1) * BANK]))
                    own.wait()
                    st.settle(dve)
                    own.link(nc.vector.bn_aggr(mv[:, :], stats[:, :, :].rearrange("p n s -> p (n s)")))
                    own.link(nc.vector.tensor_scalar(var[:, :], mv[:, 1:2], LN_EPS, None, ALU.add))
                    dve.wait_ge(rooted, t + 1)
                    own.link(nc.vector.reciprocal(rstd[:, :], root[:, :]))
                    own.link(nc.vector.tensor_scalar(bias[:, :], mv[:, 0:1], rstd[:, :], -1.0, ALU.mult, ALU.mult))
                    dve.wait_ge(normed, t + 1)
                    own.link(nc.vector.tensor_tensor(xg[:, :], xn[:, :], ln_g[:, :], ALU.mult))
                    dve.wait_ge(hs_ready, t + 1)
                    dve.wait_ge(h_stored[b], 16 * i + 16)
                    assert own.n == STEPS
                    nc.vector.tensor_tensor(h[b][:, :], hs[:, :], shift[s][:, :], ALU.add).then_inc(h_ready, 1)

                def logit(i, b, s):
                    t = 2 * i + b
                    dve.wait_ge(routed, t + 2)
                    nc.vector.tensor_tensor(logits[:, bass.ds(t * ROUTE, ROUTE)], ps_r[:, 0:ROUTE], r_bias[:, :], ALU.add).then_inc(logit_done, 1)

                each(dve, update, logit)

            @block.gpsimd
            def _(pool):
                pool.wait_ge(rows_in, ROWS_IN)
                pool.wait_ge(scale_ready, 1)

                def shift_norm(i, b, s):
                    t = 2 * i + b
                    pool.wait_ge(chain, STEPS * t + 9)
                    pool.wait_ge(x_stored[b], 16 * i + 16)
                    nc.gpsimd.tensor_tensor(xo[b][:, :], xg[:, :], ln_b[:, :], ALU.add).then_inc(x_ready, 1)
                    pool.wait_ge(x_ready, t + 1)
                    nc.gpsimd.tensor_tensor(hs[:, :], xo[b][:, :], scale[s][:, :], ALU.mult).then_inc(hs_ready, 1)

                each(pool, shift_norm)


def stage_route(nc, dr, const, layer, tiles, logits, weights, slots, block_info, tokens):
    nb = n_blocks(tiles)
    with Stage(nc, f"rt{layer}") as st:
        lg = logits[:, 0:tiles * ROUTE].rearrange("p (t r) -> p t r", r=ROUTE)
        l_grp, l_exp = lg[:, :, 0:NG], lg[:, :, NG:]
        t1 = lambda name, dt=F32: st.sb(name, [P, tiles], dt)
        tg = lambda name: st.sb(name, [P, tiles, NG])
        te = lambda name: st.sb(name, [P, tiles, NE])
        g_max, g_low, g_sum, g_prob = t1("g_max"), t1("g_low"), t1("g_sum"), t1("g_prob")
        g_diff, g_exp, g_hit, g_idx, g_one = tg("g_diff"), tg("g_exp"), tg("g_hit"), tg("g_idx"), tg("g_one")
        e_in, e_hit, e_idx, e_rest = te("e_in"), te("e_hit"), te("e_idx"), te("e_rest")
        e_max, e_low = [t1(f"e_max{k}") for k in range(2)], [t1(f"e_low{k}") for k in range(2)]
        one = [te(f"one{k}") for k in range(2)]
        both, seen = te("both"), st.sb("seen", [P, tiles + 1, NE])
        diff, ratio, denom, w_first = t1("diff"), t1("ratio"), t1("denom"), t1("w_first")
        counts, blocks, ends, starts = (st.sb(n, [P, NE]) for n in ("counts", "blocks", "ends", "starts"))
        over = st.sb("over", [P, NE, tiles])
        ranks, product = te("ranks"), te("product")
        rank, base, above, local, place, block_of = (t1(n) for n in ("rank", "base", "above", "local", "place", "block_of"))
        steps_over = st.sb("steps_over", [P, tiles, tiles])
        where = t1("where")
        table_at = [t1(f"table_at{k}", I32) for k in range(2)]
        passed, owner = st.sb("passed", [P, nb, NE]), st.sb("owner", [P, nb])
        token_id = t1("token_id", I32)
        zeros = st.sb("zeros", [P, nb], I32)
        ps = st.ps("ps", [P, BANK])
        ps_n = st.ps("ps_n", [P, BANK])
        own_sem, exp_ready, exped, both_ready, ranked, routed, zeroed = (
            st.sem(n) for n in ("own", "exp_ready", "exped", "both_ready", "ranked", "routed", "zeroed"))
        zero_in, scattered, read_back = (st.pool_dma_sem(n) for n in ("zero_in", "scattered", "read_back"))
        v = nc.vector
        with nc.Block() as block:

            @block.vector
            def _(dve):
                own = Chain(dve, own_sem)
                link = own.link
                iota_g, iota_e = bcast_mid(const("iota_g"), tiles), bcast_mid(const("iota_e"), tiles)
                link(v.tensor_reduce(g_max[:, :], l_grp, AX, ALU.max))
                v.tensor_tensor(g_diff[:, :, :], l_grp, bcast_last(g_max[:, :], NG), ALU.subtract).then_inc(exp_ready, 1)
                link(v.tensor_tensor(g_hit[:, :, :], l_grp, bcast_last(g_max[:, :], NG), ALU.is_equal))
                link(v.tensor_tensor(g_idx[:, :, :], g_hit[:, :, :], iota_g, ALU.mult))
                link(v.tensor_reduce(g_low[:, :], g_idx[:, :, :], AX, ALU.min))
                link(v.tensor_tensor(g_one[:, :, :], iota_g, bcast_last(g_low[:, :], NG), ALU.is_equal))
                link(v.tensor_scalar(g_idx[:, :, :], g_one[:, :, :], 1.0, BIG, ALU.subtract, ALU.mult))
                for g in range(NG):
                    own.inc(v.tensor_tensor(e_in[:, :, g * EPG:(g + 1) * EPG], l_exp[:, :, g * EPG:(g + 1) * EPG],
                                            g_idx[:, :, g:g + 1].broadcast_to([P, tiles, EPG]), ALU.add))
                own.wait()
                src = e_in
                for k in range(2):
                    link(v.tensor_reduce(e_max[k][:, :], src[:, :, :], AX, ALU.max))
                    link(v.tensor_tensor(e_hit[:, :, :], src[:, :, :], bcast_last(e_max[k][:, :], NE), ALU.is_equal))
                    link(v.tensor_tensor(e_idx[:, :, :], e_hit[:, :, :], iota_e, ALU.mult))
                    link(v.tensor_reduce(e_low[k][:, :], e_idx[:, :, :], AX, ALU.min))
                    link(v.tensor_tensor(one[k][:, :, :], iota_e, bcast_last(e_low[k][:, :], NE), ALU.is_equal))
                    if k == 0:
                        link(v.scalar_tensor_tensor(e_rest[:, :, :], one[0][:, :, :], -BIG, e_in[:, :, :], ALU.mult, ALU.add))
                        src = e_rest
                link(v.tensor_tensor(both[:, :, :], one[0][:, :, :], one[1][:, :, :], ALU.add))
                link(v.memset(seen[:, 0, :], 0.0))
                for t in range(tiles):
                    link(v.tensor_tensor(seen[:, t + 1, :], seen[:, t, :], both[:, t, :], ALU.add))
                dve.sem_inc(both_ready, 1)
                v.tensor_tensor(diff[:, :], e_max[1][:, :], e_max[0][:, :], ALU.subtract).then_inc(exp_ready, 1)
                dve.wait_ge(exped, 1)
                link(v.tensor_reduce(g_sum[:, :], g_exp[:, :, :], AX, ALU.add))
                link(v.reciprocal(g_prob[:, :], g_sum[:, :]))
                dve.wait_ge(exped, 2)
                link(v.tensor_scalar(denom[:, :], ratio[:, :], 1.0, None, ALU.add))
                link(v.reciprocal(w_first[:, :], denom[:, :]))
                link(v.tensor_tensor(weights[:, 0, 0:tiles], w_first[:, :], g_prob[:, :], ALU.mult))
                link(v.tensor_tensor(weights[:, 1, 0:tiles], weights[:, 0, 0:tiles], ratio[:, :], ALU.mult))
                dve.wait_ge(ranked, 1)
                link(v.tensor_copy(counts[:, :], ps_n[:, 0:NE]))
                link(v.tensor_tensor(over[:, :, :], bcast_last(counts[:, :], tiles), bcast_mid(const("steps")[:, 0:tiles], NE), ALU.is_gt))
                link(v.tensor_reduce(blocks[:, :], over[:, :, :], AX, ALU.add))
                link(v.tensor_tensor_scan(ends[:, :], const("ones")[:, 0:NE], blocks[:, :], 0.0, ALU.mult, ALU.add))
                link(v.tensor_tensor(starts[:, :], ends[:, :], blocks[:, :], ALU.subtract))
                link(v.tensor_copy(ranks[:, :, :].rearrange("p t e -> p (t e)"), ps[:, 0:tiles * NE]))
                for k in range(2):
                    link(v.tensor_tensor(product[:, :, :], ranks[:, :, :], one[k][:, :, :], ALU.mult))
                    link(v.tensor_reduce(rank[:, :], product[:, :, :], AX, ALU.add))
                    link(v.tensor_tensor(product[:, :, :], bcast_mid(starts[:, :], tiles), one[k][:, :, :], ALU.mult))
                    link(v.tensor_reduce(base[:, :], product[:, :, :], AX, ALU.add))
                    link(v.tensor_tensor(steps_over[:, :, 1:], bcast_last(rank[:, :], tiles - 1),
                                         bcast_mid(const("steps")[:, 1:tiles], tiles), ALU.is_ge))
                    link(v.tensor_reduce(above[:, :], steps_over[:, :, 1:], AX, ALU.add))
                    link(v.scalar_tensor_tensor(local[:, :], above[:, :], -float(P), rank[:, :], ALU.mult, ALU.add))
                    link(v.tensor_tensor(block_of[:, :], base[:, :], above[:, :], ALU.add))
                    link(v.scalar_tensor_tensor(place[:, :], block_of[:, :], float(P), local[:, :], ALU.mult, ALU.add))
                    link(v.tensor_copy(slots[:, k, 0:tiles], place[:, :]))
                    link(v.scalar_tensor_tensor(where[:, :], local[:, :], float(nb), block_of[:, :], ALU.mult, ALU.add))
                    link(v.tensor_copy(table_at[k][:, :], where[:, :]))
                link(v.tensor_copy(token_id[:, :], const("token")[:, 0:tiles]))
                dve.sem_inc(routed, 1)
                link(v.tensor_tensor(passed[:, :, :], bcast_mid(ends[:, :], nb), bcast_last(const("iota_b")[:, 0:nb], NE), ALU.is_le))
                link(v.tensor_reduce(owner[:, :], passed[:, :, :], AX, ALU.add))
                link(v.tensor_scalar(block_info[:, 0:nb], owner[:, :], float(NE - 1), None, ALU.min))
                link(v.tensor_copy(block_info[:, nb:nb + 1], ends[:, NE - 1:NE]))

            @block.scalar
            def _(act):
                act.wait_ge(exp_ready, 1)
                nc.scalar.activation(g_exp[:, :, :], g_diff[:, :, :], ACT.Exp).then_inc(exped, 1)
                act.wait_ge(exp_ready, 2)
                nc.scalar.activation(ratio[:, :], diff[:, :], ACT.Exp).then_inc(exped, 1)

            @block.tensor
            def _(pe):
                pe.wait_ge(both_ready, 1)
                flat = lambda ap: ap.rearrange("p t e -> p (t e)")
                nc.tensor.matmul(ps[:, 0:tiles * NE], const("before"), flat(both[:, :, :]), start=True, stop=False)
                nc.tensor.matmul(ps[:, 0:tiles * NE], const("ones"), flat(seen[:, 0:tiles, :]), start=False, stop=True)
                nc.tensor.matmul(ps_n[:, 0:NE], const("ones"), seen[:, tiles, :], start=True, stop=True).then_inc(ranked, 1)

            @block.gpsimd
            def _(pool):
                nc.gpsimd.memset(zeros[:, :], 0).then_inc(zeroed, 1)
                pool.wait_ge(zeroed, 1)
                table = dr["table"][0:P * nb, :]
                pool.dma_start(table.rearrange("(p b) one -> p (b one)", p=P), zeros[:, :]).then_inc(zero_in, 16)
                pool.wait_ge(zero_in, 16)
                pool.wait_ge(routed, 1)
                for t in range(tiles):
                    for k in range(2):
                        pool.indirect_dma_start(table, bass.IndirectOffsetOnAxis(table_at[k][:, t:t + 1], 0),
                                                token_id[:, t:t + 1], None).then_inc(scattered, 16)
                pool.wait_ge(scattered, 32 * tiles)
                pool.dma_start(tokens[:, 0:nb], table.rearrange("(p b) one -> p (b one)", p=P)).then_inc(read_back, 16)
                pool.wait_ge(read_back, 16)


def stage_experts(nc, io, dr, const, layer, tiles, block_info, tokens):
    nb = n_blocks(tiles)
    with Stage(nc, f"moe{layer}") as st:
        wg, wu = ([st.sb(f"{n}{b}", [P, KD, DE]) for b in range(2)] for n in ("wg", "wu"))
        wd = [st.sb(f"wd{b}", [P, KE, D]) for b in range(2)]
        index = [st.sb(f"index{b}", [P, 1], I32) for b in range(2)]
        rows = [st.sb(f"rows{b}", [P, D]) for b in range(2)]
        xT = st.sb("xT", [P, KD, P])
        gate, act_up = ([st.sb(f"{n}{b}", [P, DE]) for b in range(2)] for n in ("gate", "act_up"))
        aT = st.sb("aT", [P, KE, P])
        y = [st.sb(f"y{b}", [P, D]) for b in range(2)]
        ps_x = st.ps("x", [P, 2 * BANK])
        ps_g, ps_u, ps_a = (st.ps(n, [P, BANK]) for n in ("g", "u", "a"))
        ps_y = st.ps("y", [P, 2 * BANK])
        g_in, u_in, d_in = (st.sems(n, 2) for n in ("g_in", "u_in", "d_in"))
        gathered = [st.pool_dma_sem(f"gathered{b}") for b in range(2)]
        stored = st.sem("stored")
        index_ready, turned, x_read_a, x_read_v, gate_full, up_full, gated, multiplied, a_turned, a_read, y_full, y_read_a, y_read_v = (
            st.sem(n) for n in ("index_ready", "turned", "x_read_a", "x_read_v", "gate_full", "up_full", "gated", "multiplied", "a_turned",
                                "a_read", "y_full", "y_read_a", "y_read_v"))
        ident = const("ident")
        experts = lambda name: io[name][layer]

        def looped(eng, first, second=None):
            used = eng.value_load(block_info[0:1, nb:nb + 1], min_val=1, max_val=nb)
            first(0, 0)
            first(0, 1)
            if second:
                second(0, 0)
            with eng.Fori(1, nb // 2 + 1) as i:
                for b in range(2):
                    with eng.If(used > 2 * i + b):
                        first(i, b)
                    if second:
                        with eng.If(used > 2 * i + b - 1):
                            second(i if b else i - 1, 1 - b)
            return used

        with nc.Block() as block:

            @block.sync
            def _(sp):
                def load(i, b):
                    n = 2 * i + b
                    e = sp.value_load(block_info[0:1, bass.ds(n, 1)], min_val=0, max_val=NE - 1)
                    if not isinstance(i, int):
                        sp.wait_ge(up_full, n)
                    sp.dma_start(wg[b][:, :, :], experts("moe_w_gate")[e].rearrange("(p k) n -> p k n", k=KD)).then_inc(g_in[b], 16)
                    sp.dma_start(wu[b][:, :, :], experts("moe_w_up")[e].rearrange("(p k) n -> p k n", k=KD)).then_inc(u_in[b], 16)
                    if not isinstance(i, int):
                        sp.wait_ge(y_full, n - 1)
                    sp.dma_start(wd[b][:, :, :], experts("moe_w_down")[e].rearrange("(p k) n -> p k n", k=KE)).then_inc(d_in[b], 16)

                looped(sp, load)

            @block.gpsimd
            def _(pool):
                def gather(i, b):
                    n = 2 * i + b
                    if not isinstance(i, int):
                        pool.wait_ge(turned, n - 1)
                    nc.gpsimd.tensor_copy(index[b][:, :], tokens[:, bass.ds(n, 1)]).then_inc(index_ready, 1)
                    pool.wait_ge(index_ready, n + 1)
                    st.settle(pool)
                    pool.indirect_dma_start(rows[b][:, :], None, dr["h"], bass.IndirectOffsetOnAxis(index[b][:, :], 0)).then_inc(gathered[b], 16)

                looped(pool, gather)

            @block.tensor
            def _(pe):
                pe.sem_inc(up_full, 1)

                def up(i, b):
                    n = 2 * i + b
                    pe.wait_ge(gathered[b], 16 * i + 16)
                    pe.wait_ge(x_read_a, n + 1)
                    pe.wait_ge(x_read_v, n + 1)
                    xs = rows[b][:, :].rearrange("t (p k) -> t k p", k=KD)
                    for k in range(KD):
                        last = nc.tensor.transpose(ps_x[:, k * P:(k + 1) * P], xs[:, k, :], ident)
                    last.then_inc(turned, 1)
                    pe.wait_ge(x_read_a, n + 2)
                    pe.wait_ge(x_read_v, n + 2)
                    pe.wait_ge(g_in[b], 16 * i + 16)
                    pe.wait_ge(gated, n + 1)
                    for k in range(KD):
                        last = nc.tensor.matmul(ps_g[:, :], xT[:, k, :], wg[b][:, k, :], start=(k == 0), stop=(k == KD - 1))
                    last.then_inc(gate_full, 1)
                    pe.wait_ge(u_in[b], 16 * i + 16)
                    pe.wait_ge(multiplied, n + 1)
                    for k in range(KD):
                        last = nc.tensor.matmul(ps_u[:, :], xT[:, k, :], wu[b][:, k, :], start=(k == 0), stop=(k == KD - 1))
                    last.then_inc(up_full, 1)

                def down(i, b):
                    n = 2 * i + b
                    pe.wait_ge(multiplied, n + 2)
                    pe.wait_ge(a_read, n + 1)
                    cols = act_up[b][:, :].rearrange("t (p k) -> t k p", k=KE)
                    for k in range(KE):
                        last = nc.tensor.transpose(ps_a[:, k * P:(k + 1) * P], cols[:, k, :], ident)
                    last.then_inc(a_turned, 1)
                    pe.wait_ge(a_read, n + 2)
                    pe.wait_ge(d_in[b], 16 * i + 16)
                    pe.wait_ge(y_read_a, n + 1)
                    pe.wait_ge(y_read_v, n + 1)
                    for c in range(2):
                        for k in range(KE):
                            last = nc.tensor.matmul(ps_y[:, c * BANK:(c + 1) * BANK], aT[:, k, :], wd[b][:, k, c * BANK:(c + 1) * BANK],
                                                    start=(k == 0), stop=(k == KE - 1))
                    last.then_inc(y_full, 1)

                looped(pe, up, down)

            @block.scalar
            def _(act):
                act.sem_inc(x_read_a, 1)
                act.sem_inc(gated, 1)
                act.sem_inc(a_read, 1)
                act.sem_inc(y_read_a, 1)
                act.sem_inc(stored, 16)

                def first(i, b):
                    n = 2 * i + b
                    act.wait_ge(turned, n + 1)
                    act.wait_ge(up_full, n + 1)
                    nc.scalar.activation(xT[:, 0:KD // 2, :].rearrange("p k t -> p (k t)"), ps_x[:, 0:BANK], ACT.Copy).then_inc(x_read_a, 1)
                    act.wait_ge(gate_full, n + 1)
                    act.wait_ge(multiplied, n + 1)
                    nc.scalar.activation(gate[b][:, :], ps_g[:, :], ACT.Silu).then_inc(gated, 1)

                def second(i, b):
                    n = 2 * i + b
                    act.wait_ge(a_turned, n + 1)
                    nc.scalar.activation(aT[:, :, :].rearrange("p k t -> p (k t)"), ps_a[:, :], ACT.Copy).then_inc(a_read, 1)
                    act.wait_ge(y_full, n + 1)
                    act.wait_ge(stored, 16 * n + 16)
                    nc.scalar.activation(y[b][:, 0:BANK], ps_y[:, 0:BANK], ACT.Copy).then_inc(y_read_a, 1)
                    act.wait_ge(y_read_a, n + 2)
                    act.wait_ge(y_read_v, n + 2)
                    act.dma_start(dr["y"][bass.ds(n * P, P), :], y[b][:, :]).then_inc(stored, 16)

                used = looped(act, first, second)
                act.wait_ge(stored, 16 * used + 16)
                st.settle(act)

            @block.vector
            def _(dve):
                dve.sem_inc(x_read_v, 1)
                dve.sem_inc(multiplied, 1)
                dve.sem_inc(y_read_v, 1)

                def first(i, b):
                    n = 2 * i + b
                    dve.wait_ge(turned, n + 1)
                    dve.wait_ge(up_full, n + 1)
                    nc.vector.tensor_copy(xT[:, KD // 2:, :].rearrange("p k t -> p (k t)"), ps_x[:, BANK:]).then_inc(x_read_v, 1)
                    dve.wait_ge(gated, n + 2)
                    dve.wait_ge(up_full, n + 2)
                    nc.vector.tensor_tensor(act_up[b][:, :], gate[b][:, :], ps_u[:, :], ALU.mult).then_inc(multiplied, 1)

                def second(i, b):
                    n = 2 * i + b
                    dve.wait_ge(y_full, n + 1)
                    dve.wait_ge(stored, 16 * n + 16)
                    nc.vector.tensor_copy(y[b][:, BANK:], ps_y[:, BANK:]).then_inc(y_read_v, 1)

                looped(dve, first, second)


def stage_combine(nc, io, dr, const, layer, tiles, weights, slots, out):
    with Stage(nc, f"mix{layer}") as st:
        kinds = 2 if tiles > NT_X else 1
        gate = [st.sb(f"gate{s}", [P, D]) for s in range(kinds)]
        ln_g, ln_b = st.sb("ln_g", [P, D]), st.sb("ln_b", [P, D])
        x, y1, y2 = ([st.sb(f"{n}{b}", [P, D]) for b in range(2)] for n in ("x", "y1_", "y2_"))
        mixed, both, gated, res, xn, xg = (st.sb(n, [P, D]) for n in ("mixed", "both", "gated", "res", "xn", "xg"))
        xo = [st.sb(f"xo{b}", [P, D]) for b in range(2)]
        stats, mv, var, root, rstd, bias = (st.sb(n, shape) for n, shape in (
            ("stats", [P, 2, 6]), ("mv", [P, 2]), ("var", [P, 1]), ("root", [P, 1]), ("rstd", [P, 1]), ("bias", [P, 1])))
        x_in, stored = (st.sems(n, 2) for n in ("x_in", "stored"))
        y1_in, y2_in = ([st.pool_dma_sem(f"{n}_in{b}") for b in range(2)] for n in ("first", "second"))
        rows_in, chain, rooted, normed, x_ready = (st.sem(n) for n in ("rows_in", "chain", "rooted", "normed", "x_ready"))
        STEPS = 11
        ROWS_IN = 16 * (2 + kinds)
        with nc.Block() as block:

            @block.sync
            def _(sp):
                load_rows(sp, rows_in, [(ln_g[:, :], io["ln_ffn_g"][layer]), (ln_b[:, :], io["ln_ffn_b"][layer])]
                          + [(gate[s][:, :], dr["mod"][layer, s, 5 * D:6 * D]) for s in range(kinds)])
                for t in range(tiles + 2):
                    if t < tiles:
                        if t >= 2:
                            sp.wait_ge(chain, STEPS * (t - 2) + 4)
                        sp.dma_start(x[t % 2][:, :], dr["x"][t * P:(t + 1) * P, :]).then_inc(x_in[t % 2], 16)
                    if t >= 2:
                        sp.wait_ge(x_ready, t - 1)
                        sp.dma_start(out(t - 2), xo[t % 2][:, :]).then_inc(stored[t % 2], 16)
                for b in range(2):
                    sp.wait_ge(stored[b], 16 * (tiles // 2))

            @block.gpsimd
            def _(pool):
                for t in range(tiles + 1):
                    if t < tiles:
                        if t >= 2:
                            pool.wait_ge(chain, STEPS * (t - 2) + 2)
                        for k, (dst, sem) in enumerate(((y1, y1_in), (y2, y2_in))):
                            pool.indirect_dma_start(dst[t % 2][:, :], None, dr["y"],
                                                    bass.IndirectOffsetOnAxis(slots[:, k, t:t + 1], 0)).then_inc(sem[t % 2], 16)
                    if t:
                        u = t - 1
                        if u == 0:
                            pool.wait_ge(rows_in, ROWS_IN)
                        pool.wait_ge(chain, STEPS * (u + 1))
                        if u >= 2:
                            pool.wait_ge(stored[u % 2], 16 * (u // 2))
                        nc.gpsimd.tensor_tensor(xo[u % 2][:, :], xg[:, :], ln_b[:, :], ALU.add).then_inc(x_ready, 1)

            @block.scalar
            def _(act):
                for t in range(tiles):
                    act.wait_ge(chain, STEPS * t + 8)
                    nc.scalar.activation(root[:, :], var[:, :], ACT.Sqrt).then_inc(rooted, 1)
                    act.wait_ge(chain, STEPS * t + 10)
                    nc.scalar.activation(xn[:, :], res[:, :], ACT.Identity, bias=bias[:, :], scale=rstd[:, :]).then_inc(normed, 1)

            @block.vector
            def _(dve):
                dve.wait_ge(rows_in, ROWS_IN)
                for t in range(tiles):
                    s, b, n = t // NT_X, t % 2, 16 * (t // 2) + 16
                    own = Chain(dve, chain, STEPS * t)
                    dve.wait_ge(y1_in[b], n)
                    own.link(nc.vector.tensor_scalar(mixed[:, :], y1[b][:, :], weights[:, 0, t:t + 1], None, ALU.mult))
                    dve.wait_ge(y2_in[b], n)
                    own.link(nc.vector.scalar_tensor_tensor(both[:, :], y2[b][:, :], weights[:, 1, t:t + 1], mixed[:, :], ALU.mult, ALU.add))
                    own.link(nc.vector.tensor_tensor(gated[:, :], both[:, :], gate[s][:, :], ALU.mult))
                    dve.wait_ge(x_in[b], n)
                    own.link(nc.vector.scalar_tensor_tensor(res[:, :], x[b][:, :], ALPHA, gated[:, :], ALU.mult, ALU.add))
                    for c in range(2):
                        own.inc(nc.vector.bn_stats(stats[:, c, :], res[:, c * BANK:(c + 1) * BANK]))
                    own.wait()
                    st.settle(dve)
                    own.link(nc.vector.bn_aggr(mv[:, :], stats[:, :, :].rearrange("p n s -> p (n s)")))
                    own.link(nc.vector.tensor_scalar(var[:, :], mv[:, 1:2], LN_EPS, None, ALU.add))
                    dve.wait_ge(rooted, t + 1)
                    own.link(nc.vector.reciprocal(rstd[:, :], root[:, :]))
                    own.link(nc.vector.tensor_scalar(bias[:, :], mv[:, 0:1], rstd[:, :], -1.0, ALU.mult, ALU.mult))
                    dve.wait_ge(normed, t + 1)
                    if t:
                        dve.wait_ge(x_ready, t)
                    own.link(nc.vector.tensor_tensor(xg[:, :], xn[:, :], ln_g[:, :], ALU.mult))
                    assert own.n == STEPS


INPUTS = ["x", "c", "ctx", "c_ctx", "ada_w", "ada_b", "ln_mix_g", "ln_mix_b", "ln_ffn_g", "ln_ffn_b",
          "win_w_in", "win_w_out", "win_sink", "mla_w_in", "mla_q_norm", "mla_kv_norm", "mla_w_uq", "mla_w_ukv",
          "mla_w_out", "moe_w_grp", "moe_b_grp", "moe_w_rt", "moe_b_rt", "moe_w_gate", "moe_w_up", "moe_w_down"]


def program(nc, io, const_dram, const_cols, result):
    nb = n_blocks(NT_ALL)
    dr = {name: nc.dram_tensor(f"scratch_{name}", shape, dt, kind="Internal").ap() for name, shape, dt in (
        ("x", (TALL, D), F32), ("mod", (2, 2, 6 * D), F32), ("qkT", (A_QK_CHUNKS * P, TALL), F32), ("o", (TALL, D), F32),
        ("h", (TALL, D), F32), ("table", (P * nb, 1), I32), ("y", ((nb + 2) * P, D), F32))}

    def constants(st, names):
        tiles = {n: st.sb(n, [P, const_cols[n][1]]) for n in names}
        loaded = st.sem("loaded")
        with nc.Block() as block:

            @block.sync
            def _(sp):
                for n in names:
                    at, size = const_cols[n]
                    sp.dma_start(tiles[n][:, :], const_dram[:, at:at + size]).then_inc(loaded, 16)
                sp.wait_ge(loaded, 16 * len(names))

        return tiles

    with Stage(nc, "all") as every:
        Stage.settled = every.sem("settled")
        Stage.pool_dma = every.stack
        fixed = constants(every, ["ident", "ones"])
        const = lambda n: fixed[n][:, :]
        stage_mods(nc, io, dr, const)

        def feed_forward(layer, tiles, w_out, out):
            with Stage(nc, f"ff{layer}") as ff:
                logits = ff.sb("logits", [P, tiles * ROUTE])
                weights = ff.sb("weights", [P, 2, tiles])
                slots = ff.sb("slots", [P, 2, tiles], I32)
                block_info = ff.sb("block_info", [P, n_blocks(tiles) + 4], I32)
                tokens = ff.sb("tokens", [P, n_blocks(tiles) + 4], I32)
                stage_project_out(nc, io, dr, const, layer, w_out, tiles, logits)
                with Stage(nc, f"routing{layer}") as rt:
                    tables = constants(rt, ["before", "iota_e", "iota_g", "steps", "iota_b", "token"])
                    routing = lambda n: (tables[n] if n in tables else fixed[n])[:, :]
                    stage_route(nc, dr, routing, layer, tiles, logits, weights, slots, block_info, tokens)
                stage_experts(nc, io, dr, const, layer, tiles, block_info, tokens)
                stage_combine(nc, io, dr, const, layer, tiles, weights, slots, out)

        with Stage(nc, "layer0") as l0:
            v_all = l0.sb("v_all", [P, NT_ALL, A_KV * A_HD])
            with Stage(nc, "layer0_qkv") as lq:
                hT = lq.sb("hT", [P, KD, TALL])
                stage_transposed(nc, dr, const, hT, 0)
                tables = constants(lq, ["rot_a", "cos_a", "sin_a"])
                stage_window_qkv(nc, io, dr, lambda n: tables[n][:, :], hT, v_all)
            with Stage(nc, "layer0_att") as la:
                tables_m = constants(la, ["mask"])
                window = lambda n: (tables_m[n] if n in tables_m else fixed[n])[:, :]
                stage_window_attention(nc, io, dr, window, v_all)
        feed_forward(0, NT_ALL, io["win_w_out"][0], lambda t: dr["x"][t * P:(t + 1) * P, :])

        with Stage(nc, "layer1") as l1:
            tables_b = constants(l1, ["rot_b", "cos_b", "sin_b", "cos_k", "sin_k"])
            latent = lambda n: (tables_b[n] if n in tables_b else fixed[n])[:, :]
            cqT = l1.sb("cqT", [P, B_QR // P, SEQ])
            ckvT = l1.sb("ckvT", [P, B_KVR // P, TALL])
            kT = l1.sb("kT", [B_QD, TALL])
            stage_latents(nc, io, dr, latent, cqT, ckvT, kT)
            stage_latent_attention(nc, io, dr, latent, cqT, ckvT, kT)
        feed_forward(1, NT_X, io["mla_w_out"][0], lambda t: result[0, t * P:(t + 1) * P, :])


def kernel(**inputs):
    import concourse.bacc as bacc
    from concourse.bass_utils import run_bass_kernel_spmd

    nc = bacc.Bacc("TRN2", target_bir_lowering=False, num_devices=1)
    arrays, io = {}, {}
    for name in INPUTS:
        a = np.ascontiguousarray(inputs[name])
        arrays[f"in_{name}"] = a
        io[name] = nc.dram_tensor(f"in_{name}", a.shape, mybir.dt.from_np(a.dtype), kind="ExternalInput").ap()
    table, cols = constant_arrays()
    arrays["in_tables"] = table
    const_dram = nc.dram_tensor("in_tables", table.shape, F32, kind="ExternalInput").ap()
    result = nc.dram_tensor("out_x", (1, SEQ, D), F32, kind="ExternalOutput").ap()
    program(nc, io, const_dram, cols, result)
    return run_bass_kernel_spmd(nc, [arrays], core_ids=[0]).results[0]["out_x"]
```

```python
from contextlib import ExitStack

import numpy as np

import concourse.bass as bass
from concourse import mybir
from concourse.alu_op_type import AluOpType as ALU

F32 = mybir.dt.float32
BF16 = mybir.dt.bfloat16
I32 = mybir.dt.int32
ACT = mybir.ActivationFunctionType
AX = mybir.AxisListType.X

P = 128
D = 1024
KD = D // P
SEQ, CTX = 1024, 256
TALL = SEQ + CTX
NT_X, NT_C = SEQ // P, CTX // P
NT_ALL = NT_X + NT_C
BANK = 512
GRID_W = 64
ALPHA = 4.0 ** 0.25
LN_EPS, RMS_EPS = 1e-5, 1e-6

A_HEADS, A_KV, A_GROUP, A_HD = 16, 4, 4, 64
A_QK_CHUNKS = (A_HEADS + A_KV) * A_HD // P
A_SCALE = A_HD ** -0.5

B_HEADS, B_NOPE, B_ROPE, B_V = 16, 64, 32, 64
B_QR, B_KVR = 512, 256
B_QD = B_NOPE + B_ROPE
B_IN = B_QR + B_KVR + B_ROPE
B_SCALE = B_QD ** -0.5

NG, EPG = 4, 8
NE = NG * EPG
DE = 512
KE = DE // P
BIG = 1.0e30
ROUTE = NG + NE


def n_blocks(tiles):
    return tiles * 2 + NE


def rope_angles(rot_dim):
    axis = rot_dim // 2
    inv = (np.float32(10000.0) ** (-np.arange(0, axis, 2, dtype=np.float32) / np.float32(axis))).astype(np.float32)
    pos = np.arange(SEQ)
    row = (pos // GRID_W).astype(np.float32)
    col = (pos % GRID_W).astype(np.float32)
    ang = np.zeros((rot_dim, SEQ), np.float32)
    partner = np.zeros(rot_dim, int)
    sign = np.zeros(rot_dim, np.float32)
    half = axis // 2
    for a, where in enumerate((row, col)):
        for j in range(axis):
            d = a * axis + j
            ang[d] = where * inv[j % half]
            partner[d] = d + half if j < half else d - half
            sign[d] = -1.0 if j < half else 1.0
    return ang, partner, sign


def constant_arrays():
    cols, parts = {}, []

    def add(name, a):
        full = np.zeros((P, a.shape[1]), np.float32)
        full[: a.shape[0]] = a
        at = sum(x.shape[1] for x in parts)
        cols[name] = (at, a.shape[1])
        parts.append(full)

    add("ident", np.eye(P, dtype=np.float32))
    add("ones", np.ones((P, P), np.float32))
    r, c = np.arange(P)[:, None], np.arange(P)[None, :]
    add("before", (r < c).astype(np.float32))
    add("mask", np.concatenate([np.where(c >= r, 0.0, -BIG), np.where(c <= r, 0.0, -BIG)], 1))
    ang, partner, sign = rope_angles(A_HD)
    rot = np.zeros((A_HD, A_HD), np.float32)
    rot[partner, np.arange(A_HD)] = sign
    two = np.zeros((P, P), np.float32)
    two[:A_HD, :A_HD] = rot
    two[A_HD:, A_HD:] = rot
    add("rot_a", two)
    add("cos_a", np.concatenate([np.cos(ang)] * 2, 0))
    add("sin_a", np.concatenate([np.sin(ang)] * 2, 0))
    ang, partner, sign = rope_angles(B_ROPE)
    rot = np.zeros((B_QD, B_QD), np.float32)
    rot[B_NOPE + partner, B_NOPE + np.arange(B_ROPE)] = sign
    add("rot_b", rot)
    add("cos_b", np.concatenate([np.ones((B_NOPE, SEQ)), np.cos(ang)], 0))
    add("sin_b", np.concatenate([np.zeros((B_NOPE, SEQ)), np.sin(ang)], 0))
    add("cos_k", np.cos(ang).T.reshape(NT_X, P, B_ROPE).transpose(1, 0, 2).reshape(P, -1))
    add("sin_k", (np.sin(ang) * sign[:, None]).T.reshape(NT_X, P, B_ROPE).transpose(1, 0, 2).reshape(P, -1))
    add("iota_e", np.broadcast_to(np.arange(NE) - 64.0, (P, NE)))
    add("iota_g", np.broadcast_to(np.arange(NG) - 64.0, (P, NG)))
    add("steps", np.broadcast_to(np.arange(NT_ALL) * float(P), (P, NT_ALL)))
    nb = n_blocks(NT_ALL)
    add("iota_b", np.broadcast_to(np.arange(nb) * 1.0, (P, nb)))
    add("token", np.arange(P)[:, None] + np.arange(NT_ALL)[None, :] * float(P))
    return np.ascontiguousarray(np.concatenate(parts, 1), np.float32), cols


def bcast_last(ap, n):
    return ap.unsqueeze(2).broadcast_to([ap.shape[0], ap.shape[1], n])


def bcast_mid(ap, n):
    return ap.unsqueeze(1).broadcast_to([ap.shape[0], n, ap.shape[1]])


class Chain:

    def __init__(self, eng, sem, base=0):
        self.eng, self.sem, self.base, self.n = eng, sem, base, 0

    def inc(self, instruction):
        self.n += 1
        instruction.then_inc(self.sem, 1)
        return instruction

    def wait(self):
        self.eng.wait_ge(self.sem, self.base + self.n)

    def link(self, instruction):
        self.inc(instruction)
        self.wait()


class Stage:

    settled = None

    def settle(self, eng):
        eng.sem_inc(Stage.settled, 1)

    def __init__(self, nc, name):
        self.nc, self.name, self.stack, self.used = nc, name, ExitStack(), []

    def __enter__(self):
        self.stack.__enter__()
        return self

    def __exit__(self, *a):
        if self.used and a[0] is None:
            with self.nc.Block() as block:

                @block.sync
                def _(sp):
                    for sem in self.used:
                        sp.sem_clear(sem)

        return self.stack.__exit__(*a)

    def sb(self, name, shape, dt=F32):
        return self.stack.enter_context(self.nc.sbuf_tensor(f"{self.name}_{name}", shape, dt))

    def ps(self, name, shape):
        return self.stack.enter_context(self.nc.psum_tensor(f"{self.name}_ps_{name}", shape, F32))

    def sem(self, name):
        self.used.append(self.stack.enter_context(self.nc.semaphore(f"{self.name}_{name}")))
        return self.used[-1]

    def pool_dma_sem(self, name):
        return Stage.pool_dma.enter_context(self.nc.semaphore(f"{self.name}_{name}"))

    def sems(self, name, n):
        return [self.sem(f"{name}{i}") for i in range(n)]


def stage_mods(nc, io, dr, const):
    PAIRS = 6 * D // BANK // 2
    BUFS = 4
    with Stage(nc, "mods") as st:
        w = [st.sb(f"w{b}", [P, KD, BANK]) for b in range(BUFS)]
        bias = st.sb("bias", [2, 2, 6 * D])
        rows = st.sb("rows", [2, 2, 6 * D])
        c_col = st.sb("c_col", [P, 2, KD])
        s_col = st.sb("s_col", [P, 2, KD])
        ps = [st.ps(f"ps{b}", [P, BANK]) for b in range(BUFS)]
        w_in, ps_full, ps_free = (st.sems(n, BUFS) for n in ("w_in", "ps_full", "ps_free"))
        c_in, bias_in, s_ready, copied, stored = (st.sem(n) for n in ("c_in", "bias_in", "s_ready", "copied", "stored"))
        with nc.Block() as block:

            @block.sync
            def _(sp):
                sp.dma_start(c_col[:, 0, :], io["c"][0].rearrange("(p k) -> p k", k=KD)).then_inc(c_in, 16)
                sp.dma_start(c_col[:, 1, :], io["c_ctx"].rearrange("(p k) -> p k", k=KD)).then_inc(c_in, 16)

                def load(i, b):
                    src = io["ada_w"][b // 2].rearrange("(p k) n -> p k n", k=KD)
                    sp.dma_start(w[b][:, :, :], src[:, :, bass.ds((i * 2 + b % 2) * BANK, BANK)]).then_inc(w_in[b], 16)

                for b in range(BUFS):
                    load(0, b)
                with sp.Fori(1, PAIRS) as i:
                    for b in range(BUFS):
                        sp.wait_ge(ps_full[b], i)
                        load(i, b)
                for b in range(BUFS):
                    sp.wait_ge(ps_free[b], PAIRS + 1)
                for l in range(2):
                    sp.dma_start(dr["mod"][l], rows[:, l, :]).then_inc(stored, 16)
                sp.wait_ge(stored, 32)
                sp.wait_ge(copied, 32)

            @block.scalar
            def _(act):
                for l in range(2):
                    act.dma_start(bias[:, l, :], io["ada_b"][l].partition_broadcast(2)).then_inc(bias_in, 16)
                act.wait_ge(c_in, 32)
                nc.scalar.activation(s_col[:, :, :], c_col[:, :, :], ACT.Silu).then_inc(s_ready, 1)
                act.dma_start(dr["x"][0:SEQ, :], io["x"][0]).then_inc(copied, 16)
                act.dma_start(dr["x"][SEQ:TALL, :], io["ctx"][0]).then_inc(copied, 16)

            @block.vector
            def _(dve):
                for b in range(BUFS):
                    dve.sem_inc(ps_free[b], 1)
                dve.wait_ge(bias_in, 32)
                with dve.Fori(0, PAIRS) as i:
                    for b in range(BUFS):
                        at = bass.ds((i * 2 + b % 2) * BANK, BANK)
                        dve.wait_ge(ps_full[b], i + 1)
                        nc.vector.tensor_tensor(rows[:, b // 2, at], ps[b][0:2, :], bias[:, b // 2, at],
                                                ALU.add).then_inc(ps_free[b], 1)

            @block.tensor
            def _(pe):
                pe.wait_ge(s_ready, 1)
                with pe.Fori(0, PAIRS) as i:
                    for b in range(BUFS):
                        pe.wait_ge(ps_free[b], i + 1)
                        pe.wait_ge(w_in[b], 16 * i + 16)
                        for k in range(KD):
                            last = nc.tensor.matmul(ps[b][0:2, :], s_col[:, :, k], w[b][:, k, :],
                                                    start=(k == 0), stop=(k == KD - 1))
                        last.then_inc(ps_full[b], 1)


def stage_transposed(nc, dr, const, hT, layer):
    with Stage(nc, f"tr{layer}") as st:
        x = [st.sb(f"x{b}", [P, D]) for b in range(2)]
        shift = st.sb("shift", [P, 2, KD])
        scale = st.sb("scale", [P, 2, KD])
        scale1 = st.sb("scale1", [P, 2, KD])
        ps = [st.ps(f"ps{b}", [P, 2 * BANK]) for b in range(2)]
        x_in, ps_full, ps_free_a, ps_free_v = (st.sems(n, 2) for n in ("x_in", "ps_full", "ps_free_a", "ps_free_v"))
        m_in, m_ready = st.sem("m_in"), st.sem("m_ready")
        ident = const("ident")

        def halves(eng, per):
            with eng.Fori(0, NT_X // 2) as i:
                for b in range(2):
                    per(i, b, 0)
            for b in range(2):
                per(NT_X // 2, b, 1)

        with nc.Block() as block:

            @block.sync
            def _(sp):
                for s in range(2):
                    for tile, part in ((shift, 0), (scale, 1)):
                        sp.dma_start(tile[:, s, :], dr["mod"][layer, s, part * D:(part + 1) * D].rearrange("(p k) -> p k", k=KD)).then_inc(m_in, 16)

                def load(i, b):
                    sp.dma_start(x[b][:, :], dr["x"][bass.ds((i * 2 + b) * P, P), :]).then_inc(x_in[b], 16)

                for b in range(2):
                    load(0, b)
                with sp.Fori(1, NT_ALL // 2) as i:
                    for b in range(2):
                        sp.wait_ge(ps_full[b], i)
                        load(i, b)

            @block.tensor
            def _(pe):
                def turn(i, b, s):
                    pe.wait_ge(x_in[b], 16 * i + 16)
                    pe.wait_ge(ps_free_a[b], i + 1)
                    pe.wait_ge(ps_free_v[b], i + 1)
                    rows = x[b][:, :].rearrange("t (p k) -> t k p", k=KD)
                    for k in range(KD):
                        last = nc.tensor.transpose(ps[b][:, k * P:(k + 1) * P], rows[:, k, :], ident)
                    last.then_inc(ps_full[b], 1)

                halves(pe, turn)

            @block.scalar
            def _(act):
                for b in range(2):
                    act.sem_inc(ps_free_a[b], 1)
                act.wait_ge(m_ready, 1)

                def out(i, b, s):
                    act.wait_ge(ps_full[b], i + 1)
                    for k in range(0, KD // 2):
                        last = nc.scalar.activation(hT[:, k, bass.ds((i * 2 + b) * P, P)], ps[b][:, k * P:(k + 1) * P],
                                                    ACT.Identity, bias=shift[:, s, k:k + 1], scale=scale1[:, s, k:k + 1])
                    last.then_inc(ps_free_a[b], 1)

                halves(act, out)

            @block.vector
            def _(dve):
                for b in range(2):
                    dve.sem_inc(ps_free_v[b], 1)
                dve.wait_ge(m_in, 64)
                nc.vector.tensor_scalar(scale1[:, :, :], scale[:, :, :], 1.0, None, ALU.add).then_inc(m_ready, 1)
                dve.wait_ge(m_ready, 1)

                def out(i, b, s):
                    dve.wait_ge(ps_full[b], i + 1)
                    for k in range(KD // 2, KD):
                        last = nc.vector.tensor_scalar(hT[:, k, bass.ds((i * 2 + b) * P, P)], ps[b][:, k * P:(k + 1) * P],
                                                       scale1[:, s, k:k + 1], shift[:, s, k:k + 1], ALU.mult, ALU.add)
                    last.then_inc(ps_free_v[b], 1)

                halves(dve, out)


N_CUTS = [(0, BANK), (BANK, BANK), (2 * BANK, CTX)]


def stage_window_qkv(nc, io, dr, const, hT, v_all):
    with Stage(nc, "qkv") as st:
        w = [st.sb(f"w{b}", [P, KD, P]) for b in range(2)]
        wv = st.sb("wv", [P, KD, A_KV * A_HD])
        raw = [st.sb(f"raw{b}", [P, SEQ]) for b in range(2)]
        rawcos = [st.sb(f"rawcos{b}", [P, SEQ]) for b in range(2)]
        rotsin = [st.sb(f"rotsin{b}", [P, SEQ]) for b in range(2)]
        out = [st.sb(f"out{b}", [P, TALL]) for b in range(2)]
        ps = [st.ps(f"ps{n}", [P, BANK]) for n in range(3)]
        ps_rot = [st.ps(f"rot{n}", [P, BANK]) for n in range(2)]
        w_in, cos_ready, out_ready, stored = (st.sems(n, 2) for n in ("w_in", "cos_ready", "out_ready", "stored"))
        ps_full, copied = (st.sems(n, 3) for n in ("ps_full", "copied"))
        rot_full, rotsin_ready = (st.sems(n, 2) for n in ("rot_full", "rotsin_ready"))
        zeros = st.sb("zeros", [P, D])
        wv_in, v_full, v_read, zeros_ready, zeroed = (st.sem(n) for n in ("wv_in", "v_full", "v_read", "zeros_ready", "zeroed"))
        cos, sin, rot = const("cos_a"), const("sin_a"), const("rot_a")
        w_dram = io["win_w_in"][0].rearrange("(p k) n -> p k n", k=KD)
        PAIRS = A_QK_CHUNKS // 2
        with nc.Block() as block:

            @block.sync
            def _(sp):
                def load(i, b):
                    sp.dma_start(w[b][:, :, :], w_dram[:, :, bass.ds((i * 2 + b) * P, P)]).then_inc(w_in[b], 16)

                def store(i, b):
                    sp.wait_ge(out_ready[b], i + 2)
                    st.settle(sp)
                    sp.wait_ge(copied[2], 2 * i + b + 2)
                    st.settle(sp)
                    sp.dma_start(dr["qkT"][bass.ds((i * 2 + b) * P, P), :], out[b][:, :]).then_inc(stored[b], 16)

                for b in range(2):
                    sp.sem_inc(stored[b], 16)
                    load(0, b)
                sp.dma_start(wv[:, :, :], w_dram[:, :, A_QK_CHUNKS * P:]).then_inc(wv_in, 16)
                sp.wait_ge(zeros_ready, 1)
                y_rows = dr["y"].rearrange("(b p) d -> p b d", p=P)
                sp.dma_start(y_rows, zeros[:, :].unsqueeze(1).broadcast_to([P, y_rows.shape[1], D])).then_inc(zeroed, 16)
                with sp.Fori(1, PAIRS) as i:
                    for b in range(2):
                        sp.wait_ge(ps_full[2], 2 * i + b - 1)
                        load(i, b)
                        store(i - 1, b)
                for b in range(2):
                    store(PAIRS - 1, b)
                for b in range(2):
                    sp.wait_ge(stored[b], 16 * PAIRS + 16)
                sp.wait_ge(zeroed, 16)

            @block.tensor
            def _(pe):
                for n in range(2):
                    pe.sem_inc(rot_full[n], 2)
                with pe.Fori(0, PAIRS) as i:
                    for b in range(2):
                        pe.wait_ge(w_in[b], 16 * i + 16)
                        for n, (at, size) in enumerate(N_CUTS):
                            pe.wait_ge(copied[n], 2 * i + b + 1)
                            for k in range(KD):
                                last = nc.tensor.matmul(ps[n][:, 0:size], w[b][:, k, :], hT[:, k, at:at + size],
                                                        start=(k == 0), stop=(k == KD - 1))
                            last.then_inc(ps_full[n], 1)
                        for n in range(2):
                            pe.wait_ge(copied[n], 2 * i + b + 2)
                            pe.wait_ge(rotsin_ready[n], 2 * i + b + 1)
                            nc.tensor.matmul(ps_rot[n][:, :], rot, raw[b][:, n * BANK:(n + 1) * BANK],
                                             start=True, stop=True).then_inc(rot_full[n], 1)
                pe.wait_ge(wv_in, 16)
                for t in range(NT_ALL):
                    if t < 3:
                        pe.wait_ge(copied[t], 2 * PAIRS + 1)
                    else:
                        pe.wait_ge(v_read, t - 2)
                    for k in range(KD):
                        last = nc.tensor.matmul(ps[t % 3][:, 0:A_KV * A_HD], hT[:, k, t * P:(t + 1) * P], wv[:, k, :],
                                                start=(k == 0), stop=(k == KD - 1))
                    last.then_inc(v_full, 1)

            @block.scalar
            def _(act):
                for n in range(3):
                    act.sem_inc(copied[n], 1)
                with act.Fori(0, PAIRS) as i:
                    for b in range(2):
                        act.wait_ge(cos_ready[b], i + 1)
                        for n in range(2):
                            act.wait_ge(rot_full[n], 2 * i + b + 1)
                            act.wait_ge(ps_full[n], 2 * i + b + 1)
                            nc.scalar.activation(raw[b][:, n * BANK:(n + 1) * BANK], ps[n][:, :], ACT.Copy).then_inc(copied[n], 1)
                        act.wait_ge(ps_full[2], 2 * i + b + 1)
                        act.wait_ge(stored[b], 16 * i + 16)
                        nc.scalar.activation(out[b][:, SEQ:TALL], ps[2][:, 0:CTX], ACT.Copy).then_inc(copied[2], 1)
                for t in range(NT_ALL):
                    act.wait_ge(v_full, t + 1)
                    nc.scalar.activation(v_all[:, t, :], ps[t % 3][:, 0:A_KV * A_HD], ACT.Copy).then_inc(v_read, 1)

            @block.gpsimd
            def _(pool):
                nc.gpsimd.memset(zeros[:, :], 0.0).then_inc(zeros_ready, 1)
                for b in range(2):
                    pool.sem_inc(cos_ready[b], 1)
                with pool.Fori(0, PAIRS) as i:
                    for b in range(2):
                        for n in range(2):
                            pool.wait_ge(copied[n], 2 * i + b + 2)
                        pool.wait_ge(out_ready[b], i + 1)
                        nc.gpsimd.tensor_tensor(rawcos[b][:, :], raw[b][:, :], cos, ALU.mult).then_inc(cos_ready[b], 1)

            @block.vector
            def _(dve):
                for n in range(2):
                    dve.sem_inc(rotsin_ready[n], 1)
                    dve.sem_inc(out_ready[n], 1)
                with dve.Fori(0, PAIRS) as i:
                    for b in range(2):
                        dve.wait_ge(out_ready[b], i + 1)
                        for n in range(2):
                            dve.wait_ge(rot_full[n], 2 * i + b + 3)
                            nc.vector.tensor_tensor(rotsin[b][:, n * BANK:(n + 1) * BANK], ps_rot[n][:, :],
                                                    sin[:, n * BANK:(n + 1) * BANK], ALU.mult).then_inc(rotsin_ready[n], 1)
                        for n in range(2):
                            dve.wait_ge(rotsin_ready[n], 2 * i + b + 2)
                        dve.wait_ge(cos_ready[b], i + 2)
                        dve.wait_ge(stored[b], 16 * i + 16)
                        nc.vector.tensor_tensor(out[b][:, 0:SEQ], rawcos[b][:, :], rotsin[b][:, :], ALU.add).then_inc(out_ready[b], 1)


def stage_window_attention(nc, io, dr, const, v_all):
    BLOCKS = NT_ALL
    STEPS = BLOCKS * A_GROUP
    W3 = 3 * P
    with Stage(nc, "wat") as st:
        q = st.sb("q", [A_HD, A_GROUP, TALL])
        k = st.sb("k", [A_HD, TALL])
        ident_h, mask_h = st.sb("ident_h", [P, P], BF16), st.sb("mask_h", [P, 2 * P], BF16)
        sinks, sink, neg_sink = st.sb("sinks", [P, A_HEADS]), st.sb("sink", [P, A_GROUP]), st.sb("neg_sink", [P, A_GROUP])
        probs = [st.sb(f"probs{b}", [P, W3 + CTX]) for b in range(2)]
        probsT = [st.sb(f"probsT{b}", [P, W3 + CTX]) for b in range(2)]
        outs = [st.sb(f"outs{b}", [P, A_GROUP * A_HD]) for b in range(2)]
        top, neg_max, total, sink_exp, denom, inv = (st.sb(n, [P, 4]) for n in ("top", "neg_max", "total", "sink_exp", "denom", "inv"))
        ps_s = [st.ps(f"s{b}", [P, 2 * BANK]) for b in range(2)]
        ps_t = [st.ps(f"t{b}", [P, BANK]) for b in range(2)]
        ps_o = [st.ps(f"o{b}", [P, BANK]) for b in range(2)]
        q_in, k_in, sinks_in, sink_ready, const_ready = (st.sem(n) for n in ("q_in", "k_in", "sinks_in", "sink_ready", "const_ready"))
        scored, top_ready, max_ready, exp_done, sink_exp_done, pv_full, inv_step, out_done = (
            st.sem(n) for n in ("scored", "top_ready", "max_ready", "exp_done", "sink_exp_done", "pv_full", "inv_step", "out_done"))
        turned, turned_read = st.sems("turned", 2), st.sems("turned_read", 2)
        stored = st.sems("stored", 2)
        ident = const("ident")

        def shape_of(u):
            blk = u // A_GROUP
            tiles = [t for t in (blk - 1, blk, blk + 1) if 0 <= t < NT_X] if blk < NT_X else []
            keys = tiles + [NT_X, NT_X + 1]
            return blk, tiles, keys, BANK - P * len(tiles), (len(keys) + 1) // 2

        with nc.Block() as block:

            @block.sync
            def _(sp):
                sp.dma_start(sinks[:, :], io["win_sink"][0].partition_broadcast(P)).then_inc(sinks_in, 16)
                for b in range(2):
                    sp.sem_inc(stored[b], 16)

                def load(g):
                    sp.dma_start(q[:, :, :], dr["qkT"][bass.ds(g * A_GROUP * A_HD, A_GROUP * A_HD), :]
                                 .rearrange("(h d) t -> d h t", d=A_HD)).then_inc(q_in, 16)
                    sp.dma_start(k[:, :], dr["qkT"][bass.ds(g * A_HD + A_HEADS * A_HD, A_HD), :]).then_inc(k_in, 16)

                def store(g):
                    for blk in range(BLOCKS):
                        sp.wait_ge(out_done, g * STEPS + A_GROUP * (blk + 1) + 2)
                        st.settle(sp)
                        sp.dma_start(dr["o"][blk * P:(blk + 1) * P, bass.ds(g * A_GROUP * A_HD, A_GROUP * A_HD)],
                                     outs[blk % 2][:, :]).then_inc(stored[blk % 2], 16)

                load(0)
                store(0)
                with sp.Fori(1, A_KV) as g:
                    sp.wait_ge(scored, g * STEPS)
                    load(g)
                    store(g)
                for b in range(2):
                    sp.wait_ge(stored[b], 16 * (A_KV * BLOCKS // 2 + 1))

            @block.gpsimd
            def _(pool):
                nc.gpsimd.tensor_copy(ident_h[:, :], ident).then_inc(const_ready, 1)
                nc.gpsimd.tensor_copy(mask_h[:, :], const("mask")).then_inc(const_ready, 1)

            @block.tensor
            def _(pe):
                pe.sem_inc(pv_full, 2)
                pe.sem_inc(turned[0], 2)
                pe.sem_inc(turned[1], 2)
                pe.wait_ge(const_ready, 2)
                with pe.Fori(0, A_KV) as g:

                    def scores(u):
                        blk, tiles, keys, at, _ = shape_of(u)
                        s = ps_s[u % 2]
                        qb = q[:, u % A_GROUP, blk * P:(blk + 1) * P]
                        pe.wait_ge(exp_done, g * STEPS + u + 1)
                        if tiles:
                            nc.tensor.matmul(s[:, at:BANK], qb, k[:, tiles[0] * P:(tiles[-1] + 1) * P], start=True, stop=False)
                            for t, m in ((blk - 1, 0), (blk + 1, 1)):
                                if t in tiles:
                                    c = at + (t - tiles[0]) * P
                                    nc.tensor.matmul(s[:, c:c + P], ident_h[:, :], mask_h[:, m * P:(m + 1) * P],
                                                     start=False, stop=(t == tiles[-1]) or blk == NT_X - 1)
                        nc.tensor.matmul(s[:, BANK:BANK + CTX], qb, k[:, SEQ:TALL], start=True, stop=True).then_inc(scored, 1)

                    def turn(u):
                        _, _, keys, _, cut = shape_of(u)
                        pe.wait_ge(exp_done, g * STEPS + u + 3)
                        for half, cs in ((0, range(0, cut)), (1, range(cut, len(keys)))):
                            pe.wait_ge(turned_read[half], g * STEPS + u + 1)
                            for c in cs:
                                last = nc.tensor.transpose(ps_t[half][:, (c - cs[0]) * P:(c - cs[0] + 1) * P],
                                                           probs[u % 2][:, c * P:(c + 1) * P], ident)
                            last.then_inc(turned[half], 1)

                    def mix(u):
                        _, _, keys, _, _ = shape_of(u)
                        for half in range(2):
                            pe.wait_ge(turned_read[half], g * STEPS + u + 2)
                        pe.wait_ge(out_done, g * STEPS + u + 1)
                        for c, t in enumerate(keys):
                            last = nc.tensor.matmul(ps_o[u % 2][:, 0:A_HD], probsT[u % 2][:, c * P:(c + 1) * P],
                                                    v_all[:, t, bass.ds(g * A_HD, A_HD)], start=(c == 0), stop=(c == len(keys) - 1))
                        last.then_inc(pv_full, 1)

                    pe.wait_ge(q_in, 16 * g + 16)
                    pe.wait_ge(k_in, 16 * g + 16)
                    scores(0)
                    for u in range(STEPS):
                        if u + 1 < STEPS:
                            scores(u + 1)
                        if u:
                            mix(u - 1)
                        turn(u)
                    mix(STEPS - 1)

            @block.scalar
            def _(act):
                act.sem_inc(exp_done, 2)
                act.sem_inc(turned_read[0], 1)
                act.wait_ge(sinks_in, 16)
                with act.Fori(0, A_KV) as g:
                    act.wait_ge(out_done, g * STEPS + 2)
                    nc.scalar.activation(sink[:, :], sinks[:, bass.ds(g * A_GROUP, A_GROUP)], ACT.Copy).then_inc(sink_ready, 1)
                    nc.scalar.activation(neg_sink[:, :], sinks[:, bass.ds(g * A_GROUP, A_GROUP)], ACT.Copy, scale=-1.0).then_inc(sink_ready, 1)
                    act.wait_ge(sink_ready, 2 * g + 2)

                    def exps(u):
                        blk, tiles, keys, at, _ = shape_of(u)
                        j = u % 4
                        act.wait_ge(turned[1], g * STEPS + u + 1)
                        act.wait_ge(max_ready, g * STEPS + u + 1)
                        nc.scalar.activation(probs[u % 2][:, 0:len(keys) * P], ps_s[u % 2][:, at:BANK + CTX], ACT.Exp,
                                             bias=neg_max[:, j:j + 1], scale=A_SCALE, accum_out=total[:, j:j + 1]).then_inc(exp_done, 1)
                        nc.scalar.activation(sink_exp[:, j:j + 1], sink[:, u % A_GROUP:u % A_GROUP + 1], ACT.Exp,
                                             bias=neg_max[:, j:j + 1]).then_inc(sink_exp_done, 1)

                    def read(u):
                        cut = shape_of(u)[4]
                        act.wait_ge(turned[0], g * STEPS + u + 3)
                        act.wait_ge(pv_full, g * STEPS + u + 1)
                        nc.scalar.activation(probsT[u % 2][:, 0:cut * P], ps_t[0][:, 0:cut * P], ACT.Copy).then_inc(turned_read[0], 1)

                    exps(0)
                    for u in range(STEPS):
                        if u + 1 < STEPS:
                            exps(u + 1)
                        read(u)

            @block.vector
            def _(dve):
                dve.sem_inc(out_done, 2)
                dve.sem_inc(turned_read[1], 1)
                with dve.Fori(0, A_KV) as g:
                    dve.wait_ge(sink_ready, 2 * g + 2)

                    def maxima(u):
                        _, _, _, at, _ = shape_of(u)
                        j = u % 4
                        dve.wait_ge(scored, g * STEPS + u + 1)
                        nc.vector.tensor_reduce(top[:, j:j + 1], ps_s[u % 2][:, at:BANK + CTX], AX, ALU.max).then_inc(top_ready, 1)
                        dve.wait_ge(top_ready, g * STEPS + u + 1)
                        nc.vector.tensor_scalar(neg_max[:, j:j + 1], top[:, j:j + 1], -A_SCALE,
                                                neg_sink[:, u % A_GROUP:u % A_GROUP + 1], ALU.mult, ALU.min).then_inc(max_ready, 1)

                    def read(u):
                        _, _, keys, _, cut = shape_of(u)
                        dve.wait_ge(turned[1], g * STEPS + u + 3)
                        dve.wait_ge(pv_full, g * STEPS + u + 1)
                        nc.vector.tensor_copy(probsT[u % 2][:, cut * P:len(keys) * P],
                                              ps_t[1][:, 0:(len(keys) - cut) * P]).then_inc(turned_read[1], 1)

                    def finish(u):
                        blk, h, j = u // A_GROUP, u % A_GROUP, u % 4
                        n = 2 * (g * STEPS + u)
                        dve.wait_ge(sink_exp_done, g * STEPS + u + 1)
                        nc.vector.tensor_tensor(denom[:, j:j + 1], total[:, j:j + 1], sink_exp[:, j:j + 1], ALU.add).then_inc(inv_step, 1)
                        dve.wait_ge(inv_step, n + 1)
                        nc.vector.reciprocal(inv[:, j:j + 1], denom[:, j:j + 1]).then_inc(inv_step, 1)
                        dve.wait_ge(inv_step, n + 2)
                        dve.wait_ge(pv_full, g * STEPS + u + 3)
                        if h == 0:
                            dve.wait_ge(stored[blk % 2], 16 * (g * (BLOCKS // 2) + blk // 2) + 16)
                        nc.vector.tensor_scalar(outs[blk % 2][:, h * A_HD:(h + 1) * A_HD], ps_o[u % 2][:, 0:A_HD],
                                                inv[:, j:j + 1], None, ALU.mult).then_inc(out_done, 1)

                    maxima(0)
                    for u in range(STEPS):
                        if u + 1 < STEPS:
                            maxima(u + 1)
                        read(u)
                        if u:
                            finish(u - 1)
                    finish(STEPS - 1)


def stage_latents(nc, io, dr, const, cqT, ckvT, kT):
    with Stage(nc, "lat") as st:
        w = st.sb("w", [P, KD, B_IN])
        x = [st.sb(f"x{b}", [P, D]) for b in range(2)]
        xT = [st.sb(f"xT{b}", [P, KD, P]) for b in range(2)]
        lat = [st.sb(f"lat{b}", [P, B_IN]) for b in range(2)]
        shift, scale, scale1 = (st.sb(n, [P, 2, KD]) for n in ("shift", "scale", "scale1"))
        q_gain, kv_gain = st.sb("q_gain", [P, B_QR // P]), st.sb("kv_gain", [P, B_KVR // P])
        squares = [st.sb(f"squares{n}", [P, BANK]) for n in range(2)]
        sums, mean, root, rstd = (st.sb(n, [P, 2, 2]) for n in ("sums", "mean", "root", "rstd"))
        kcos, ksin = st.sb("kcos", [P, B_ROPE]), st.sb("ksin", [P, B_ROPE])
        ps_x = [st.ps(f"x{b}", [P, 2 * BANK]) for b in range(2)]
        ps_c = st.ps("c", [P, 2 * BANK])
        ps_z = st.ps("z", [P, 2 * BANK])
        x_in = st.sems("x_in", 2)
        w_in, m_in, m_ready = st.sem("w_in"), st.sem("m_in"), st.sem("m_ready")
        turned, xT_a, xT_v, projected, squared, rooted, chain, c_read, c_scaled, lat_full, z_read_a, z_read_v = (
            st.sem(n) for n in ("turned", "xT_a", "xT_v", "projected", "squared", "rooted", "chain", "c_read", "c_scaled", "lat_full", "z_read_a", "z_read_v"))
        ident = const("ident")
        KQ, KV = B_QR // P, B_KVR // P
        ROPE_AT = B_QR + B_KVR
        CHAIN = 4

        def skewed(eng, first, second):
            first(0, 0, 0)
            first(0, 1, 0)
            second(0, 0, 0)
            with eng.Fori(1, NT_X // 2) as i:
                first(i, 0, 0)
                second(i - 1, 1, 0)
                first(i, 1, 0)
                second(i, 0, 0)
            first(NT_X // 2, 0, 1)
            second(NT_X // 2 - 1, 1, 0)
            first(NT_X // 2, 1, 1)
            second(NT_X // 2, 0, 1)
            second(NT_X // 2, 1, 1)

        with nc.Block() as block:

            @block.sync
            def _(sp):
                for s in range(2):
                    for tile, part in ((shift, 0), (scale, 1)):
                        sp.dma_start(tile[:, s, :], dr["mod"][1, s, part * D:(part + 1) * D].rearrange("(p k) -> p k", k=KD)).then_inc(m_in, 16)
                sp.dma_start(q_gain[:, :], io["mla_q_norm"][0].rearrange("(p k) -> p k", k=KQ)).then_inc(m_in, 16)
                sp.dma_start(kv_gain[:, :], io["mla_kv_norm"][0].rearrange("(p k) -> p k", k=KV)).then_inc(m_in, 16)

                def load(i, b):
                    sp.dma_start(x[b][:, :], dr["x"][bass.ds((i * 2 + b) * P, P), :]).then_inc(x_in[b], 16)

                for b in range(2):
                    load(0, b)
                sp.dma_start(w[:, :, :], io["mla_w_in"][0].rearrange("(p k) n -> p k n", k=KD)).then_inc(w_in, 16)
                with sp.Fori(1, NT_ALL // 2) as i:
                    for b in range(2):
                        sp.wait_ge(turned, 2 * i + b - 1)
                        load(i, b)

            @block.tensor
            def _(pe):
                def turn_and_project(i, b, s):
                    t = 2 * i + b
                    rows = x[b][:, :].rearrange("t (p k) -> t k p", k=KD)
                    pe.wait_ge(x_in[b], 16 * i + 16)
                    pe.wait_ge(xT_a, t + 1)
                    pe.wait_ge(xT_v, t + 1)
                    for k in range(KD):
                        last = nc.tensor.transpose(ps_x[b][:, k * P:(k + 1) * P], rows[:, k, :], ident)
                    last.then_inc(turned, 1)
                    pe.wait_ge(xT_a, t + 3)
                    pe.wait_ge(xT_v, t + 3)
                    pe.wait_ge(c_read, t + 1)
                    pe.wait_ge(c_scaled, t + 1)
                    cuts = ((0, B_QR), (B_QR, B_IN)) if s == 0 else ((B_QR, B_IN),)
                    for lo, hi in cuts:
                        for k in range(KD):
                            last = nc.tensor.matmul(ps_c[:, lo:hi], xT[b][:, k, :], w[:, k, lo:hi],
                                                    start=(k == 0), stop=(k == KD - 1))
                    last.then_inc(projected, 1)

                def turn_latents(i, b, s):
                    t = 2 * i + b
                    pe.wait_ge(c_read, t + 2)
                    pe.wait_ge(c_scaled, t + 2)
                    pe.wait_ge(z_read_a, t + 1)
                    pe.wait_ge(z_read_v, t + 1)
                    if s == 0:
                        cq = lat[b][:, 0:B_QR].rearrange("t (p k) -> t k p", k=KQ)
                        for k in range(KQ):
                            nc.tensor.transpose(ps_z[:, k * P:(k + 1) * P], cq[:, k, :], ident)
                    kv = lat[b][:, B_QR:ROPE_AT].rearrange("t (p k) -> t k p", k=KV)
                    for k in range(KV):
                        nc.tensor.transpose(ps_z[:, BANK + k * P:BANK + (k + 1) * P], kv[:, k, :], ident)
                    nc.tensor.transpose(ps_z[0:B_ROPE, BANK + KV * P:BANK + (KV + 1) * P], lat[b][:, ROPE_AT:B_IN],
                                        ident).then_inc(lat_full, 1)

                pe.sem_inc(projected, 2)
                pe.sem_inc(lat_full, 2)
                pe.wait_ge(w_in, 16)
                skewed(pe, turn_and_project, turn_latents)

            @block.scalar
            def _(act):
                act.sem_inc(xT_a, 2)
                act.sem_inc(c_scaled, 1)
                act.sem_inc(z_read_a, 1)
                act.wait_ge(m_ready, 1)

                def scale_latents(i, b, s):
                    t = 2 * i + b
                    act.wait_ge(turned, t + 1)
                    act.wait_ge(projected, t + 1)
                    for k in range(KD // 2):
                        last = nc.scalar.activation(xT[b][:, k, :], ps_x[b][:, k * P:(k + 1) * P], ACT.Identity,
                                                    bias=shift[:, s, k:k + 1], scale=scale1[:, s, k:k + 1])
                    last.then_inc(xT_a, 1)
                    act.wait_ge(projected, t + 3)
                    act.wait_ge(c_read, t + 1)
                    if s == 0:
                        nc.scalar.activation(squares[0][:, 0:B_QR], ps_c[:, 0:B_QR], ACT.Square, accum_out=sums[:, b, 0:1])
                    act.wait_ge(chain, CHAIN * t + 1)
                    nc.scalar.activation(squares[1][:, 0:B_KVR], ps_c[:, B_QR:ROPE_AT], ACT.Square,
                                         accum_out=sums[:, b, 1:2]).then_inc(squared, 1)
                    act.wait_ge(chain, CHAIN * t + 3)
                    nc.scalar.activation(root[:, b, s:2], mean[:, b, s:2], ACT.Sqrt).then_inc(rooted, 1)
                    act.wait_ge(chain, CHAIN * t + 4)
                    act.wait_ge(lat_full, t + 1)
                    nc.scalar.activation(lat[b][:, B_QR:ROPE_AT], ps_c[:, B_QR:ROPE_AT], ACT.Copy,
                                         scale=rstd[:, b, 1:2]).then_inc(c_scaled, 1)

                def gain(i, b, s):
                    t = 2 * i + b
                    act.wait_ge(lat_full, t + 3)
                    if s == 0:
                        for k in range(KQ):
                            last = nc.scalar.activation(cqT[:, k, bass.ds(t * P, P)], ps_z[:, k * P:(k + 1) * P], ACT.Copy,
                                                        scale=q_gain[:, k:k + 1])
                        last.then_inc(z_read_a, 1)
                    else:
                        act.sem_inc(z_read_a, 1)

                skewed(act, scale_latents, gain)

            @block.vector
            def _(dve):
                dve.sem_inc(xT_v, 2)
                dve.sem_inc(c_read, 1)
                dve.sem_inc(z_read_v, 1)
                dve.wait_ge(m_in, 96)
                nc.vector.tensor_scalar(scale1[:, :, :], scale[:, :, :], 1.0, None, ALU.add).then_inc(m_ready, 1)
                dve.wait_ge(m_ready, 1)

                def scale_latents(i, b, s):
                    t = 2 * i + b
                    dve.wait_ge(turned, t + 1)
                    dve.wait_ge(projected, t + 1)
                    for k in range(KD // 2, KD):
                        last = nc.vector.tensor_scalar(xT[b][:, k, :], ps_x[b][:, k * P:(k + 1) * P],
                                                       scale1[:, s, k:k + 1], shift[:, s, k:k + 1], ALU.mult, ALU.add)
                    last.then_inc(xT_v, 1)
                    own = Chain(dve, chain, CHAIN * t)
                    rope = ps_c[:, ROPE_AT:B_IN]
                    dve.wait_ge(projected, t + 3)
                    dve.wait_ge(lat_full, t + 1)
                    if s == 0:
                        halves = lambda ap: ap.rearrange("p (a h j) -> p a h j", a=2, h=2)
                        tk = bass.ds(t * B_ROPE, B_ROPE)
                        r, sn, o = halves(rope), halves(const("sin_k")[:, tk]), halves(ksin[:, :])
                        nc.vector.tensor_tensor(o[:, :, 0, :], r[:, :, 1, :], sn[:, :, 0, :], ALU.mult)
                        nc.vector.tensor_tensor(o[:, :, 1, :], r[:, :, 0, :], sn[:, :, 1, :], ALU.mult)
                        own.link(nc.vector.tensor_tensor(kcos[:, :], rope, const("cos_k")[:, tk], ALU.mult))
                        own.link(nc.vector.tensor_tensor(lat[b][:, ROPE_AT:B_IN], kcos[:, :], ksin[:, :], ALU.add))
                    else:
                        own.link(nc.vector.tensor_copy(lat[b][:, ROPE_AT:B_IN], rope))
                        dve.sem_inc(chain, 1)
                        own.n += 1
                    dve.wait_ge(squared, t + 1)
                    if s == 0:
                        nc.vector.tensor_scalar(mean[:, b, 0:1], sums[:, b, 0:1], 1.0 / B_QR, RMS_EPS, ALU.mult, ALU.add)
                    own.link(nc.vector.tensor_scalar(mean[:, b, 1:2], sums[:, b, 1:2], 1.0 / B_KVR, RMS_EPS, ALU.mult, ALU.add))
                    lo = 0 if s == 0 else 1
                    dve.wait_ge(rooted, t + 1)
                    own.link(nc.vector.reciprocal(rstd[:, b, lo:2], root[:, b, lo:2]))
                    if s == 0:
                        nc.vector.tensor_scalar(lat[b][:, 0:B_QR], ps_c[:, 0:B_QR], rstd[:, b, 0:1], None, ALU.mult).then_inc(c_read, 1)
                    else:
                        dve.sem_inc(c_read, 1)
                    assert own.n == CHAIN

                def gain(i, b, s):
                    t = 2 * i + b
                    dve.wait_ge(lat_full, t + 3)
                    for k in range(KV):
                        nc.vector.tensor_scalar(ckvT[:, k, bass.ds(t * P, P)], ps_z[:, BANK + k * P:BANK + (k + 1) * P],
                                                kv_gain[:, k:k + 1], None, ALU.mult)
                    for copy in kT:
                        last = nc.vector.tensor_copy(copy[B_NOPE:B_QD, bass.ds(t * P, P)],
                                                     ps_z[0:B_ROPE, BANK + KV * P:BANK + (KV + 1) * P])
                    last.then_inc(z_read_v, 1)

                skewed(dve, scale_latents, gain)


def stage_latent_attention(nc, io, dr, const, cqT, ckvT, kT):
    UN, CH = 8, NT_ALL
    KQ, KV = B_QR // P, B_KVR // P
    VW = B_V + 1
    F32R = mybir.dt.float32r
    with Stage(nc, "mla") as st:
        wq, wk = st.sb("wq", [P, KQ, B_QD]), st.sb("wk", [P, KV, B_NOPE])
        wv = st.sb("wv", [P, KV, BANK])
        v_all = st.sb("v_all", [P, NT_ALL, B_HEADS, VW])
        o_all = st.sb("o_all", [P, NT_X, B_HEADS * B_V])
        q_raw, q_cos, q_sin = (st.sb(n, [B_QD, SEQ]) for n in ("q_raw", "q_cos", "q_sin"))
        qT = [st.sb(f"qT{b}", [B_QD + 1, SEQ]) for b in range(2)]
        q_round, k_round = st.sb("q_round", [B_QD, SEQ], F32R), st.sb("k_round", [B_QD, TALL], F32R)
        probs = [st.sb(f"probs{b}", [P, CH, BANK]) for b in range(2)]
        top, inv = st.sb("top", [P, UN]), st.sb("inv", [P, 4])
        ps_a = st.ps("a", [P, 3 * BANK])
        ps_b = [st.ps(f"b{n}", [P, BANK]) for n in range(2)]
        ps_o, ps_m = st.ps("o", [P, BANK]), st.ps("m", [P, BANK])
        w_in, wv_in, ones_ready, v_full, v_read = (st.sem(n) for n in ("w_in", "wv_in", "ones_ready", "v_full", "v_read"))
        q_full, k_full, rot_full, q_copied, k_copied, sin_ready, cos_ready, q_ready, rounded = (
            st.sem(n) for n in ("q_full", "k_full", "rot_full", "q_copied", "k_copied", "sin_ready", "cos_ready", "q_ready", "rounded"))
        scored, max_ready, row_full, row_ready, key_scored, exp_done, pv_full, inv_ready, out_done, stored = (
            st.sem(n) for n in ("scored", "max_ready", "row_full", "row_ready", "key_scored", "exp_done", "pv_full", "inv_ready", "out_done", "stored"))
        ident = const("ident")
        cos, sin, rot = const("cos_b")[0:B_QD, :], const("sin_b")[0:B_QD, :], const("rot_b")[0:B_QD, :]
        ukv = io["mla_w_ukv"][0].rearrange("(p k) (h e) -> p k h e", k=KV, e=B_NOPE + B_V)
        ukv_flat = io["mla_w_ukv"][0].rearrange("(p k) n -> p k n", k=KV)
        uq = io["mla_w_uq"][0].rearrange("(p k) n -> p k n", k=KQ)
        HV = BANK // B_V
        a_bank = lambda n: ps_a[:, n * BANK:(n + 1) * BANK]

        def heads(eng, head):
            with eng.Fori(0, B_HEADS // 2 - 1) as i:
                for b in range(2):
                    head(2 * i + b, b, False)
            for b in range(2):
                head(B_HEADS - 2 + b, b, b == 1)

        first = lambda h: isinstance(h, int) and h == 0

        with nc.Block() as block:

            @block.sync
            def _(sp):
                def load(h):
                    sp.dma_start(wq[:, :, :], uq[:, :, bass.ds(h * B_QD, B_QD)]).then_inc(w_in, 16)
                    sp.dma_start(wk[:, :, :], ukv_flat[:, :, bass.ds(h * (B_NOPE + B_V), B_NOPE)]).then_inc(w_in, 16)

                load(0)
                for n in range(2):
                    if n:
                        sp.wait_ge(v_full, NT_ALL)
                    for k in range(KV):
                        sp.dma_start(wv[:, k, :].rearrange("p (h e) -> p h e", e=B_V),
                                     ukv[:, k, n * HV:(n + 1) * HV, B_NOPE:]).then_inc(wv_in, 16)
                with sp.Fori(1, B_HEADS) as h:
                    sp.wait_ge(k_full, 3 * h)
                    load(h)
                sp.wait_ge(out_done, 2 * B_HEADS)
                for t in range(NT_X):
                    sp.dma_start(dr["o"][t * P:(t + 1) * P, :], o_all[:, t, :]).then_inc(stored, 16)
                sp.wait_ge(stored, 16 * NT_X)

            @block.gpsimd
            def _(pool):
                nc.gpsimd.memset(v_all[:, :, :, B_V:VW].rearrange("p t h e -> p (t h e)"), 1.0).then_inc(ones_ready, 1)
                for b in range(2):
                    pool.wait_ge(ones_ready, b + 1)
                    nc.gpsimd.memset(kT[b][B_QD:B_QD + 1, :], 1.0).then_inc(ones_ready, 1)
                pool.wait_ge(ones_ready, 3)

                def times_cos(h):
                    pool.wait_ge(q_copied, 2 * h + 2)
                    if not first(h):
                        pool.wait_ge(q_ready, h)
                    nc.gpsimd.tensor_tensor(q_cos[:, :], q_raw[:, :], cos, ALU.mult).then_inc(cos_ready, 1)

                def round_k(h, b):
                    pool.wait_ge(k_copied, 3 * h + 3)
                    if not first(h):
                        pool.wait_ge(scored, UN * h)
                    st.settle(pool)
                    nc.gpsimd.tensor_copy(k_round[:, :], kT[b][0:B_QD, :]).then_inc(rounded, 1)

                def round_q(h, b):
                    pool.wait_ge(q_ready, h + 1)
                    st.settle(pool)
                    nc.gpsimd.tensor_copy(q_round[:, :], qT[b][0:B_QD, :]).then_inc(rounded, 1)

                def prepare(h, b):
                    times_cos(h)
                    round_k(h, b)
                    round_q(h, b)

                prepare(0, 0)
                heads(pool, lambda h, b, last: None if last else prepare(h + 1, 1 - b))

            @block.tensor
            def _(pe):
                pe.wait_ge(ones_ready, 3)
                for n in range(2):
                    pe.wait_ge(wv_in, 32 * (n + 1))
                    for t in range(NT_ALL):
                        u = n * NT_ALL + t
                        if u >= 3:
                            pe.wait_ge(v_read, u - 2)
                        for k in range(KV):
                            last = nc.tensor.matmul(a_bank(u % 3), ckvT[:, k, t * P:(t + 1) * P], wv[:, k, :],
                                                    start=(k == 0), stop=(k == KV - 1))
                        last.then_inc(v_full, 1)
                pe.wait_ge(v_read, 2 * NT_ALL)

                def project(h):
                    if not first(h):
                        pe.wait_ge(max_ready, UN * h)
                    pe.wait_ge(w_in, 32 * h + 32)
                    for n in range(2):
                        for k in range(KQ):
                            last = nc.tensor.matmul(a_bank(n)[0:B_QD, :], wq[:, k, :], cqT[:, k, n * BANK:(n + 1) * BANK],
                                                    start=(k == 0), stop=(k == KQ - 1))
                        last.then_inc(q_full, 1)
                    for n, (at, size) in enumerate(N_CUTS):
                        if n:
                            pe.wait_ge(q_copied, 2 * h + n)
                        for k in range(KV):
                            last = nc.tensor.matmul(a_bank((2 + n) % 3)[0:B_NOPE, 0:size], wk[:, k, :], ckvT[:, k, at:at + size],
                                                    start=(k == 0), stop=(k == KV - 1))
                        last.then_inc(k_full, 1)
                    for n in range(2):
                        pe.wait_ge(q_copied, 2 * h + n + 1)
                        pe.wait_ge(k_copied, 3 * h + n + 1)
                        nc.tensor.matmul(a_bank((2 + n) % 3)[0:B_QD, :], rot, q_raw[:, n * BANK:(n + 1) * BANK],
                                         start=True, stop=True).then_inc(rot_full, 1)

                def unit(h, u):
                    if u == 0:
                        pe.wait_ge(rounded, 2 * h + 2)
                        pe.wait_ge(k_copied, 3 * h + 3)
                        pe.wait_ge(sin_ready, 2 * h + 2)
                    else:
                        pe.wait_ge(max_ready, UN * h + u)
                    for at, size in N_CUTS:
                        last = nc.tensor.matmul(ps_a[:, at:at + size], q_round[:, u * P:(u + 1) * P], k_round[:, at:at + size],
                                                start=True, stop=True)
                    last.then_inc(scored, 1)

                def row(h, u):
                    pe.wait_ge(max_ready, UN * h + u + 1)
                    if u % 4 == 0 and not (first(h) and u == 0):
                        pe.wait_ge(row_ready, 2 * h + u // 4)
                    last = nc.tensor.transpose(ps_m[0:1, (u % 4) * P:(u % 4 + 1) * P], top[:, u:u + 1], ident)
                    if u % 4 == 3:
                        last.then_inc(row_full, 1)

                def chunk(h, b, half, c):
                    n = 2 * CH * h + CH * half + c
                    if c == 0:
                        pe.wait_ge(row_ready, 2 * h + half + 1)
                    if not (first(h) and half == 0 and c < 2):
                        pe.wait_ge(exp_done, n - 1)
                    nc.tensor.matmul(ps_b[c % 2][:, :], kT[b][:, c * P:(c + 1) * P], qT[b][:, half * BANK:(half + 1) * BANK],
                                     start=True, stop=True).then_inc(key_scored, 1)

                def mix(h, half, s):
                    if s == 0:
                        pe.wait_ge(exp_done, CH * (2 * h + half + 1))
                        if not (first(h) and half == 0):
                            pe.wait_ge(out_done, 2 * h + half)
                    for c in range(CH):
                        last = nc.tensor.matmul(ps_o[:, s * VW:(s + 1) * VW], probs[half][:, c, s * P:(s + 1) * P],
                                                v_all[:, c, bass.ds(h, 1), :].rearrange("p h e -> p (h e)"),
                                                start=(c == 0), stop=(c == CH - 1))
                    if s == 3:
                        last.then_inc(pv_full, 1)

                def head(h, b, last):
                    before = None if first(h) else (h - 1, 1)
                    between = {0: [(unit, h, 4)], 1: [(mix, 0)], 2: [(unit, h, 5), (row, h, 4)], 3: [(mix, 1)],
                               4: [(unit, h, 6), (row, h, 5)], 5: [(mix, 2)], 6: [(unit, h, 7), (row, h, 6)], 7: [(mix, 3)],
                               8: [(row, h, 7)]}
                    for c in range(CH):
                        chunk(h, b, 0, c)
                        for what, *where in between.get(c, ()):
                            if what is not mix:
                                what(*where)
                            elif before:
                                mix(*before, *where)
                    if not last:
                        project(h + 1)
                    nxt = h + 1
                    between = {0: [(mix, 0)], 1: [(mix, 1)], 2: [(unit, nxt, 0)], 3: [(unit, nxt, 1)],
                               4: [(unit, nxt, 2), (row, nxt, 0)], 5: [(unit, nxt, 3), (row, nxt, 1)], 6: [(row, nxt, 2)],
                               7: [(row, nxt, 3)], 8: [(mix, 2)], 9: [(mix, 3)]}
                    for c in range(CH):
                        chunk(h, b, 1, c)
                        for what, *where in between.get(c, ()):
                            if what is mix:
                                mix(h, 0, *where)
                            elif not last:
                                what(*where)

                project(0)
                for u in range(4):
                    unit(0, u)
                    row(0, u)
                for b in range(2):
                    head(b, b, False)
                with pe.Fori(1, B_HEADS // 2 - 1) as i:
                    for b in range(2):
                        head(2 * i + b, b, False)
                for b in range(2):
                    head(B_HEADS - 2 + b, b, b == 1)
                for s in range(4):
                    mix(B_HEADS - 1, 1, s)

            @block.scalar
            def _(act):
                for n in range(2):
                    for t in range(NT_ALL):
                        u = n * NT_ALL + t
                        act.wait_ge(v_full, u + 1)
                        nc.scalar.activation(v_all[:, t, n * HV:(n + 1) * HV, 0:B_V], a_bank(u % 3).rearrange("p (h e) -> p h e", e=B_V),
                                             ACT.Copy).then_inc(v_read, 1)

                def copies(h, b):
                    if not first(h):
                        act.wait_ge(q_ready, h)
                    for n in range(2):
                        act.wait_ge(q_full, 2 * h + n + 1)
                        nc.scalar.activation(q_raw[:, n * BANK:(n + 1) * BANK], a_bank(n)[0:B_QD, :], ACT.Copy).then_inc(q_copied, 1)
                    for n, (at, size) in enumerate(N_CUTS):
                        act.wait_ge(k_full, 3 * h + n + 1)
                        nc.scalar.activation(kT[b][0:B_NOPE, at:at + size], a_bank((2 + n) % 3)[0:B_NOPE, 0:size],
                                             ACT.Copy).then_inc(k_copied, 1)

                def exps(h, half):
                    for c in range(CH):
                        act.wait_ge(key_scored, CH * (2 * h + half) + c + 1)
                        nc.scalar.activation(probs[half][:, c, :], ps_b[c % 2][:, :], ACT.Exp, scale=B_SCALE).then_inc(exp_done, 1)

                def head(h, b, last):
                    exps(h, 0)
                    if not last:
                        copies(h + 1, 1 - b)
                    exps(h, 1)

                copies(0, 0)
                heads(act, head)

            @block.vector
            def _(dve):
                def rotate(h, b):
                    for n in range(2):
                        dve.wait_ge(rot_full, 2 * h + n + 1)
                        nc.vector.tensor_tensor(q_sin[:, n * BANK:(n + 1) * BANK], a_bank((2 + n) % 3)[0:B_QD, :],
                                                sin[:, n * BANK:(n + 1) * BANK], ALU.mult).then_inc(sin_ready, 1)
                    dve.wait_ge(sin_ready, 2 * h + 2)
                    dve.wait_ge(cos_ready, h + 1)
                    nc.vector.tensor_tensor(qT[b][0:B_QD, :], q_cos[:, :], q_sin[:, :], ALU.add).then_inc(q_ready, 1)

                def maximum(h, u):
                    dve.wait_ge(scored, UN * h + u + 1)
                    nc.vector.tensor_reduce(top[:, u:u + 1], ps_a[:, 0:TALL], AX, ALU.max).then_inc(max_ready, 1)

                def row(h, b, half):
                    dve.wait_ge(row_full, 2 * h + half + 1)
                    nc.vector.tensor_scalar(qT[b][B_QD:B_QD + 1, half * BANK:(half + 1) * BANK], ps_m[0:1, :], -1.0, None,
                                            ALU.mult).then_inc(row_ready, 1)

                def finish(h, half):
                    n = 2 * h + half
                    sums = ps_o[:, 0:4 * VW].rearrange("p (s e) -> p s e", e=VW)
                    dve.wait_ge(pv_full, n + 1)
                    nc.vector.reciprocal(inv[:, :], sums[:, :, B_V]).then_inc(inv_ready, 1)
                    dve.wait_ge(inv_ready, n + 1)
                    nc.vector.tensor_tensor(o_all[:, half * 4:half * 4 + 4, bass.ds(h * B_V, B_V)], sums[:, :, 0:B_V],
                                            bcast_last(inv[:, :], B_V), ALU.mult).then_inc(out_done, 1)

                def head(h, b, last):
                    for u in range(4, 8):
                        maximum(h, u)
                    if not first(h):
                        finish(h - 1, 1)
                    row(h, b, 1)
                    if not last:
                        rotate(h + 1, 1 - b)
                        for u in range(4):
                            maximum(h + 1, u)
                        row(h + 1, 1 - b, 0)
                    finish(h, 0)

                rotate(0, 0)
                for u in range(4):
                    maximum(0, u)
                row(0, 0, 0)
                for b in range(2):
                    head(b, b, False)
                with dve.Fori(1, B_HEADS // 2 - 1) as i:
                    for b in range(2):
                        head(2 * i + b, b, False)
                for b in range(2):
                    head(B_HEADS - 2 + b, b, b == 1)
                finish(B_HEADS - 1, 1)


def load_rows(sp, sem, pairs):
    for tile, row in pairs:
        sp.dma_start(tile, row.partition_broadcast(P)).then_inc(sem, 16)
    return 16 * len(pairs)


def stage_project_out(nc, io, dr, const, layer, w_out, tiles, logits):
    with Stage(nc, f"out{layer}") as st:
        w, wr = st.sb("w", [P, KD, D]), st.sb("wr", [P, KD, ROUTE])
        r_bias = st.sb("r_bias", [P, ROUTE])
        kinds = 2 if tiles > NT_X else 1
        gate, scale, shift = ([st.sb(f"{n}{s}", [P, D]) for s in range(kinds)] for n in ("gate", "scale", "shift"))
        ln_g, ln_b = st.sb("ln_g", [P, D]), st.sb("ln_b", [P, D])
        o, x = ([st.sb(f"{n}{b}", [P, D]) for b in range(2)] for n in ("o", "x"))
        oT, hT = st.sb("oT", [P, KD, P]), st.sb("hT", [P, KD, P])
        gated, res, xn, xg, hs = (st.sb(n, [P, D]) for n in ("gated", "res", "xn", "xg", "hs"))
        xo, h = ([st.sb(f"{n}{b}", [P, D]) for b in range(2)] for n in ("xo", "h"))
        stats, mv, var, rstd, bias = st.sb("stats", [P, 2, 6]), st.sb("mv", [P, 2]), st.sb("var", [P, 1]), st.sb("rstd", [P, 1]), st.sb("bias", [P, 1])
        root = st.sb("root", [P, 1])
        ps_o, ps_y, ps_h = (st.ps(n, [P, 2 * BANK]) for n in ("o", "y", "h"))
        ps_r = st.ps("r", [P, BANK])
        o_in, x_in, x_stored, h_stored = (st.sems(n, 2) for n in ("o_in", "x_in", "x_stored", "h_stored"))
        w_in, rows_in, scale_ready, o_turned, o_read, y_full, h_turned, h_read, routed = (
            st.sem(n) for n in ("w_in", "rows_in", "scale_ready", "o_turned", "o_read", "y_full", "h_turned", "h_read", "routed"))
        chain, rooted, normed, x_ready, hs_ready, h_ready, logit_done = (
            st.sem(n) for n in ("chain", "rooted", "normed", "x_ready", "hs_ready", "h_ready", "logit_done"))
        ident = const("ident")
        STEPS = 9
        mod = lambda s, part: dr["mod"][layer, s, part * D:(part + 1) * D]

        def each(eng, first, second=None):
            pairs = NT_X // 2
            seq = lambda i, b, s: first(i, b, s)
            sec = second or (lambda i, b, s: None)
            seq(0, 0, 0)
            seq(0, 1, 0)
            sec(0, 0, 0)
            with eng.Fori(1, pairs) as i:
                seq(i, 0, 0)
                sec(i - 1, 1, 0)
                seq(i, 1, 0)
                sec(i, 0, 0)
            if kinds == 2:
                seq(pairs, 0, 1)
                sec(pairs - 1, 1, 0)
                seq(pairs, 1, 1)
                sec(pairs, 0, 1)
                sec(pairs, 1, 1)
            else:
                sec(pairs - 1, 1, 0)

        with nc.Block() as block:

            @block.sync
            def _(sp):
                def load(i, b):
                    t = bass.ds((i * 2 + b) * P, P)
                    sp.dma_start(o[b][:, :], dr["o"][t, :]).then_inc(o_in[b], 16)
                    sp.dma_start(x[b][:, :], dr["x"][t, :]).then_inc(x_in[b], 16)

                def store(i, b):
                    t = bass.ds((i * 2 + b) * P, P)
                    sp.wait_ge(x_ready, 2 * i + b + 1)
                    sp.dma_start(dr["x"][t, :], xo[b][:, :]).then_inc(x_stored[b], 16)
                    sp.wait_ge(h_ready, 2 * i + b + 1)
                    sp.dma_start(dr["h"][t, :], h[b][:, :]).then_inc(h_stored[b], 16)

                for b in range(2):
                    sp.sem_inc(x_stored[b], 16)
                    sp.sem_inc(h_stored[b], 16)
                    load(0, b)
                sp.dma_start(w[:, :, :], w_out.rearrange("(p k) n -> p k n", k=KD)).then_inc(w_in, 16)
                pairs = [(ln_g[:, :], io["ln_mix_g"][layer]), (ln_b[:, :], io["ln_mix_b"][layer]),
                         (r_bias[:, 0:NG], io["moe_b_grp"][layer]), (r_bias[:, NG:], io["moe_b_rt"][layer])]
                for s in range(kinds):
                    pairs += [(gate[s][:, :], mod(s, 2)), (shift[s][:, :], mod(s, 3)), (scale[s][:, :], mod(s, 4))]
                load_rows(sp, rows_in, pairs)
                sp.dma_start(wr[:, :, 0:NG], io["moe_w_grp"][layer].rearrange("(p k) n -> p k n", k=KD)).then_inc(rows_in, 16)
                sp.dma_start(wr[:, :, NG:], io["moe_w_rt"][layer].rearrange("(p k) n -> p k n", k=KD)).then_inc(rows_in, 16)
                with sp.Fori(1, tiles // 2) as i:
                    for b in range(2):
                        sp.wait_ge(chain, STEPS * (2 * i + b - 2) + 2)
                        load(i, b)
                        store(i - 1, b)
                for b in range(2):
                    store(tiles // 2 - 1, b)
                for b in range(2):
                    sp.wait_ge(x_stored[b], 16 * (tiles // 2) + 16)
                    sp.wait_ge(h_stored[b], 16 * (tiles // 2) + 16)

            ROWS_IN = 16 * (4 + 3 * kinds + 2)

            @block.tensor
            def _(pe):
                pe.sem_inc(y_full, 1)
                pe.sem_inc(routed, 1)
                pe.wait_ge(rows_in, ROWS_IN)
                pe.wait_ge(w_in, 16)

                def project(i, b, s):
                    t = 2 * i + b
                    pe.wait_ge(o_in[b], 16 * i + 16)
                    pe.wait_ge(o_read, t + 1)
                    rows = o[b][:, :].rearrange("t (p k) -> t k p", k=KD)
                    for k in range(KD):
                        last = nc.tensor.transpose(ps_o[:, k * P:(k + 1) * P], rows[:, k, :], ident)
                    last.then_inc(o_turned, 1)
                    pe.wait_ge(o_read, t + 2)
                    if not (isinstance(i, int) and t == 0):
                        pe.wait_ge(chain, STEPS * t - (STEPS - 1))
                    for n in range(2):
                        for k in range(KD):
                            last = nc.tensor.matmul(ps_y[:, n * BANK:(n + 1) * BANK], oT[:, k, :], w[:, k, n * BANK:(n + 1) * BANK],
                                                    start=(k == 0), stop=(k == KD - 1))
                    last.then_inc(y_full, 1)

                def route(i, b, s):
                    t = 2 * i + b
                    pe.wait_ge(h_ready, t + 1)
                    pe.wait_ge(h_read, t + 1)
                    rows = h[b][:, :].rearrange("t (p k) -> t k p", k=KD)
                    for k in range(KD):
                        last = nc.tensor.transpose(ps_h[:, k * P:(k + 1) * P], rows[:, k, :], ident)
                    last.then_inc(h_turned, 1)
                    pe.wait_ge(h_read, t + 2)
                    pe.wait_ge(logit_done, t + 1)
                    for k in range(KD):
                        last = nc.tensor.matmul(ps_r[:, 0:ROUTE], hT[:, k, :], wr[:, k, :], start=(k == 0), stop=(k == KD - 1))
                    last.then_inc(routed, 1)

                each(pe, project, route)

            @block.scalar
            def _(act):
                act.sem_inc(o_read, 1)
                act.sem_inc(h_read, 1)

                def first(i, b, s):
                    t = 2 * i + b
                    act.wait_ge(o_turned, t + 1)
                    act.wait_ge(y_full, t + 1)
                    nc.scalar.activation(oT[:, :, :].rearrange("p k t -> p (k t)"), ps_o[:, :], ACT.Copy).then_inc(o_read, 1)

                def norm(i, b, s):
                    t = 2 * i + b
                    act.wait_ge(chain, STEPS * t + 6)
                    nc.scalar.activation(root[:, :], var[:, :], ACT.Sqrt).then_inc(rooted, 1)
                    act.wait_ge(chain, STEPS * t + 8)
                    nc.scalar.activation(xn[:, :], res[:, :], ACT.Identity, bias=bias[:, :], scale=rstd[:, :]).then_inc(normed, 1)
                    act.wait_ge(h_turned, t + 1)
                    act.wait_ge(routed, t + 1)
                    nc.scalar.activation(hT[:, :, :].rearrange("p k t -> p (k t)"), ps_h[:, :], ACT.Copy).then_inc(h_read, 1)

                each(act, first, norm)

            @block.vector
            def _(dve):
                dve.sem_inc(logit_done, 1)
                dve.wait_ge(rows_in, ROWS_IN)
                for s in range(kinds):
                    last = nc.vector.tensor_scalar(scale[s][:, :], scale[s][:, :], 1.0, None, ALU.add)
                last.then_inc(scale_ready, 1)
                dve.wait_ge(scale_ready, 1)

                def update(i, b, s):
                    t = 2 * i + b
                    own = Chain(dve, chain, STEPS * t)
                    dve.wait_ge(y_full, t + 2)
                    own.link(nc.vector.tensor_tensor(gated[:, :], ps_y[:, :], gate[s][:, :], ALU.mult))
                    dve.wait_ge(x_in[b], 16 * i + 16)
                    own.link(nc.vector.scalar_tensor_tensor(res[:, :], x[b][:, :], ALPHA, gated[:, :], ALU.mult, ALU.add))
                    for n in range(2):
                        own.inc(nc.vector.bn_stats(stats[:, n, :], res[:, n * BANK:(n + 1) * BANK]))
                    own.wait()
                    st.settle(dve)
                    own.link(nc.vector.bn_aggr(mv[:, :], stats[:, :, :].rearrange("p n s -> p (n s)")))
                    own.link(nc.vector.tensor_scalar(var[:, :], mv[:, 1:2], LN_EPS, None, ALU.add))
                    dve.wait_ge(rooted, t + 1)
                    own.link(nc.vector.reciprocal(rstd[:, :], root[:, :]))
                    own.link(nc.vector.tensor_scalar(bias[:, :], mv[:, 0:1], rstd[:, :], -1.0, ALU.mult, ALU.mult))
                    dve.wait_ge(normed, t + 1)
                    own.link(nc.vector.tensor_tensor(xg[:, :], xn[:, :], ln_g[:, :], ALU.mult))
                    dve.wait_ge(hs_ready, t + 1)
                    dve.wait_ge(h_stored[b], 16 * i + 16)
                    assert own.n == STEPS
                    nc.vector.tensor_tensor(h[b][:, :], hs[:, :], shift[s][:, :], ALU.add).then_inc(h_ready, 1)

                def logit(i, b, s):
                    t = 2 * i + b
                    dve.wait_ge(routed, t + 2)
                    nc.vector.tensor_tensor(logits[:, bass.ds(t * ROUTE, ROUTE)], ps_r[:, 0:ROUTE], r_bias[:, :], ALU.add).then_inc(logit_done, 1)

                each(dve, update, logit)

            @block.gpsimd
            def _(pool):
                pool.wait_ge(rows_in, ROWS_IN)
                pool.wait_ge(scale_ready, 1)

                def shift_norm(i, b, s):
                    t = 2 * i + b
                    pool.wait_ge(chain, STEPS * t + 9)
                    pool.wait_ge(x_stored[b], 16 * i + 16)
                    nc.gpsimd.tensor_tensor(xo[b][:, :], xg[:, :], ln_b[:, :], ALU.add).then_inc(x_ready, 1)
                    pool.wait_ge(x_ready, t + 1)
                    nc.gpsimd.tensor_tensor(hs[:, :], xo[b][:, :], scale[s][:, :], ALU.mult).then_inc(hs_ready, 1)

                each(pool, shift_norm)


def stage_route(nc, dr, const, layer, tiles, logits, weights, slots, block_info, tokens):
    nb = n_blocks(tiles)
    with Stage(nc, f"rt{layer}") as st:
        lg = logits[:, 0:tiles * ROUTE].rearrange("p (t r) -> p t r", r=ROUTE)
        l_grp, l_exp = lg[:, :, 0:NG], lg[:, :, NG:]
        t1 = lambda name, dt=F32: st.sb(name, [P, tiles], dt)
        tg = lambda name: st.sb(name, [P, tiles, NG])
        te = lambda name: st.sb(name, [P, tiles, NE])
        g_max, g_low, g_sum, g_prob = t1("g_max"), t1("g_low"), t1("g_sum"), t1("g_prob")
        g_diff, g_exp, g_hit, g_idx, g_one = tg("g_diff"), tg("g_exp"), tg("g_hit"), tg("g_idx"), tg("g_one")
        e_in, e_hit, e_idx, e_rest = te("e_in"), te("e_hit"), te("e_idx"), te("e_rest")
        e_max, e_low = [t1(f"e_max{k}") for k in range(2)], [t1(f"e_low{k}") for k in range(2)]
        one = [te(f"one{k}") for k in range(2)]
        both, seen = te("both"), st.sb("seen", [P, tiles + 1, NE])
        diff, ratio, denom, w_first = t1("diff"), t1("ratio"), t1("denom"), t1("w_first")
        counts, blocks, ends, starts = (st.sb(n, [P, NE]) for n in ("counts", "blocks", "ends", "starts"))
        over = st.sb("over", [P, NE, tiles])
        ranks, product = te("ranks"), te("product")
        rank, base, above, local, place, block_of = (t1(n) for n in ("rank", "base", "above", "local", "place", "block_of"))
        steps_over = st.sb("steps_over", [P, tiles, tiles])
        where = t1("where")
        table_at = [t1(f"table_at{k}", I32) for k in range(2)]
        passed, owner = st.sb("passed", [P, nb, NE]), st.sb("owner", [P, nb])
        token_id = t1("token_id", I32)
        zeros = st.sb("zeros", [P, nb], I32)
        ps = st.ps("ps", [P, BANK])
        ps_n = st.ps("ps_n", [P, BANK])
        own_sem, exp_ready, exped, both_ready, ranked, routed, zeroed = (
            st.sem(n) for n in ("own", "exp_ready", "exped", "both_ready", "ranked", "routed", "zeroed"))
        zero_in, scattered, read_back = (st.pool_dma_sem(n) for n in ("zero_in", "scattered", "read_back"))
        v = nc.vector
        with nc.Block() as block:

            @block.vector
            def _(dve):
                own = Chain(dve, own_sem)
                link = own.link
                iota_g, iota_e = bcast_mid(const("iota_g"), tiles), bcast_mid(const("iota_e"), tiles)
                link(v.tensor_reduce(g_max[:, :], l_grp, AX, ALU.max))
                v.tensor_tensor(g_diff[:, :, :], l_grp, bcast_last(g_max[:, :], NG), ALU.subtract).then_inc(exp_ready, 1)
                link(v.tensor_tensor(g_hit[:, :, :], l_grp, bcast_last(g_max[:, :], NG), ALU.is_equal))
                link(v.tensor_tensor(g_idx[:, :, :], g_hit[:, :, :], iota_g, ALU.mult))
                link(v.tensor_reduce(g_low[:, :], g_idx[:, :, :], AX, ALU.min))
                link(v.tensor_tensor(g_one[:, :, :], iota_g, bcast_last(g_low[:, :], NG), ALU.is_equal))
                link(v.tensor_scalar(g_idx[:, :, :], g_one[:, :, :], 1.0, BIG, ALU.subtract, ALU.mult))
                for g in range(NG):
                    own.inc(v.tensor_tensor(e_in[:, :, g * EPG:(g + 1) * EPG], l_exp[:, :, g * EPG:(g + 1) * EPG],
                                            g_idx[:, :, g:g + 1].broadcast_to([P, tiles, EPG]), ALU.add))
                own.wait()
                src = e_in
                for k in range(2):
                    link(v.tensor_reduce(e_max[k][:, :], src[:, :, :], AX, ALU.max))
                    link(v.tensor_tensor(e_hit[:, :, :], src[:, :, :], bcast_last(e_max[k][:, :], NE), ALU.is_equal))
                    link(v.tensor_tensor(e_idx[:, :, :], e_hit[:, :, :], iota_e, ALU.mult))
                    link(v.tensor_reduce(e_low[k][:, :], e_idx[:, :, :], AX, ALU.min))
                    link(v.tensor_tensor(one[k][:, :, :], iota_e, bcast_last(e_low[k][:, :], NE), ALU.is_equal))
                    if k == 0:
                        link(v.scalar_tensor_tensor(e_rest[:, :, :], one[0][:, :, :], -BIG, e_in[:, :, :], ALU.mult, ALU.add))
                        src = e_rest
                link(v.tensor_tensor(both[:, :, :], one[0][:, :, :], one[1][:, :, :], ALU.add))
                link(v.memset(seen[:, 0, :], 0.0))
                for t in range(tiles):
                    link(v.tensor_tensor(seen[:, t + 1, :], seen[:, t, :], both[:, t, :], ALU.add))
                dve.sem_inc(both_ready, 1)
                v.tensor_tensor(diff[:, :], e_max[1][:, :], e_max[0][:, :], ALU.subtract).then_inc(exp_ready, 1)
                dve.wait_ge(exped, 1)
                link(v.tensor_reduce(g_sum[:, :], g_exp[:, :, :], AX, ALU.add))
                link(v.reciprocal(g_prob[:, :], g_sum[:, :]))
                dve.wait_ge(exped, 2)
                link(v.tensor_scalar(denom[:, :], ratio[:, :], 1.0, None, ALU.add))
                link(v.reciprocal(w_first[:, :], denom[:, :]))
                link(v.tensor_tensor(weights[:, 0, 0:tiles], w_first[:, :], g_prob[:, :], ALU.mult))
                link(v.tensor_tensor(weights[:, 1, 0:tiles], weights[:, 0, 0:tiles], ratio[:, :], ALU.mult))
                dve.wait_ge(ranked, 1)
                link(v.tensor_copy(counts[:, :], ps_n[:, 0:NE]))
                link(v.tensor_tensor(over[:, :, :], bcast_last(counts[:, :], tiles), bcast_mid(const("steps")[:, 0:tiles], NE), ALU.is_gt))
                link(v.tensor_reduce(blocks[:, :], over[:, :, :], AX, ALU.add))
                link(v.tensor_tensor_scan(ends[:, :], const("ones")[:, 0:NE], blocks[:, :], 0.0, ALU.mult, ALU.add))
                link(v.tensor_tensor(starts[:, :], ends[:, :], blocks[:, :], ALU.subtract))
                link(v.tensor_copy(ranks[:, :, :].rearrange("p t e -> p (t e)"), ps[:, 0:tiles * NE]))
                for k in range(2):
                    link(v.tensor_tensor(product[:, :, :], ranks[:, :, :], one[k][:, :, :], ALU.mult))
                    link(v.tensor_reduce(rank[:, :], product[:, :, :], AX, ALU.add))
                    link(v.tensor_tensor(product[:, :, :], bcast_mid(starts[:, :], tiles), one[k][:, :, :], ALU.mult))
                    link(v.tensor_reduce(base[:, :], product[:, :, :], AX, ALU.add))
                    link(v.tensor_tensor(steps_over[:, :, 1:], bcast_last(rank[:, :], tiles - 1),
                                         bcast_mid(const("steps")[:, 1:tiles], tiles), ALU.is_ge))
                    link(v.tensor_reduce(above[:, :], steps_over[:, :, 1:], AX, ALU.add))
                    link(v.scalar_tensor_tensor(local[:, :], above[:, :], -float(P), rank[:, :], ALU.mult, ALU.add))
                    link(v.tensor_tensor(block_of[:, :], base[:, :], above[:, :], ALU.add))
                    link(v.scalar_tensor_tensor(place[:, :], block_of[:, :], float(P), local[:, :], ALU.mult, ALU.add))
                    link(v.tensor_copy(slots[:, k, 0:tiles], place[:, :]))
                    link(v.scalar_tensor_tensor(where[:, :], local[:, :], float(nb), block_of[:, :], ALU.mult, ALU.add))
                    link(v.tensor_copy(table_at[k][:, :], where[:, :]))
                link(v.tensor_copy(token_id[:, :], const("token")[:, 0:tiles]))
                dve.sem_inc(routed, 1)
                link(v.tensor_tensor(passed[:, :, :], bcast_mid(ends[:, :], nb), bcast_last(const("iota_b")[:, 0:nb], NE), ALU.is_le))
                link(v.tensor_reduce(owner[:, :], passed[:, :, :], AX, ALU.add))
                link(v.tensor_scalar(block_info[:, 0:nb], owner[:, :], float(NE - 1), None, ALU.min))
                link(v.tensor_copy(block_info[:, nb:nb + 1], ends[:, NE - 1:NE]))

            @block.scalar
            def _(act):
                act.wait_ge(exp_ready, 1)
                nc.scalar.activation(g_exp[:, :, :], g_diff[:, :, :], ACT.Exp).then_inc(exped, 1)
                act.wait_ge(exp_ready, 2)
                nc.scalar.activation(ratio[:, :], diff[:, :], ACT.Exp).then_inc(exped, 1)

            @block.tensor
            def _(pe):
                pe.wait_ge(both_ready, 1)
                flat = lambda ap: ap.rearrange("p t e -> p (t e)")
                nc.tensor.matmul(ps[:, 0:tiles * NE], const("before"), flat(both[:, :, :]), start=True, stop=False)
                nc.tensor.matmul(ps[:, 0:tiles * NE], const("ones"), flat(seen[:, 0:tiles, :]), start=False, stop=True)
                nc.tensor.matmul(ps_n[:, 0:NE], const("ones"), seen[:, tiles, :], start=True, stop=True).then_inc(ranked, 1)

            @block.gpsimd
            def _(pool):
                nc.gpsimd.memset(zeros[:, :], 0).then_inc(zeroed, 1)
                pool.wait_ge(zeroed, 1)
                table = dr["table"][0:P * nb, :]
                pool.dma_start(table.rearrange("(p b) one -> p (b one)", p=P), zeros[:, :]).then_inc(zero_in, 16)
                pool.wait_ge(zero_in, 16)
                pool.wait_ge(routed, 1)
                for t in range(tiles):
                    for k in range(2):
                        pool.indirect_dma_start(table, bass.IndirectOffsetOnAxis(table_at[k][:, t:t + 1], 0),
                                                token_id[:, t:t + 1], None).then_inc(scattered, 16)
                pool.wait_ge(scattered, 32 * tiles)
                pool.dma_start(tokens[:, 0:nb], table.rearrange("(p b) one -> p (b one)", p=P)).then_inc(read_back, 16)
                pool.wait_ge(read_back, 16)


def stage_experts(nc, io, dr, const, layer, tiles, block_info, tokens):
    nb = n_blocks(tiles)
    with Stage(nc, f"moe{layer}") as st:
        wg, wu = ([st.sb(f"{n}{b}", [P, KD, DE]) for b in range(2)] for n in ("wg", "wu"))
        wd = [st.sb(f"wd{b}", [P, KE, D]) for b in range(2)]
        index = [st.sb(f"index{b}", [P, 1], I32) for b in range(2)]
        rows = [st.sb(f"rows{b}", [P, D]) for b in range(2)]
        xT = st.sb("xT", [P, KD, P])
        gate, act_up = ([st.sb(f"{n}{b}", [P, DE]) for b in range(2)] for n in ("gate", "act_up"))
        aT = st.sb("aT", [P, KE, P])
        y = [st.sb(f"y{b}", [P, D]) for b in range(2)]
        ps_x = st.ps("x", [P, 2 * BANK])
        ps_g, ps_u, ps_a = (st.ps(n, [P, BANK]) for n in ("g", "u", "a"))
        ps_y = st.ps("y", [P, 2 * BANK])
        g_in, u_in, d_in = (st.sems(n, 2) for n in ("g_in", "u_in", "d_in"))
        gathered = [st.pool_dma_sem(f"gathered{b}") for b in range(2)]
        stored = st.sem("stored")
        index_ready, turned, x_read_a, x_read_v, gate_full, up_full, gated, multiplied, a_turned, a_read, y_full, y_read_a, y_read_v = (
            st.sem(n) for n in ("index_ready", "turned", "x_read_a", "x_read_v", "gate_full", "up_full", "gated", "multiplied", "a_turned",
                                "a_read", "y_full", "y_read_a", "y_read_v"))
        ident = const("ident")
        experts = lambda name: io[name][layer]

        def looped(eng, first, second=None):
            used = eng.value_load(block_info[0:1, nb:nb + 1], min_val=1, max_val=nb)
            first(0, 0)
            first(0, 1)
            if second:
                second(0, 0)
            with eng.Fori(1, nb // 2 + 1) as i:
                for b in range(2):
                    with eng.If(used > 2 * i + b):
                        first(i, b)
                    if second:
                        with eng.If(used > 2 * i + b - 1):
                            second(i if b else i - 1, 1 - b)
            return used

        with nc.Block() as block:

            @block.sync
            def _(sp):
                def load(i, b):
                    n = 2 * i + b
                    e = sp.value_load(block_info[0:1, bass.ds(n, 1)], min_val=0, max_val=NE - 1)
                    if not isinstance(i, int):
                        sp.wait_ge(up_full, n)
                    sp.dma_start(wg[b][:, :, :], experts("moe_w_gate")[e].rearrange("(p k) n -> p k n", k=KD)).then_inc(g_in[b], 16)
                    sp.dma_start(wu[b][:, :, :], experts("moe_w_up")[e].rearrange("(p k) n -> p k n", k=KD)).then_inc(u_in[b], 16)
                    if not isinstance(i, int):
                        sp.wait_ge(y_full, n - 1)
                    sp.dma_start(wd[b][:, :, :], experts("moe_w_down")[e].rearrange("(p k) n -> p k n", k=KE)).then_inc(d_in[b], 16)

                looped(sp, load)

            @block.gpsimd
            def _(pool):
                def gather(i, b):
                    n = 2 * i + b
                    if not isinstance(i, int):
                        pool.wait_ge(turned, n - 1)
                    nc.gpsimd.tensor_copy(index[b][:, :], tokens[:, bass.ds(n, 1)]).then_inc(index_ready, 1)
                    pool.wait_ge(index_ready, n + 1)
                    st.settle(pool)
                    pool.indirect_dma_start(rows[b][:, :], None, dr["h"], bass.IndirectOffsetOnAxis(index[b][:, :], 0)).then_inc(gathered[b], 16)

                looped(pool, gather)

            @block.tensor
            def _(pe):
                pe.sem_inc(up_full, 1)

                def up(i, b):
                    n = 2 * i + b
                    pe.wait_ge(gathered[b], 16 * i + 16)
                    pe.wait_ge(x_read_a, n + 1)
                    pe.wait_ge(x_read_v, n + 1)
                    xs = rows[b][:, :].rearrange("t (p k) -> t k p", k=KD)
                    for k in range(KD):
                        last = nc.tensor.transpose(ps_x[:, k * P:(k + 1) * P], xs[:, k, :], ident)
                    last.then_inc(turned, 1)
                    pe.wait_ge(x_read_a, n + 2)
                    pe.wait_ge(x_read_v, n + 2)
                    pe.wait_ge(g_in[b], 16 * i + 16)
                    pe.wait_ge(gated, n + 1)
                    for k in range(KD):
                        last = nc.tensor.matmul(ps_g[:, :], xT[:, k, :], wg[b][:, k, :], start=(k == 0), stop=(k == KD - 1))
                    last.then_inc(gate_full, 1)
                    pe.wait_ge(u_in[b], 16 * i + 16)
                    pe.wait_ge(multiplied, n + 1)
                    for k in range(KD):
                        last = nc.tensor.matmul(ps_u[:, :], xT[:, k, :], wu[b][:, k, :], start=(k == 0), stop=(k == KD - 1))
                    last.then_inc(up_full, 1)

                def down(i, b):
                    n = 2 * i + b
                    pe.wait_ge(multiplied, n + 2)
                    pe.wait_ge(a_read, n + 1)
                    cols = act_up[b][:, :].rearrange("t (p k) -> t k p", k=KE)
                    for k in range(KE):
                        last = nc.tensor.transpose(ps_a[:, k * P:(k + 1) * P], cols[:, k, :], ident)
                    last.then_inc(a_turned, 1)
                    pe.wait_ge(a_read, n + 2)
                    pe.wait_ge(d_in[b], 16 * i + 16)
                    pe.wait_ge(y_read_a, n + 1)
                    pe.wait_ge(y_read_v, n + 1)
                    for c in range(2):
                        for k in range(KE):
                            last = nc.tensor.matmul(ps_y[:, c * BANK:(c + 1) * BANK], aT[:, k, :], wd[b][:, k, c * BANK:(c + 1) * BANK],
                                                    start=(k == 0), stop=(k == KE - 1))
                    last.then_inc(y_full, 1)

                looped(pe, up, down)

            @block.scalar
            def _(act):
                act.sem_inc(x_read_a, 1)
                act.sem_inc(gated, 1)
                act.sem_inc(a_read, 1)
                act.sem_inc(y_read_a, 1)
                act.sem_inc(stored, 16)

                def first(i, b):
                    n = 2 * i + b
                    act.wait_ge(turned, n + 1)
                    act.wait_ge(up_full, n + 1)
                    nc.scalar.activation(xT[:, 0:KD // 2, :].rearrange("p k t -> p (k t)"), ps_x[:, 0:BANK], ACT.Copy).then_inc(x_read_a, 1)
                    act.wait_ge(gate_full, n + 1)
                    act.wait_ge(multiplied, n + 1)
                    nc.scalar.activation(gate[b][:, :], ps_g[:, :], ACT.Silu).then_inc(gated, 1)

                def second(i, b):
                    n = 2 * i + b
                    act.wait_ge(a_turned, n + 1)
                    nc.scalar.activation(aT[:, :, :].rearrange("p k t -> p (k t)"), ps_a[:, :], ACT.Copy).then_inc(a_read, 1)
                    act.wait_ge(y_full, n + 1)
                    act.wait_ge(stored, 16 * n + 16)
                    nc.scalar.activation(y[b][:, 0:BANK], ps_y[:, 0:BANK], ACT.Copy).then_inc(y_read_a, 1)
                    act.wait_ge(y_read_a, n + 2)
                    act.wait_ge(y_read_v, n + 2)
                    act.dma_start(dr["y"][bass.ds(n * P, P), :], y[b][:, :]).then_inc(stored, 16)

                used = looped(act, first, second)
                act.wait_ge(stored, 16 * used + 16)
                st.settle(act)

            @block.vector
            def _(dve):
                dve.sem_inc(x_read_v, 1)
                dve.sem_inc(multiplied, 1)
                dve.sem_inc(y_read_v, 1)

                def first(i, b):
                    n = 2 * i + b
                    dve.wait_ge(turned, n + 1)
                    dve.wait_ge(up_full, n + 1)
                    nc.vector.tensor_copy(xT[:, KD // 2:, :].rearrange("p k t -> p (k t)"), ps_x[:, BANK:]).then_inc(x_read_v, 1)
                    dve.wait_ge(gated, n + 2)
                    dve.wait_ge(up_full, n + 2)
                    nc.vector.tensor_tensor(act_up[b][:, :], gate[b][:, :], ps_u[:, :], ALU.mult).then_inc(multiplied, 1)

                def second(i, b):
                    n = 2 * i + b
                    dve.wait_ge(y_full, n + 1)
                    dve.wait_ge(stored, 16 * n + 16)
                    nc.vector.tensor_copy(y[b][:, BANK:], ps_y[:, BANK:]).then_inc(y_read_v, 1)

                looped(dve, first, second)


def stage_combine(nc, io, dr, const, layer, tiles, weights, slots, out):
    with Stage(nc, f"mix{layer}") as st:
        kinds = 2 if tiles > NT_X else 1
        gate = [st.sb(f"gate{s}", [P, D]) for s in range(kinds)]
        ln_g, ln_b = st.sb("ln_g", [P, D]), st.sb("ln_b", [P, D])
        x, y1, y2 = ([st.sb(f"{n}{b}", [P, D]) for b in range(2)] for n in ("x", "y1_", "y2_"))
        mixed, both, gated, res, xn, xg = (st.sb(n, [P, D]) for n in ("mixed", "both", "gated", "res", "xn", "xg"))
        xo = [st.sb(f"xo{b}", [P, D]) for b in range(2)]
        stats, mv, var, root, rstd, bias = (st.sb(n, shape) for n, shape in (
            ("stats", [P, 2, 6]), ("mv", [P, 2]), ("var", [P, 1]), ("root", [P, 1]), ("rstd", [P, 1]), ("bias", [P, 1])))
        x_in, stored = (st.sems(n, 2) for n in ("x_in", "stored"))
        y1_in, y2_in = ([st.pool_dma_sem(f"{n}_in{b}") for b in range(2)] for n in ("first", "second"))
        rows_in, chain, rooted, normed, x_ready = (st.sem(n) for n in ("rows_in", "chain", "rooted", "normed", "x_ready"))
        STEPS = 11
        ROWS_IN = 16 * (2 + kinds)
        with nc.Block() as block:

            @block.sync
            def _(sp):
                load_rows(sp, rows_in, [(ln_g[:, :], io["ln_ffn_g"][layer]), (ln_b[:, :], io["ln_ffn_b"][layer])]
                          + [(gate[s][:, :], dr["mod"][layer, s, 5 * D:6 * D]) for s in range(kinds)])
                for t in range(tiles + 2):
                    if t < tiles:
                        if t >= 2:
                            sp.wait_ge(chain, STEPS * (t - 2) + 4)
                        sp.dma_start(x[t % 2][:, :], dr["x"][t * P:(t + 1) * P, :]).then_inc(x_in[t % 2], 16)
                    if t >= 2:
                        sp.wait_ge(x_ready, t - 1)
                        sp.dma_start(out(t - 2), xo[t % 2][:, :]).then_inc(stored[t % 2], 16)
                for b in range(2):
                    sp.wait_ge(stored[b], 16 * (tiles // 2))

            @block.gpsimd
            def _(pool):
                for t in range(tiles + 1):
                    if t < tiles:
                        if t >= 2:
                            pool.wait_ge(chain, STEPS * (t - 2) + 2)
                        for k, (dst, sem) in enumerate(((y1, y1_in), (y2, y2_in))):
                            pool.indirect_dma_start(dst[t % 2][:, :], None, dr["y"],
                                                    bass.IndirectOffsetOnAxis(slots[:, k, t:t + 1], 0)).then_inc(sem[t % 2], 16)
                    if t:
                        u = t - 1
                        if u == 0:
                            pool.wait_ge(rows_in, ROWS_IN)
                        pool.wait_ge(chain, STEPS * (u + 1))
                        if u >= 2:
                            pool.wait_ge(stored[u % 2], 16 * (u // 2))
                        nc.gpsimd.tensor_tensor(xo[u % 2][:, :], xg[:, :], ln_b[:, :], ALU.add).then_inc(x_ready, 1)

            @block.scalar
            def _(act):
                for t in range(tiles):
                    act.wait_ge(chain, STEPS * t + 8)
                    nc.scalar.activation(root[:, :], var[:, :], ACT.Sqrt).then_inc(rooted, 1)
                    act.wait_ge(chain, STEPS * t + 10)
                    nc.scalar.activation(xn[:, :], res[:, :], ACT.Identity, bias=bias[:, :], scale=rstd[:, :]).then_inc(normed, 1)

            @block.vector
            def _(dve):
                dve.wait_ge(rows_in, ROWS_IN)
                for t in range(tiles):
                    s, b, n = t // NT_X, t % 2, 16 * (t // 2) + 16
                    own = Chain(dve, chain, STEPS * t)
                    dve.wait_ge(y1_in[b], n)
                    own.link(nc.vector.tensor_scalar(mixed[:, :], y1[b][:, :], weights[:, 0, t:t + 1], None, ALU.mult))
                    dve.wait_ge(y2_in[b], n)
                    own.link(nc.vector.scalar_tensor_tensor(both[:, :], y2[b][:, :], weights[:, 1, t:t + 1], mixed[:, :], ALU.mult, ALU.add))
                    own.link(nc.vector.tensor_tensor(gated[:, :], both[:, :], gate[s][:, :], ALU.mult))
                    dve.wait_ge(x_in[b], n)
                    own.link(nc.vector.scalar_tensor_tensor(res[:, :], x[b][:, :], ALPHA, gated[:, :], ALU.mult, ALU.add))
                    for c in range(2):
                        own.inc(nc.vector.bn_stats(stats[:, c, :], res[:, c * BANK:(c + 1) * BANK]))
                    own.wait()
                    st.settle(dve)
                    own.link(nc.vector.bn_aggr(mv[:, :], stats[:, :, :].rearrange("p n s -> p (n s)")))
                    own.link(nc.vector.tensor_scalar(var[:, :], mv[:, 1:2], LN_EPS, None, ALU.add))
                    dve.wait_ge(rooted, t + 1)
                    own.link(nc.vector.reciprocal(rstd[:, :], root[:, :]))
                    own.link(nc.vector.tensor_scalar(bias[:, :], mv[:, 0:1], rstd[:, :], -1.0, ALU.mult, ALU.mult))
                    dve.wait_ge(normed, t + 1)
                    if t:
                        dve.wait_ge(x_ready, t)
                    own.link(nc.vector.tensor_tensor(xg[:, :], xn[:, :], ln_g[:, :], ALU.mult))
                    assert own.n == STEPS


INPUTS = ["x", "c", "ctx", "c_ctx", "ada_w", "ada_b", "ln_mix_g", "ln_mix_b", "ln_ffn_g", "ln_ffn_b",
          "win_w_in", "win_w_out", "win_sink", "mla_w_in", "mla_q_norm", "mla_kv_norm", "mla_w_uq", "mla_w_ukv",
          "mla_w_out", "moe_w_grp", "moe_b_grp", "moe_w_rt", "moe_b_rt", "moe_w_gate", "moe_w_up", "moe_w_down"]


def program(nc, io, const_dram, const_cols, result):
    nb = n_blocks(NT_ALL)
    dr = {name: nc.dram_tensor(f"scratch_{name}", shape, dt, kind="Internal").ap() for name, shape, dt in (
        ("x", (TALL, D), F32), ("mod", (2, 2, 6 * D), F32), ("qkT", (A_QK_CHUNKS * P, TALL), F32), ("o", (TALL, D), F32),
        ("h", (TALL, D), F32), ("table", (P * nb, 1), I32), ("y", ((nb + 2) * P, D), F32))}

    def constants(st, names):
        tiles = {n: st.sb(n, [P, const_cols[n][1]]) for n in names}
        loaded = st.sem("loaded")
        with nc.Block() as block:

            @block.sync
            def _(sp):
                for n in names:
                    at, size = const_cols[n]
                    sp.dma_start(tiles[n][:, :], const_dram[:, at:at + size]).then_inc(loaded, 16)
                sp.wait_ge(loaded, 16 * len(names))

        return tiles

    with Stage(nc, "all") as every:
        Stage.settled = every.sem("settled")
        Stage.pool_dma = every.stack
        fixed = constants(every, ["ident", "ones"])
        const = lambda n: fixed[n][:, :]
        stage_mods(nc, io, dr, const)

        def feed_forward(layer, tiles, w_out, out):
            with Stage(nc, f"ff{layer}") as ff:
                logits = ff.sb("logits", [P, tiles * ROUTE])
                weights = ff.sb("weights", [P, 2, tiles])
                slots = ff.sb("slots", [P, 2, tiles], I32)
                block_info = ff.sb("block_info", [P, n_blocks(tiles) + 4], I32)
                tokens = ff.sb("tokens", [P, n_blocks(tiles) + 4], I32)
                stage_project_out(nc, io, dr, const, layer, w_out, tiles, logits)
                with Stage(nc, f"routing{layer}") as rt:
                    tables = constants(rt, ["before", "iota_e", "iota_g", "steps", "iota_b", "token"])
                    routing = lambda n: (tables[n] if n in tables else fixed[n])[:, :]
                    stage_route(nc, dr, routing, layer, tiles, logits, weights, slots, block_info, tokens)
                stage_experts(nc, io, dr, const, layer, tiles, block_info, tokens)
                stage_combine(nc, io, dr, const, layer, tiles, weights, slots, out)

        with Stage(nc, "layer0") as l0:
            v_all = l0.sb("v_all", [P, NT_ALL, A_KV * A_HD])
            with Stage(nc, "layer0_qkv") as lq:
                hT = lq.sb("hT", [P, KD, TALL])
                stage_transposed(nc, dr, const, hT, 0)
                tables = constants(lq, ["rot_a", "cos_a", "sin_a"])
                stage_window_qkv(nc, io, dr, lambda n: tables[n][:, :], hT, v_all)
            with Stage(nc, "layer0_att") as la:
                tables_m = constants(la, ["mask"])
                window = lambda n: (tables_m[n] if n in tables_m else fixed[n])[:, :]
                stage_window_attention(nc, io, dr, window, v_all)
        feed_forward(0, NT_ALL, io["win_w_out"][0], lambda t: dr["x"][t * P:(t + 1) * P, :])

        with Stage(nc, "layer1") as l1:
            tables_b = constants(l1, ["rot_b", "cos_b", "sin_b", "cos_k", "sin_k"])
            latent = lambda n: (tables_b[n] if n in tables_b else fixed[n])[:, :]
            cqT = l1.sb("cqT", [P, B_QR // P, SEQ])
            ckvT = l1.sb("ckvT", [P, B_KVR // P, TALL])
            kT = [l1.sb(f"kT{b}", [B_QD + 1, TALL]) for b in range(2)]
            stage_latents(nc, io, dr, latent, cqT, ckvT, kT)
            stage_latent_attention(nc, io, dr, latent, cqT, ckvT, kT)
        feed_forward(1, NT_X, io["mla_w_out"][0], lambda t: result[0, t * P:(t + 1) * P, :])


def kernel(**inputs):
    import concourse.bacc as bacc
    from concourse.bass_utils import run_bass_kernel_spmd

    nc = bacc.Bacc("TRN2", target_bir_lowering=False, num_devices=1)
    arrays, io = {}, {}
    for name in INPUTS:
        a = np.ascontiguousarray(inputs[name])
        arrays[f"in_{name}"] = a
        io[name] = nc.dram_tensor(f"in_{name}", a.shape, mybir.dt.from_np(a.dtype), kind="ExternalInput").ap()
    table, cols = constant_arrays()
    arrays["in_tables"] = table
    const_dram = nc.dram_tensor("in_tables", table.shape, F32, kind="ExternalInput").ap()
    result = nc.dram_tensor("out_x", (1, SEQ, D), F32, kind="ExternalOutput").ap()
    program(nc, io, const_dram, cols, result)
    return run_bass_kernel_spmd(nc, [arrays], core_ids=[0]).results[0]["out_x"]
```

```python
from contextlib import ExitStack

import numpy as np

import concourse.bass as bass
from concourse import mybir
from concourse.alu_op_type import AluOpType as ALU

F32 = mybir.dt.float32
BF16 = mybir.dt.bfloat16
F32R = mybir.dt.float32r
I32 = mybir.dt.int32
ACT = mybir.ActivationFunctionType
AX = mybir.AxisListType.X

P = 128
D = 1024
KD = D // P
SEQ, CTX = 1024, 256
TALL = SEQ + CTX
NT_X, NT_C = SEQ // P, CTX // P
NT_ALL = NT_X + NT_C
BANK = 512
GRID_W = 64
ALPHA = 4.0 ** 0.25
LN_EPS, RMS_EPS = 1e-5, 1e-6

A_HEADS, A_KV, A_GROUP, A_HD = 16, 4, 4, 64
A_QK_CHUNKS = (A_HEADS + A_KV) * A_HD // P
A_SCALE = A_HD ** -0.5

B_HEADS, B_NOPE, B_ROPE, B_V = 16, 64, 32, 64
B_QR, B_KVR = 512, 256
B_QD = B_NOPE + B_ROPE
B_IN = B_QR + B_KVR + B_ROPE
B_SCALE = B_QD ** -0.5

NG, EPG = 4, 8
NE = NG * EPG
DE = 512
KE = DE // P
BIG = 1.0e30
ROUTE = NG + NE


def n_blocks(tiles):
    return tiles * 2 + NE


def rope_angles(rot_dim):
    axis = rot_dim // 2
    inv = (np.float32(10000.0) ** (-np.arange(0, axis, 2, dtype=np.float32) / np.float32(axis))).astype(np.float32)
    pos = np.arange(SEQ)
    row = (pos // GRID_W).astype(np.float32)
    col = (pos % GRID_W).astype(np.float32)
    ang = np.zeros((rot_dim, SEQ), np.float32)
    partner = np.zeros(rot_dim, int)
    sign = np.zeros(rot_dim, np.float32)
    half = axis // 2
    for a, where in enumerate((row, col)):
        for j in range(axis):
            d = a * axis + j
            ang[d] = where * inv[j % half]
            partner[d] = d + half if j < half else d - half
            sign[d] = -1.0 if j < half else 1.0
    return ang, partner, sign


def constant_arrays():
    cols, parts = {}, []

    def add(name, a):
        full = np.zeros((P, a.shape[1]), np.float32)
        full[: a.shape[0]] = a
        at = sum(x.shape[1] for x in parts)
        cols[name] = (at, a.shape[1])
        parts.append(full)

    add("ident", np.eye(P, dtype=np.float32))
    add("ones", np.ones((P, P), np.float32))
    r, c = np.arange(P)[:, None], np.arange(P)[None, :]
    add("before", (r < c).astype(np.float32))
    add("mask", np.concatenate([np.where(c >= r, 0.0, -BIG), np.where(c <= r, 0.0, -BIG)], 1))
    ang, partner, sign = rope_angles(A_HD)
    rot = np.zeros((A_HD, A_HD), np.float32)
    rot[partner, np.arange(A_HD)] = sign
    two = np.zeros((P, P), np.float32)
    two[:A_HD, :A_HD] = rot
    two[A_HD:, A_HD:] = rot
    add("rot_a", two)
    add("cos_a", np.concatenate([np.cos(ang)] * 2, 0))
    add("sin_a", np.concatenate([np.sin(ang)] * 2, 0))
    ang, partner, sign = rope_angles(B_ROPE)
    rot = np.zeros((B_QD, B_QD), np.float32)
    rot[B_NOPE + partner, B_NOPE + np.arange(B_ROPE)] = sign
    add("rot_b", rot)
    add("cos_b", np.concatenate([np.ones((B_NOPE, SEQ)), np.cos(ang)], 0))
    add("sin_b", np.concatenate([np.zeros((B_NOPE, SEQ)), np.sin(ang)], 0))
    add("cos_k", np.cos(ang).T.reshape(NT_X, P, B_ROPE).transpose(1, 0, 2).reshape(P, -1))
    add("sin_k", (np.sin(ang) * sign[:, None]).T.reshape(NT_X, P, B_ROPE).transpose(1, 0, 2).reshape(P, -1))
    add("iota_e", np.broadcast_to(np.arange(NE) - 64.0, (P, NE)))
    add("iota_g", np.broadcast_to(np.arange(NG) - 64.0, (P, NG)))
    add("steps", np.broadcast_to(np.arange(NT_ALL) * float(P), (P, NT_ALL)))
    nb = n_blocks(NT_ALL)
    add("iota_b", np.broadcast_to(np.arange(nb) * 1.0, (P, nb)))
    add("token", np.arange(P)[:, None] + np.arange(NT_ALL)[None, :] * float(P))
    return np.ascontiguousarray(np.concatenate(parts, 1), np.float32), cols


def bcast_last(ap, n):
    return ap.unsqueeze(2).broadcast_to([ap.shape[0], ap.shape[1], n])


def bcast_mid(ap, n):
    return ap.unsqueeze(1).broadcast_to([ap.shape[0], n, ap.shape[1]])


class Chain:

    def __init__(self, eng, sem, base=0):
        self.eng, self.sem, self.base, self.n = eng, sem, base, 0

    def inc(self, instruction):
        self.n += 1
        instruction.then_inc(self.sem, 1)
        return instruction

    def wait(self):
        self.eng.wait_ge(self.sem, self.base + self.n)

    def link(self, instruction):
        self.inc(instruction)
        self.wait()


class Stage:

    settled = None

    def settle(self, eng):
        eng.sem_inc(Stage.settled, 1)

    def __init__(self, nc, name):
        self.nc, self.name, self.stack, self.used = nc, name, ExitStack(), []

    def __enter__(self):
        self.stack.__enter__()
        return self

    def __exit__(self, *a):
        if self.used and a[0] is None:
            with self.nc.Block() as block:

                @block.sync
                def _(sp):
                    for sem in self.used:
                        sp.sem_clear(sem)

        return self.stack.__exit__(*a)

    def sb(self, name, shape, dt=F32):
        return self.stack.enter_context(self.nc.sbuf_tensor(f"{self.name}_{name}", shape, dt))

    def ps(self, name, shape):
        return self.stack.enter_context(self.nc.psum_tensor(f"{self.name}_ps_{name}", shape, F32))

    def sem(self, name):
        self.used.append(self.stack.enter_context(self.nc.semaphore(f"{self.name}_{name}")))
        return self.used[-1]

    def pool_dma_sem(self, name):
        return Stage.pool_dma.enter_context(self.nc.semaphore(f"{self.name}_{name}"))

    def sems(self, name, n):
        return [self.sem(f"{name}{i}") for i in range(n)]


def stage_mods(nc, io, dr, const):
    PAIRS = 6 * D // BANK // 2
    BUFS = 4
    with Stage(nc, "mods") as st:
        w = [st.sb(f"w{b}", [P, KD, BANK]) for b in range(BUFS)]
        bias = st.sb("bias", [2, 2, 6 * D])
        rows = st.sb("rows", [2, 2, 6 * D])
        c_col = st.sb("c_col", [P, 2, KD])
        s_col = st.sb("s_col", [P, 2, KD])
        ps = [st.ps(f"ps{b}", [P, BANK]) for b in range(BUFS)]
        w_in, ps_full, ps_free = (st.sems(n, BUFS) for n in ("w_in", "ps_full", "ps_free"))
        c_in, bias_in, s_ready, copied, stored = (st.sem(n) for n in ("c_in", "bias_in", "s_ready", "copied", "stored"))
        with nc.Block() as block:

            @block.sync
            def _(sp):
                sp.dma_start(c_col[:, 0, :], io["c"][0].rearrange("(p k) -> p k", k=KD)).then_inc(c_in, 16)
                sp.dma_start(c_col[:, 1, :], io["c_ctx"].rearrange("(p k) -> p k", k=KD)).then_inc(c_in, 16)

                def load(i, b):
                    src = io["ada_w"][b // 2].rearrange("(p k) n -> p k n", k=KD)
                    sp.dma_start(w[b][:, :, :], src[:, :, bass.ds((i * 2 + b % 2) * BANK, BANK)]).then_inc(w_in[b], 16)

                for b in range(BUFS):
                    load(0, b)
                with sp.Fori(1, PAIRS) as i:
                    for b in range(BUFS):
                        sp.wait_ge(ps_full[b], i)
                        load(i, b)
                for b in range(BUFS):
                    sp.wait_ge(ps_free[b], PAIRS + 1)
                for l in range(2):
                    sp.dma_start(dr["mod"][l], rows[:, l, :]).then_inc(stored, 16)
                sp.wait_ge(stored, 32)
                sp.wait_ge(copied, 32)

            @block.scalar
            def _(act):
                for l in range(2):
                    act.dma_start(bias[:, l, :], io["ada_b"][l].partition_broadcast(2)).then_inc(bias_in, 16)
                act.wait_ge(c_in, 32)
                nc.scalar.activation(s_col[:, :, :], c_col[:, :, :], ACT.Silu).then_inc(s_ready, 1)
                act.dma_start(dr["x"][0:SEQ, :], io["x"][0]).then_inc(copied, 16)
                act.dma_start(dr["x"][SEQ:TALL, :], io["ctx"][0]).then_inc(copied, 16)

            @block.vector
            def _(dve):
                for b in range(BUFS):
                    dve.sem_inc(ps_free[b], 1)
                dve.wait_ge(bias_in, 32)
                with dve.Fori(0, PAIRS) as i:
                    for b in range(BUFS):
                        at = bass.ds((i * 2 + b % 2) * BANK, BANK)
                        dve.wait_ge(ps_full[b], i + 1)
                        nc.vector.tensor_tensor(rows[:, b // 2, at], ps[b][0:2, :], bias[:, b // 2, at],
                                                ALU.add).then_inc(ps_free[b], 1)

            @block.tensor
            def _(pe):
                pe.wait_ge(s_ready, 1)
                with pe.Fori(0, PAIRS) as i:
                    for b in range(BUFS):
                        pe.wait_ge(ps_free[b], i + 1)
                        pe.wait_ge(w_in[b], 16 * i + 16)
                        for k in range(KD):
                            last = nc.tensor.matmul(ps[b][0:2, :], s_col[:, :, k], w[b][:, k, :],
                                                    start=(k == 0), stop=(k == KD - 1))
                        last.then_inc(ps_full[b], 1)


def stage_transposed(nc, dr, const, hT, layer):
    with Stage(nc, f"tr{layer}") as st:
        x = [st.sb(f"x{b}", [P, D]) for b in range(2)]
        shift = st.sb("shift", [P, 2, KD])
        scale = st.sb("scale", [P, 2, KD])
        scale1 = st.sb("scale1", [P, 2, KD])
        ps = [st.ps(f"ps{b}", [P, 2 * BANK]) for b in range(2)]
        x_in, ps_full, ps_free_a, ps_free_v = (st.sems(n, 2) for n in ("x_in", "ps_full", "ps_free_a", "ps_free_v"))
        m_in, m_ready = st.sem("m_in"), st.sem("m_ready")
        ident = const("ident")

        def halves(eng, per):
            with eng.Fori(0, NT_X // 2) as i:
                for b in range(2):
                    per(i, b, 0)
            for b in range(2):
                per(NT_X // 2, b, 1)

        with nc.Block() as block:

            @block.sync
            def _(sp):
                for s in range(2):
                    for tile, part in ((shift, 0), (scale, 1)):
                        sp.dma_start(tile[:, s, :], dr["mod"][layer, s, part * D:(part + 1) * D].rearrange("(p k) -> p k", k=KD)).then_inc(m_in, 16)

                def load(i, b):
                    sp.dma_start(x[b][:, :], dr["x"][bass.ds((i * 2 + b) * P, P), :]).then_inc(x_in[b], 16)

                for b in range(2):
                    load(0, b)
                with sp.Fori(1, NT_ALL // 2) as i:
                    for b in range(2):
                        sp.wait_ge(ps_full[b], i)
                        load(i, b)

            @block.tensor
            def _(pe):
                def turn(i, b, s):
                    pe.wait_ge(x_in[b], 16 * i + 16)
                    pe.wait_ge(ps_free_a[b], i + 1)
                    pe.wait_ge(ps_free_v[b], i + 1)
                    rows = x[b][:, :].rearrange("t (p k) -> t k p", k=KD)
                    for k in range(KD):
                        last = nc.tensor.transpose(ps[b][:, k * P:(k + 1) * P], rows[:, k, :], ident)
                    last.then_inc(ps_full[b], 1)

                halves(pe, turn)

            @block.scalar
            def _(act):
                for b in range(2):
                    act.sem_inc(ps_free_a[b], 1)
                act.wait_ge(m_ready, 1)

                def out(i, b, s):
                    act.wait_ge(ps_full[b], i + 1)
                    for k in range(0, KD // 2):
                        last = nc.scalar.activation(hT[:, k, bass.ds((i * 2 + b) * P, P)], ps[b][:, k * P:(k + 1) * P],
                                                    ACT.Identity, bias=shift[:, s, k:k + 1], scale=scale1[:, s, k:k + 1])
                    last.then_inc(ps_free_a[b], 1)

                halves(act, out)

            @block.vector
            def _(dve):
                for b in range(2):
                    dve.sem_inc(ps_free_v[b], 1)
                dve.wait_ge(m_in, 64)
                nc.vector.tensor_scalar(scale1[:, :, :], scale[:, :, :], 1.0, None, ALU.add).then_inc(m_ready, 1)
                dve.wait_ge(m_ready, 1)

                def out(i, b, s):
                    dve.wait_ge(ps_full[b], i + 1)
                    for k in range(KD // 2, KD):
                        last = nc.vector.tensor_scalar(hT[:, k, bass.ds((i * 2 + b) * P, P)], ps[b][:, k * P:(k + 1) * P],
                                                       scale1[:, s, k:k + 1], shift[:, s, k:k + 1], ALU.mult, ALU.add)
                    last.then_inc(ps_free_v[b], 1)

                halves(dve, out)


N_CUTS = [(0, BANK), (BANK, BANK), (2 * BANK, CTX)]


def stage_window_qkv(nc, io, dr, const, hT, v_all):
    with Stage(nc, "qkv") as st:
        w = [st.sb(f"w{b}", [P, KD, P]) for b in range(2)]
        wv = st.sb("wv", [P, KD, A_KV * A_HD])
        raw = [st.sb(f"raw{b}", [P, SEQ]) for b in range(2)]
        rawcos = [st.sb(f"rawcos{b}", [P, SEQ]) for b in range(2)]
        rotsin = [st.sb(f"rotsin{b}", [P, SEQ]) for b in range(2)]
        out = [st.sb(f"out{b}", [P, TALL]) for b in range(2)]
        ps = [st.ps(f"ps{n}", [P, BANK]) for n in range(3)]
        ps_rot = [st.ps(f"rot{n}", [P, BANK]) for n in range(2)]
        w_in, cos_ready, out_ready, stored = (st.sems(n, 2) for n in ("w_in", "cos_ready", "out_ready", "stored"))
        ps_full, copied = (st.sems(n, 3) for n in ("ps_full", "copied"))
        rot_full, rotsin_ready = (st.sems(n, 2) for n in ("rot_full", "rotsin_ready"))
        wv_in, v_full, v_read, ones_ready = (st.sem(n) for n in ("wv_in", "v_full", "v_read", "ones_ready"))
        cos, sin, rot = const("cos_a"), const("sin_a"), const("rot_a")
        w_dram = io["win_w_in"][0].rearrange("(p k) n -> p k n", k=KD)
        PAIRS = A_QK_CHUNKS // 2
        with nc.Block() as block:

            @block.sync
            def _(sp):
                def load(i, b):
                    sp.dma_start(w[b][:, :, :], w_dram[:, :, bass.ds((i * 2 + b) * P, P)]).then_inc(w_in[b], 16)

                def store(i, b):
                    sp.wait_ge(out_ready[b], i + 2)
                    st.settle(sp)
                    sp.wait_ge(copied[2], 2 * i + b + 2)
                    st.settle(sp)
                    sp.dma_start(dr["qkT"][bass.ds((i * 2 + b) * P, P), :], out[b][:, :]).then_inc(stored[b], 16)

                for b in range(2):
                    sp.sem_inc(stored[b], 16)
                    load(0, b)
                sp.dma_start(wv[:, :, :], w_dram[:, :, A_QK_CHUNKS * P:]).then_inc(wv_in, 16)
                with sp.Fori(1, PAIRS) as i:
                    for b in range(2):
                        sp.wait_ge(ps_full[2], 2 * i + b - 1)
                        load(i, b)
                        store(i - 1, b)
                for b in range(2):
                    store(PAIRS - 1, b)
                for b in range(2):
                    sp.wait_ge(stored[b], 16 * PAIRS + 16)

            @block.tensor
            def _(pe):
                for n in range(2):
                    pe.sem_inc(rot_full[n], 2)
                with pe.Fori(0, PAIRS) as i:
                    for b in range(2):
                        pe.wait_ge(w_in[b], 16 * i + 16)
                        for n, (at, size) in enumerate(N_CUTS):
                            pe.wait_ge(copied[n], 2 * i + b + 1)
                            for k in range(KD):
                                last = nc.tensor.matmul(ps[n][:, 0:size], w[b][:, k, :], hT[:, k, at:at + size],
                                                        start=(k == 0), stop=(k == KD - 1))
                            last.then_inc(ps_full[n], 1)
                        for n in range(2):
                            pe.wait_ge(copied[n], 2 * i + b + 2)
                            pe.wait_ge(rotsin_ready[n], 2 * i + b + 1)
                            nc.tensor.matmul(ps_rot[n][:, :], rot, raw[b][:, n * BANK:(n + 1) * BANK],
                                             start=True, stop=True).then_inc(rot_full[n], 1)
                pe.wait_ge(wv_in, 16)
                for t in range(NT_ALL):
                    if t < 3:
                        pe.wait_ge(copied[t], 2 * PAIRS + 1)
                    else:
                        pe.wait_ge(v_read, t - 2)
                    for k in range(KD):
                        last = nc.tensor.matmul(ps[t % 3][:, 0:A_KV * A_HD], hT[:, k, t * P:(t + 1) * P], wv[:, k, :],
                                                start=(k == 0), stop=(k == KD - 1))
                    last.then_inc(v_full, 1)

            @block.scalar
            def _(act):
                for n in range(3):
                    act.sem_inc(copied[n], 1)
                with act.Fori(0, PAIRS) as i:
                    for b in range(2):
                        act.wait_ge(cos_ready[b], i + 1)
                        for n in range(2):
                            act.wait_ge(rot_full[n], 2 * i + b + 1)
                            act.wait_ge(ps_full[n], 2 * i + b + 1)
                            nc.scalar.activation(raw[b][:, n * BANK:(n + 1) * BANK], ps[n][:, :], ACT.Copy).then_inc(copied[n], 1)
                        act.wait_ge(ps_full[2], 2 * i + b + 1)
                        act.wait_ge(stored[b], 16 * i + 16)
                        nc.scalar.activation(out[b][:, SEQ:TALL], ps[2][:, 0:CTX], ACT.Copy).then_inc(copied[2], 1)
                for t in range(NT_ALL):
                    act.wait_ge(v_full, t + 1)
                    nc.scalar.activation(v_all[:, t, :, 0:A_HD], ps[t % 3][:, 0:A_KV * A_HD].rearrange("p (h e) -> p h e", e=A_HD), ACT.Copy).then_inc(v_read, 1)

            @block.gpsimd
            def _(pool):
                nc.gpsimd.memset(v_all[:, :, :, A_HD:].rearrange("p t h e -> p (t h e)"), 1.0).then_inc(ones_ready, 1)
                pool.wait_ge(ones_ready, 1)
                for b in range(2):
                    pool.sem_inc(cos_ready[b], 1)
                with pool.Fori(0, PAIRS) as i:
                    for b in range(2):
                        for n in range(2):
                            pool.wait_ge(copied[n], 2 * i + b + 2)
                        pool.wait_ge(out_ready[b], i + 1)
                        nc.gpsimd.tensor_tensor(rawcos[b][:, :], raw[b][:, :], cos, ALU.mult).then_inc(cos_ready[b], 1)

            @block.vector
            def _(dve):
                for n in range(2):
                    dve.sem_inc(rotsin_ready[n], 1)
                    dve.sem_inc(out_ready[n], 1)
                with dve.Fori(0, PAIRS) as i:
                    for b in range(2):
                        dve.wait_ge(out_ready[b], i + 1)
                        for n in range(2):
                            dve.wait_ge(rot_full[n], 2 * i + b + 3)
                            nc.vector.tensor_tensor(rotsin[b][:, n * BANK:(n + 1) * BANK], ps_rot[n][:, :],
                                                    sin[:, n * BANK:(n + 1) * BANK], ALU.mult).then_inc(rotsin_ready[n], 1)
                        for n in range(2):
                            dve.wait_ge(rotsin_ready[n], 2 * i + b + 2)
                        dve.wait_ge(cos_ready[b], i + 2)
                        dve.wait_ge(stored[b], 16 * i + 16)
                        nc.vector.tensor_tensor(out[b][:, 0:SEQ], rawcos[b][:, :], rotsin[b][:, :], ALU.add).then_inc(out_ready[b], 1)


def stage_window_attention(nc, io, dr, const, v_all):
    BLOCKS = NT_ALL
    PAIR = [(b, blk) for b in range(2) for blk in range(BLOCKS)]
    STEPS, TURNS = len(PAIR), A_KV // 2
    HQ, VW = A_GROUP * P, A_HD + 1

    def window(blk):
        return [t for t in (blk - 1, blk, blk + 1) if 0 <= t < NT_X] if blk < NT_X else []

    def keys_of(s):
        return window(PAIR[s][1]) + [NT_X, NT_X + 1]

    before = [sum(len(keys_of(z)) for z in range(s)) for s in range(STEPS + 1)]
    CHUNKS = before[STEPS]
    FILL = dr["y"].shape[0] // P // TURNS
    FIRST = 2

    with Stage(nc, "wat") as st:
        q = [st.sb(f"q{b}", [P, A_GROUP, TALL]) for b in range(2)]
        k = [st.sb(f"k{b}", [P, TALL]) for b in range(2)]
        q_round = [st.sb(f"q_round{b}", [P, A_GROUP, P], F32R) for b in range(2)]
        k_round = [st.sb(f"k_round{b}", [P, TALL], F32R) for b in range(2)]
        ident_h, mask_h = st.sb("ident_h", [P, P], BF16), st.sb("mask_h", [P, 2 * P], BF16)
        zeros = st.sb("zeros", [P, TALL])
        sinks, sink_raw = st.sb("sinks", [P, A_HEADS]), st.sb("sink_raw", [P, A_HEADS])
        probs = [st.sb(f"probs{b}", [P, 5, HQ]) for b in range(2)]
        outs = [st.sb(f"outs{b}", [P, A_GROUP, A_HD]) for b in range(2)]
        raw, top, denom, inv = (st.sb(n, [P, A_GROUP]) for n in ("raw", "top", "denom", "inv"))
        diff, sink_exp = ([st.sb(f"{n}{b}", [P, A_GROUP]) for b in range(4)] for n in ("diff", "sink_exp"))
        ps_a = [st.ps(f"a{b}", [P, 2 * BANK]) for b in range(2)]
        ps_b = [st.ps(f"b{b}", [P, BANK]) for b in range(2)]
        ps_o, ps_m = st.ps("o", [P, BANK]), st.ps("m", [P, BANK])
        q_in, q_first_in, k_in, stored = (st.sems(n, 2) for n in ("q_in", "q_first_in", "k_in", "stored"))
        filled = st.sem("filled")
        sinks_in, sink_ready, zeros_full, k_zeroed, q_zeroed, zeros_ready, ones_ready, const_ready, q_rounded, k_rounded, scored, max_ready, top_ready, diff_ready = (
            st.sem(n) for n in ("sinks_in", "sink_ready", "zeros_full", "k_zeroed", "q_zeroed", "zeros_ready", "ones_ready", "const_ready", "q_rounded", "k_rounded", "scored", "max_ready", "top_ready", "diff_ready"))
        row_full, row_ready, key_scored, exp_done, sink_exp_done, pv_full, inv_step, out_done = (
            st.sem(n) for n in ("row_full", "row_ready", "key_scored", "exp_done", "sink_exp_done", "pv_full", "inv_step", "out_done"))
        ident = const("ident")

        with nc.Block() as block:

            @block.sync
            def _(sp):
                sp.dma_start(sinks[:, :], io["win_sink"][0].partition_broadcast(P)).then_inc(sinks_in, 16)
                for b in range(2):
                    sp.sem_inc(stored[b], 16)

                def load(i, b):
                    g = 2 * i + b
                    sp.dma_start(k[b][0:A_HD, :], dr["qkT"][bass.ds(g * A_HD + A_HEADS * A_HD, A_HD), :]).then_inc(k_in[b], 16)
                    for sem, at, end in ((q_first_in[b], 0, FIRST * P), (q_in[b], FIRST * P, TALL)):
                        sp.dma_start(q[b][0:A_HD, :, at:end], dr["qkT"][bass.ds(g * A_GROUP * A_HD, A_GROUP * A_HD), at:end]
                                     .rearrange("(h d) t -> d h t", d=A_HD)).then_inc(sem, 16)

                def store(i, b):
                    for s, (b_s, blk) in enumerate(PAIR):
                        if b_s == b:
                            sp.wait_ge(out_done, i * STEPS + s + 2)
                            st.settle(sp)
                            sp.dma_start(dr["o"][blk * P:(blk + 1) * P, bass.ds((2 * i + b) * A_GROUP * A_HD, A_GROUP * A_HD)],
                                         outs[s % 2][:, :, :].rearrange("p h e -> p (h e)")).then_inc(stored[s % 2], 16)
                            fill(i, s)

                def fill(i, s):
                    lo, hi = s * FILL // STEPS, (s + 1) * FILL // STEPS
                    sp.dma_start(dr["y"][bass.ds((i * FILL + lo) * P, (hi - lo) * P), :].rearrange("(b p) d -> p b d", p=P),
                                 bcast_mid(zeros[:, 0:D], hi - lo)).then_inc(filled, 16)

                for b in range(2):
                    load(0, b)
                sp.wait_ge(zeros_full, 1)
                with sp.Fori(0, TURNS - 1) as i:
                    for b in range(2):
                        store(i, b)
                        load(i + 1, b)
                for b in range(2):
                    store(TURNS - 1, b)
                for b in range(2):
                    sp.wait_ge(stored[b], 16 * (TURNS * STEPS // 2 + 1))
                sp.wait_ge(filled, 16 * TURNS * STEPS)

            @block.gpsimd
            def _(pool):
                pool.wait_ge(k_zeroed, 2)
                for b in range(2):
                    nc.gpsimd.memset(k[b][A_HD:VW, :], 1.0).then_inc(ones_ready, 1)
                    pool.wait_ge(ones_ready, b + 1)
                with pool.Fori(0, TURNS) as i:
                    for b in range(2):
                        pool.wait_ge(k_in[b], 16 * i + 16)
                        pool.wait_ge(scored, i * STEPS * A_GROUP + 2 * A_GROUP)
                        st.settle(pool)
                        nc.gpsimd.tensor_copy(k_round[b][0:A_HD, :], k[b][0:A_HD, :]).then_inc(k_rounded, 1)
                        for s, (b_s, blk) in enumerate(PAIR):
                            if b_s == b:
                                if blk in (0, FIRST):
                                    pool.wait_ge((q_first_in if blk == 0 else q_in)[b], 16 * i + 16)
                                pool.wait_ge(scored, (i * STEPS + s + 1) * A_GROUP)
                                st.settle(pool)
                                nc.gpsimd.tensor_copy(q_round[s % 2][0:A_HD, :, :], q[b][0:A_HD, :, blk * P:(blk + 1) * P]).then_inc(q_rounded, 1)

            @block.tensor
            def _(pe):
                pe.sem_inc(scored, 2 * A_GROUP)
                pe.sem_inc(pv_full, 2)
                pe.wait_ge(ones_ready, 2)
                pe.wait_ge(zeros_ready, 4)
                pe.wait_ge(q_zeroed, 2 * A_GROUP)
                pe.wait_ge(const_ready, 2)
                with pe.Fori(0, TURNS) as i:

                    def scores(s, h):
                        b, blk = PAIR[s]
                        tiles = window(blk)
                        at = BANK - P * len(tiles)
                        u = A_GROUP * (i * STEPS + s) + h
                        if h == 0:
                            pe.wait_ge(q_rounded, i * STEPS + s + 1)
                            pe.wait_ge(k_rounded, 2 * i + b + 1)
                        pe.wait_ge(max_ready, u + 1)
                        qb, a = q_round[s % 2][:, h, :], ps_a[h % 2]
                        if tiles:
                            nc.tensor.matmul(a[:, at:BANK], qb, k_round[b][:, tiles[0] * P:(tiles[-1] + 1) * P], start=True, stop=False)
                            masked = [(t, m) for t, m in ((blk - 1, 0), (blk + 1, 1)) if t in tiles]
                            for t, m in masked:
                                c = at + (t - tiles[0]) * P
                                nc.tensor.matmul(a[:, c:c + P], ident_h[:, :], mask_h[:, m * P:(m + 1) * P],
                                                 start=False, stop=(t, m) == masked[-1])
                        nc.tensor.matmul(a[:, BANK:BANK + CTX], qb, k_round[b][:, SEQ:TALL], start=True, stop=True).then_inc(scored, 1)

                    def rows(s):
                        pe.wait_ge(top_ready, i * STEPS + s + 1)
                        pe.wait_ge(row_ready, i * STEPS + s + 1)
                        for h in range(A_GROUP):
                            last = nc.tensor.transpose(ps_m[0:1, h * P:(h + 1) * P], top[:, h:h + 1], ident)
                        last.then_inc(row_full, 1)

                    def chunk(s, c):
                        b, blk = PAIR[s]
                        t = keys_of(s)[c]
                        n = before[s] + c
                        if c == 0:
                            if blk in (0, FIRST):
                                pe.wait_ge((q_first_in if blk == 0 else q_in)[b], 16 * i + 16)
                            pe.wait_ge(row_ready, i * STEPS + s + 2)
                        pe.wait_ge(exp_done, i * CHUNKS + n + 1)
                        mask = {blk - 1: 1, blk + 1: 0}.get(t) if t < NT_X and blk < NT_X else None
                        last = nc.tensor.matmul(ps_b[n % 2][:, :], k[b][:, t * P:(t + 1) * P], q[b][:, :, blk * P:(blk + 1) * P],
                                                start=True, stop=mask is None)
                        if mask is not None:
                            last = nc.tensor.matmul(ps_b[n % 2][:, :].rearrange("p (h q) -> p h q", h=A_GROUP), ident_h[:, :],
                                                    bcast_mid(mask_h[:, mask * P:(mask + 1) * P], A_GROUP), start=False, stop=True)
                        last.then_inc(key_scored, 1)

                    def mix(s, h):
                        b, _ = PAIR[s]
                        keys = keys_of(s)
                        if h == 0:
                            pe.wait_ge(exp_done, i * CHUNKS + before[s + 1] + 2)
                            pe.wait_ge(out_done, i * STEPS + s + 1)
                        for c, t in enumerate(keys):
                            last = nc.tensor.matmul(ps_o[:, h * VW:(h + 1) * VW], probs[s % 2][:, c, h * P:(h + 1) * P],
                                                    v_all[:, t, bass.ds(2 * i + b, 1), :].rearrange("p h e -> p (h e)"),
                                                    start=(c == 0), stop=(c == len(keys) - 1))
                        if h == A_GROUP - 1:
                            last.then_inc(pv_full, 1)

                    for h in range(A_GROUP):
                        scores(0, h)
                    rows(0)
                    for s in range(STEPS):
                        more, earlier = s + 1 < STEPS, s > 0
                        n = len(keys_of(s))
                        chunk(s, 0)
                        if more:
                            scores(s + 1, 0)
                            scores(s + 1, 1)
                        if earlier:
                            mix(s - 1, 0)
                        chunk(s, 1)
                        if more:
                            scores(s + 1, 2)
                        if earlier:
                            mix(s - 1, 1)
                        if n > 2:
                            chunk(s, 2)
                        if more:
                            scores(s + 1, 3)
                        if earlier:
                            mix(s - 1, 2)
                        for c in range(3, n):
                            chunk(s, c)
                        if more:
                            rows(s + 1)
                        if earlier:
                            mix(s - 1, 3)
                    for h in range(A_GROUP):
                        mix(STEPS - 1, h)

            @block.scalar
            def _(act):
                act.sem_inc(exp_done, 2)
                nc.scalar.activation(ident_h[:, :], ident, ACT.Copy).then_inc(const_ready, 1)
                nc.scalar.activation(mask_h[:, :], const("mask"), ACT.Copy).then_inc(const_ready, 1)
                act.wait_ge(zeros_full, 1)
                for b in range(2):
                    for h in range(A_GROUP):
                        nc.scalar.activation(q[b][A_HD:P, h, :], zeros[A_HD:P, :], ACT.Copy).then_inc(q_zeroed, 1)
                with act.Fori(0, TURNS) as i:

                    def sink_part(s):
                        act.wait_ge(diff_ready, i * STEPS + s + 1)
                        nc.scalar.activation(sink_exp[s % 4][:, :], diff[s % 4][:, :], ACT.Exp, scale=A_SCALE).then_inc(sink_exp_done, 1)

                    sink_part(0)
                    for s in range(STEPS):
                        act.wait_ge(pv_full, i * STEPS + s + 1)
                        for c in range(len(keys_of(s))):
                            n = before[s] + c
                            act.wait_ge(key_scored, i * CHUNKS + n + 1)
                            nc.scalar.activation(probs[s % 2][:, c, :], ps_b[n % 2][:, :], ACT.Exp, scale=A_SCALE).then_inc(exp_done, 1)
                        if s + 1 < STEPS:
                            sink_part(s + 1)

            @block.vector
            def _(dve):
                dve.sem_inc(out_done, 1)
                dve.sem_inc(max_ready, 2)
                dve.sem_inc(row_ready, 1)
                dve.wait_ge(sinks_in, 16)
                nc.vector.tensor_scalar(sink_raw[:, :], sinks[:, :], 1.0 / A_SCALE, None, ALU.mult).then_inc(sink_ready, 1)
                nc.vector.memset(zeros[:, :], 0.0).then_inc(zeros_full, 1)
                for b in range(2):
                    nc.vector.memset(k[b][A_HD:P, :], 0.0).then_inc(k_zeroed, 1)
                for b in range(2):
                    nc.vector.memset(k_round[b][A_HD:P, :].bitcast(F32), 0.0).then_inc(zeros_ready, 1)
                    nc.vector.memset(q_round[b][A_HD:P, :, :].bitcast(F32), 0.0).then_inc(zeros_ready, 1)
                dve.wait_ge(sink_ready, 1)
                dve.wait_ge(q_zeroed, 2 * A_GROUP)
                with dve.Fori(0, TURNS) as i:

                    def maxima(s):
                        b, blk = PAIR[s]
                        at = BANK - P * len(window(blk))
                        for h in range(A_GROUP):
                            dve.wait_ge(scored, A_GROUP * (i * STEPS + s) + h + 1 + 2 * A_GROUP)
                            nc.vector.tensor_reduce(raw[:, h:h + 1], ps_a[h % 2][:, at:BANK + CTX], AX, ALU.max).then_inc(max_ready, 1)
                        sink_g = sink_raw[:, bass.ds((2 * i + b) * A_GROUP, A_GROUP)]
                        dve.wait_ge(max_ready, A_GROUP * (i * STEPS + s + 1) + 2)
                        nc.vector.tensor_tensor(top[:, :], raw[:, :], sink_g, ALU.max).then_inc(top_ready, 1)
                        dve.wait_ge(top_ready, i * STEPS + s + 1)
                        nc.vector.tensor_tensor(diff[s % 4][:, :], sink_g, top[:, :], ALU.subtract).then_inc(diff_ready, 1)
                        dve.wait_ge(row_full, i * STEPS + s + 1)
                        nc.vector.tensor_scalar(q[b][A_HD:VW, :, blk * P:(blk + 1) * P], ps_m[0:1, :].rearrange("p (h q) -> p h q", h=A_GROUP),
                                                -1.0, None, ALU.mult).then_inc(row_ready, 1)

                    def finish(s):
                        sums = ps_o[:, 0:A_GROUP * VW].rearrange("p (h e) -> p h e", e=VW)
                        n = 2 * (i * STEPS + s)
                        dve.wait_ge(sink_exp_done, i * STEPS + s + 1)
                        dve.wait_ge(pv_full, i * STEPS + s + 3)
                        nc.vector.tensor_tensor(denom[:, :], sums[:, :, A_HD], sink_exp[s % 4][:, :], ALU.add).then_inc(inv_step, 1)
                        dve.wait_ge(inv_step, n + 1)
                        nc.vector.reciprocal(inv[:, :], denom[:, :]).then_inc(inv_step, 1)
                        dve.wait_ge(inv_step, n + 2)
                        dve.wait_ge(stored[s % 2], 16 * (i * (STEPS // 2) + s // 2) + 16)
                        nc.vector.tensor_tensor(outs[s % 2][:, :, :], sums[:, :, 0:A_HD], bcast_last(inv[:, :], A_HD),
                                                ALU.mult).then_inc(out_done, 1)

                    maxima(0)
                    for s in range(STEPS):
                        if s + 1 < STEPS:
                            maxima(s + 1)
                        if s:
                            finish(s - 1)
                    finish(STEPS - 1)


def stage_latents(nc, io, dr, const, cqT, ckvT, kT):
    with Stage(nc, "lat") as st:
        w = st.sb("w", [P, KD, B_IN])
        x = [st.sb(f"x{b}", [P, D]) for b in range(2)]
        xT = [st.sb(f"xT{b}", [P, KD, P]) for b in range(2)]
        lat = [st.sb(f"lat{b}", [P, B_IN]) for b in range(2)]
        shift, scale, scale1 = (st.sb(n, [P, 2, KD]) for n in ("shift", "scale", "scale1"))
        q_gain, kv_gain = st.sb("q_gain", [P, B_QR // P]), st.sb("kv_gain", [P, B_KVR // P])
        squares = [st.sb(f"squares{n}", [P, BANK]) for n in range(2)]
        sums, mean, root, rstd = (st.sb(n, [P, 2, 2]) for n in ("sums", "mean", "root", "rstd"))
        kcos, ksin = st.sb("kcos", [P, B_ROPE]), st.sb("ksin", [P, B_ROPE])
        ps_x = [st.ps(f"x{b}", [P, 2 * BANK]) for b in range(2)]
        ps_c = st.ps("c", [P, 2 * BANK])
        ps_z = st.ps("z", [P, 2 * BANK])
        x_in = st.sems("x_in", 2)
        w_in, m_in, m_ready = st.sem("w_in"), st.sem("m_in"), st.sem("m_ready")
        turned, xT_a, xT_v, projected, squared, rooted, chain, c_read, c_scaled, lat_full, z_read_a, z_read_v = (
            st.sem(n) for n in ("turned", "xT_a", "xT_v", "projected", "squared", "rooted", "chain", "c_read", "c_scaled", "lat_full", "z_read_a", "z_read_v"))
        ident = const("ident")
        KQ, KV = B_QR // P, B_KVR // P
        ROPE_AT = B_QR + B_KVR
        CHAIN = 4

        def skewed(eng, turn, first, second):
            X = NT_X // 2
            turn(0, 0, 0)
            turn(0, 1, 0)
            first(0, 0, 0)
            turn(1, 0, 0)
            first(0, 1, 0)
            second(0, 0, 0)

            def pair(i, s_next):
                turn(i, 1, 0)
                first(i, 0, 0)
                second(i - 1, 1, 0)
                turn(i + 1, 0, s_next)
                first(i, 1, 0)
                second(i, 0, 0)

            with eng.Fori(1, X - 1) as i:
                pair(i, 0)
            pair(X - 1, 1)
            turn(X, 1, 1)
            first(X, 0, 1)
            second(X - 1, 1, 0)
            first(X, 1, 1)
            second(X, 0, 1)
            second(X, 1, 1)

        with nc.Block() as block:

            @block.sync
            def _(sp):
                def load(i, b):
                    sp.dma_start(x[b][:, :], dr["x"][bass.ds((i * 2 + b) * P, P), :]).then_inc(x_in[b], 16)

                for b in range(2):
                    load(0, b)
                for s in range(2):
                    for tile, part in ((shift, 0), (scale, 1)):
                        sp.dma_start(tile[:, s, :], dr["mod"][1, s, part * D:(part + 1) * D].rearrange("(p k) -> p k", k=KD)).then_inc(m_in, 16)
                sp.dma_start(q_gain[:, :], io["mla_q_norm"][0].rearrange("(p k) -> p k", k=KQ)).then_inc(m_in, 16)
                sp.dma_start(kv_gain[:, :], io["mla_kv_norm"][0].rearrange("(p k) -> p k", k=KV)).then_inc(m_in, 16)
                sp.dma_start(w[:, :, :], io["mla_w_in"][0].rearrange("(p k) n -> p k n", k=KD)).then_inc(w_in, 16)
                with sp.Fori(1, NT_ALL // 2) as i:
                    for b in range(2):
                        sp.wait_ge(turned, 2 * i + b - 1)
                        load(i, b)

            @block.tensor
            def _(pe):
                def turn(i, b, s):
                    t = 2 * i + b
                    rows = x[b][:, :].rearrange("t (p k) -> t k p", k=KD)
                    pe.wait_ge(x_in[b], 16 * i + 16)
                    pe.wait_ge(xT_a, t + 1)
                    pe.wait_ge(xT_v, t + 1)
                    for k in range(KD):
                        last = nc.tensor.transpose(ps_x[b][:, k * P:(k + 1) * P], rows[:, k, :], ident)
                    last.then_inc(turned, 1)

                def project(i, b, s):
                    t = 2 * i + b
                    if isinstance(i, int) and t == 0:
                        pe.wait_ge(w_in, 16)
                    pe.wait_ge(xT_a, t + 3)
                    pe.wait_ge(xT_v, t + 3)
                    pe.wait_ge(c_read, t + 1)
                    pe.wait_ge(c_scaled, t + 1)
                    cuts = ((0, B_QR), (B_QR, B_IN)) if s == 0 else ((B_QR, B_IN),)
                    for lo, hi in cuts:
                        for k in range(KD):
                            last = nc.tensor.matmul(ps_c[:, lo:hi], xT[b][:, k, :], w[:, k, lo:hi],
                                                    start=(k == 0), stop=(k == KD - 1))
                    last.then_inc(projected, 1)

                def turn_latents(i, b, s):
                    t = 2 * i + b
                    pe.wait_ge(c_read, t + 2)
                    pe.wait_ge(c_scaled, t + 2)
                    pe.wait_ge(z_read_a, t + 1)
                    pe.wait_ge(z_read_v, t + 1)
                    if s == 0:
                        cq = lat[b][:, 0:B_QR].rearrange("t (p k) -> t k p", k=KQ)
                        for k in range(KQ):
                            nc.tensor.transpose(ps_z[:, k * P:(k + 1) * P], cq[:, k, :], ident)
                    kv = lat[b][:, B_QR:ROPE_AT].rearrange("t (p k) -> t k p", k=KV)
                    for k in range(KV):
                        nc.tensor.transpose(ps_z[:, BANK + k * P:BANK + (k + 1) * P], kv[:, k, :], ident)
                    nc.tensor.transpose(ps_z[0:B_ROPE, BANK + KV * P:BANK + (KV + 1) * P], lat[b][:, ROPE_AT:B_IN],
                                        ident).then_inc(lat_full, 1)

                pe.sem_inc(projected, 2)
                pe.sem_inc(lat_full, 2)
                skewed(pe, turn, project, turn_latents)

            @block.scalar
            def _(act):
                act.sem_inc(xT_a, 2)
                act.sem_inc(c_scaled, 1)
                act.sem_inc(z_read_a, 1)
                act.wait_ge(m_ready, 1)

                def modulate(i, b, s):
                    t = 2 * i + b
                    act.wait_ge(turned, t + 1)
                    act.wait_ge(projected, t + 1)
                    for k in range(KD // 2):
                        last = nc.scalar.activation(xT[b][:, k, :], ps_x[b][:, k * P:(k + 1) * P], ACT.Identity,
                                                    bias=shift[:, s, k:k + 1], scale=scale1[:, s, k:k + 1])
                    last.then_inc(xT_a, 1)

                def scale_latents(i, b, s):
                    t = 2 * i + b
                    act.wait_ge(projected, t + 3)
                    act.wait_ge(c_read, t + 1)
                    if s == 0:
                        nc.scalar.activation(squares[0][:, 0:B_QR], ps_c[:, 0:B_QR], ACT.Square, accum_out=sums[:, b, 0:1])
                    act.wait_ge(chain, CHAIN * t + 1)
                    nc.scalar.activation(squares[1][:, 0:B_KVR], ps_c[:, B_QR:ROPE_AT], ACT.Square,
                                         accum_out=sums[:, b, 1:2]).then_inc(squared, 1)
                    act.wait_ge(chain, CHAIN * t + 3)
                    nc.scalar.activation(root[:, b, s:2], mean[:, b, s:2], ACT.Sqrt).then_inc(rooted, 1)
                    act.wait_ge(chain, CHAIN * t + 4)
                    act.wait_ge(lat_full, t + 1)
                    nc.scalar.activation(lat[b][:, B_QR:ROPE_AT], ps_c[:, B_QR:ROPE_AT], ACT.Copy,
                                         scale=rstd[:, b, 1:2]).then_inc(c_scaled, 1)

                def gain(i, b, s):
                    t = 2 * i + b
                    act.wait_ge(lat_full, t + 3)
                    if s == 0:
                        for k in range(KQ):
                            last = nc.scalar.activation(cqT[:, k, bass.ds(t * P, P)], ps_z[:, k * P:(k + 1) * P], ACT.Copy,
                                                        scale=q_gain[:, k:k + 1])
                        last.then_inc(z_read_a, 1)
                    else:
                        act.sem_inc(z_read_a, 1)

                skewed(act, modulate, scale_latents, gain)

            @block.vector
            def _(dve):
                dve.sem_inc(xT_v, 2)
                dve.sem_inc(c_read, 1)
                dve.sem_inc(z_read_v, 1)
                dve.wait_ge(m_in, 96)
                nc.vector.tensor_scalar(scale1[:, :, :], scale[:, :, :], 1.0, None, ALU.add).then_inc(m_ready, 1)
                dve.wait_ge(m_ready, 1)

                def modulate(i, b, s):
                    t = 2 * i + b
                    dve.wait_ge(turned, t + 1)
                    dve.wait_ge(projected, t + 1)
                    for k in range(KD // 2, KD):
                        last = nc.vector.tensor_scalar(xT[b][:, k, :], ps_x[b][:, k * P:(k + 1) * P],
                                                       scale1[:, s, k:k + 1], shift[:, s, k:k + 1], ALU.mult, ALU.add)
                    last.then_inc(xT_v, 1)

                def scale_latents(i, b, s):
                    t = 2 * i + b
                    own = Chain(dve, chain, CHAIN * t)
                    rope = ps_c[:, ROPE_AT:B_IN]
                    dve.wait_ge(projected, t + 3)
                    dve.wait_ge(lat_full, t + 1)
                    if s == 0:
                        halves = lambda ap: ap.rearrange("p (a h j) -> p a h j", a=2, h=2)
                        tk = bass.ds(t * B_ROPE, B_ROPE)
                        r, sn, o = halves(rope), halves(const("sin_k")[:, tk]), halves(ksin[:, :])
                        nc.vector.tensor_tensor(o[:, :, 0, :], r[:, :, 1, :], sn[:, :, 0, :], ALU.mult)
                        nc.vector.tensor_tensor(o[:, :, 1, :], r[:, :, 0, :], sn[:, :, 1, :], ALU.mult)
                        own.link(nc.vector.tensor_tensor(kcos[:, :], rope, const("cos_k")[:, tk], ALU.mult))
                        own.link(nc.vector.tensor_tensor(lat[b][:, ROPE_AT:B_IN], kcos[:, :], ksin[:, :], ALU.add))
                    else:
                        own.link(nc.vector.tensor_copy(lat[b][:, ROPE_AT:B_IN], rope))
                        dve.sem_inc(chain, 1)
                        own.n += 1
                    dve.wait_ge(squared, t + 1)
                    if s == 0:
                        nc.vector.tensor_scalar(mean[:, b, 0:1], sums[:, b, 0:1], 1.0 / B_QR, RMS_EPS, ALU.mult, ALU.add)
                    own.link(nc.vector.tensor_scalar(mean[:, b, 1:2], sums[:, b, 1:2], 1.0 / B_KVR, RMS_EPS, ALU.mult, ALU.add))
                    lo = 0 if s == 0 else 1
                    dve.wait_ge(rooted, t + 1)
                    own.link(nc.vector.reciprocal(rstd[:, b, lo:2], root[:, b, lo:2]))
                    if s == 0:
                        nc.vector.tensor_scalar(lat[b][:, 0:B_QR], ps_c[:, 0:B_QR], rstd[:, b, 0:1], None, ALU.mult).then_inc(c_read, 1)
                    else:
                        dve.sem_inc(c_read, 1)
                    assert own.n == CHAIN

                def gain(i, b, s):
                    t = 2 * i + b
                    dve.wait_ge(lat_full, t + 3)
                    for k in range(KV):
                        nc.vector.tensor_scalar(ckvT[:, k, bass.ds(t * P, P)], ps_z[:, BANK + k * P:BANK + (k + 1) * P],
                                                kv_gain[:, k:k + 1], None, ALU.mult)
                    for copy in kT:
                        last = nc.vector.tensor_copy(copy[B_NOPE:B_QD, bass.ds(t * P, P)],
                                                     ps_z[0:B_ROPE, BANK + KV * P:BANK + (KV + 1) * P])
                    last.then_inc(z_read_v, 1)

                skewed(dve, modulate, scale_latents, gain)


def stage_latent_attention(nc, io, dr, const, cqT, ckvT, kT):
    UN, CH = 8, NT_ALL
    KQ, KV = B_QR // P, B_KVR // P
    VW = B_V + 1
    with Stage(nc, "mla") as st:
        wq, wk = st.sb("wq", [P, KQ, B_QD]), st.sb("wk", [P, KV, B_NOPE])
        wv = [st.sb(f"wv{n}", [P, KV, BANK]) for n in range(2)]
        v_all = st.sb("v_all", [P, NT_ALL, B_HEADS, VW])
        o_all = st.sb("o_all", [P, NT_X, B_HEADS * B_V])
        q_raw, q_cos, q_sin = (st.sb(n, [B_QD, SEQ]) for n in ("q_raw", "q_cos", "q_sin"))
        qT = [st.sb(f"qT{b}", [B_QD + 1, SEQ]) for b in range(2)]
        q_round, k_round = st.sb("q_round", [B_QD, SEQ], F32R), st.sb("k_round", [B_QD, TALL], F32R)
        probs = [st.sb(f"probs{b}", [P, CH, BANK]) for b in range(2)]
        top, inv = st.sb("top", [P, UN]), st.sb("inv", [P, 4])
        ps_a = st.ps("a", [P, 3 * BANK])
        ps_b = [st.ps(f"b{n}", [P, BANK]) for n in range(2)]
        ps_o, ps_m = st.ps("o", [P, BANK]), st.ps("m", [P, BANK])
        wv_in = st.sems("wv_in", 2)
        w_in, ones_ready, v_full, v_read = (st.sem(n) for n in ("w_in", "ones_ready", "v_full", "v_read"))
        q_full, k_full, rot_full, q_copied, k_copied, sin_ready, cos_ready, q_ready, rounded = (
            st.sem(n) for n in ("q_full", "k_full", "rot_full", "q_copied", "k_copied", "sin_ready", "cos_ready", "q_ready", "rounded"))
        scored, max_ready, row_full, row_ready, key_scored, exp_done, pv_full, inv_ready, out_done, stored = (
            st.sem(n) for n in ("scored", "max_ready", "row_full", "row_ready", "key_scored", "exp_done", "pv_full", "inv_ready", "out_done", "stored"))
        ident = const("ident")
        cos, sin, rot = const("cos_b")[0:B_QD, :], const("sin_b")[0:B_QD, :], const("rot_b")[0:B_QD, :]
        ukv = io["mla_w_ukv"][0].rearrange("(p k) (h e) -> p k h e", k=KV, e=B_NOPE + B_V)
        ukv_flat = io["mla_w_ukv"][0].rearrange("(p k) n -> p k n", k=KV)
        uq = io["mla_w_uq"][0].rearrange("(p k) n -> p k n", k=KQ)
        HV = BANK // B_V
        a_bank = lambda n: ps_a[:, n * BANK:(n + 1) * BANK]

        def heads(eng, head):
            with eng.Fori(0, B_HEADS // 2 - 1) as i:
                for b in range(2):
                    head(2 * i + b, b, False)
            for b in range(2):
                head(B_HEADS - 2 + b, b, b == 1)

        first = lambda h: isinstance(h, int) and h == 0

        with nc.Block() as block:

            @block.sync
            def _(sp):
                def load(h):
                    sp.dma_start(wq[:, :, :], uq[:, :, bass.ds(h * B_QD, B_QD)]).then_inc(w_in, 16)
                    sp.dma_start(wk[:, :, :], ukv_flat[:, :, bass.ds(h * (B_NOPE + B_V), B_NOPE)]).then_inc(w_in, 16)

                for n in range(2):
                    for k in range(KV):
                        sp.dma_start(wv[n][:, k, :].rearrange("p (h e) -> p h e", e=B_V),
                                     ukv[:, k, n * HV:(n + 1) * HV, B_NOPE:]).then_inc(wv_in[n], 16)
                load(0)
                with sp.Fori(1, B_HEADS) as h:
                    sp.wait_ge(k_full, 3 * h)
                    load(h)
                for lo, hi in ((0, B_HEADS - 2), (B_HEADS - 2, B_HEADS)):
                    sp.wait_ge(out_done, 2 * hi)
                    cols = slice(lo * B_V, hi * B_V)
                    for t in range(NT_X):
                        sp.dma_start(dr["o"][t * P:(t + 1) * P, cols], o_all[:, t, cols]).then_inc(stored, 16)
                sp.wait_ge(stored, 2 * 16 * NT_X)

            @block.gpsimd
            def _(pool):
                nc.gpsimd.memset(v_all[:, :, :, B_V:VW].rearrange("p t h e -> p (t h e)"), 1.0).then_inc(ones_ready, 1)
                for b in range(2):
                    pool.wait_ge(ones_ready, b + 1)
                    nc.gpsimd.memset(kT[b][B_QD:B_QD + 1, :], 1.0).then_inc(ones_ready, 1)
                pool.wait_ge(ones_ready, 3)

                def times_cos(h):
                    pool.wait_ge(q_copied, 2 * h + 2)
                    if not first(h):
                        pool.wait_ge(q_ready, h)
                    nc.gpsimd.tensor_tensor(q_cos[:, :], q_raw[:, :], cos, ALU.mult).then_inc(cos_ready, 1)

                def round_k(h, b):
                    pool.wait_ge(k_copied, 3 * h + 3)
                    if not first(h):
                        pool.wait_ge(scored, UN * h)
                    st.settle(pool)
                    nc.gpsimd.tensor_copy(k_round[:, :], kT[b][0:B_QD, :]).then_inc(rounded, 1)

                def round_q(h, b):
                    pool.wait_ge(q_ready, h + 1)
                    st.settle(pool)
                    nc.gpsimd.tensor_copy(q_round[:, :], qT[b][0:B_QD, :]).then_inc(rounded, 1)

                def prepare(h, b):
                    times_cos(h)
                    round_k(h, b)
                    round_q(h, b)

                prepare(0, 0)
                heads(pool, lambda h, b, last: None if last else prepare(h + 1, 1 - b))

            @block.tensor
            def _(pe):
                pe.wait_ge(ones_ready, 3)
                for n in range(2):
                    pe.wait_ge(wv_in[n], 16 * KV)
                    for t in range(NT_ALL):
                        u = n * NT_ALL + t
                        if u >= 3:
                            pe.wait_ge(v_read, u - 2)
                        for k in range(KV):
                            last = nc.tensor.matmul(a_bank(u % 3), ckvT[:, k, t * P:(t + 1) * P], wv[n][:, k, :],
                                                    start=(k == 0), stop=(k == KV - 1))
                        last.then_inc(v_full, 1)
                pe.wait_ge(v_read, 2 * NT_ALL)

                def project(h):
                    if not first(h):
                        pe.wait_ge(max_ready, UN * h)
                    pe.wait_ge(w_in, 32 * h + 32)
                    for n in range(2):
                        for k in range(KQ):
                            last = nc.tensor.matmul(a_bank(n)[0:B_QD, :], wq[:, k, :], cqT[:, k, n * BANK:(n + 1) * BANK],
                                                    start=(k == 0), stop=(k == KQ - 1))
                        last.then_inc(q_full, 1)
                    for n, (at, size) in enumerate(N_CUTS):
                        if n:
                            pe.wait_ge(q_copied, 2 * h + n)
                        for k in range(KV):
                            last = nc.tensor.matmul(a_bank((2 + n) % 3)[0:B_NOPE, 0:size], wk[:, k, :], ckvT[:, k, at:at + size],
                                                    start=(k == 0), stop=(k == KV - 1))
                        last.then_inc(k_full, 1)
                    for n in range(2):
                        pe.wait_ge(q_copied, 2 * h + n + 1)
                        pe.wait_ge(k_copied, 3 * h + n + 1)
                        nc.tensor.matmul(a_bank((2 + n) % 3)[0:B_QD, :], rot, q_raw[:, n * BANK:(n + 1) * BANK],
                                         start=True, stop=True).then_inc(rot_full, 1)

                def unit(h, u):
                    if u == 0:
                        pe.wait_ge(rounded, 2 * h + 2)
                        pe.wait_ge(k_copied, 3 * h + 3)
                        pe.wait_ge(sin_ready, 2 * h + 2)
                    else:
                        pe.wait_ge(max_ready, UN * h + u)
                    for at, size in N_CUTS:
                        last = nc.tensor.matmul(ps_a[:, at:at + size], q_round[:, u * P:(u + 1) * P], k_round[:, at:at + size],
                                                start=True, stop=True)
                    last.then_inc(scored, 1)

                def row(h, u):
                    pe.wait_ge(max_ready, UN * h + u + 1)
                    if u % 4 == 0 and not (first(h) and u == 0):
                        pe.wait_ge(row_ready, 2 * h + u // 4)
                    last = nc.tensor.transpose(ps_m[0:1, (u % 4) * P:(u % 4 + 1) * P], top[:, u:u + 1], ident)
                    if u % 4 == 3:
                        last.then_inc(row_full, 1)

                def chunk(h, b, half, c):
                    n = 2 * CH * h + CH * half + c
                    if c == 0:
                        pe.wait_ge(row_ready, 2 * h + half + 1)
                    if not (first(h) and half == 0 and c < 2):
                        pe.wait_ge(exp_done, n - 1)
                    nc.tensor.matmul(ps_b[c % 2][:, :], kT[b][:, c * P:(c + 1) * P], qT[b][:, half * BANK:(half + 1) * BANK],
                                     start=True, stop=True).then_inc(key_scored, 1)

                def mix(h, half, s):
                    if s == 0:
                        pe.wait_ge(exp_done, CH * (2 * h + half + 1))
                        if not (first(h) and half == 0):
                            pe.wait_ge(out_done, 2 * h + half)
                    for c in range(CH):
                        last = nc.tensor.matmul(ps_o[:, s * VW:(s + 1) * VW], probs[half][:, c, s * P:(s + 1) * P],
                                                v_all[:, c, bass.ds(h, 1), :].rearrange("p h e -> p (h e)"),
                                                start=(c == 0), stop=(c == CH - 1))
                    if s == 3:
                        last.then_inc(pv_full, 1)

                def head(h, b, last):
                    before = None if first(h) else (h - 1, 1)
                    between = {0: [(unit, h, 4)], 1: [(mix, 0)], 2: [(unit, h, 5), (row, h, 4)], 3: [(mix, 1)],
                               4: [(unit, h, 6), (row, h, 5)], 5: [(mix, 2)], 6: [(unit, h, 7), (row, h, 6)], 7: [(mix, 3)],
                               8: [(row, h, 7)]}
                    for c in range(CH):
                        chunk(h, b, 0, c)
                        for what, *where in between.get(c, ()):
                            if what is not mix:
                                what(*where)
                            elif before:
                                mix(*before, *where)
                    if not last:
                        project(h + 1)
                    nxt = h + 1
                    between = {0: [(mix, 0)], 1: [(mix, 1)], 2: [(unit, nxt, 0)], 3: [(mix, 2), (unit, nxt, 1), (row, nxt, 0)],
                               5: [(unit, nxt, 2), (row, nxt, 1)], 6: [(mix, 3), (unit, nxt, 3), (row, nxt, 2)], 8: [(row, nxt, 3)]}
                    for c in range(CH):
                        chunk(h, b, 1, c)
                        for what, *where in between.get(c, ()):
                            if what is mix:
                                mix(h, 0, *where)
                            elif not last:
                                what(*where)

                project(0)
                for u in range(4):
                    unit(0, u)
                    row(0, u)
                for b in range(2):
                    head(b, b, False)
                with pe.Fori(1, B_HEADS // 2 - 1) as i:
                    for b in range(2):
                        head(2 * i + b, b, False)
                for b in range(2):
                    head(B_HEADS - 2 + b, b, b == 1)
                for s in range(4):
                    mix(B_HEADS - 1, 1, s)

            @block.scalar
            def _(act):
                for n in range(2):
                    for t in range(NT_ALL):
                        u = n * NT_ALL + t
                        act.wait_ge(v_full, u + 1)
                        nc.scalar.activation(v_all[:, t, n * HV:(n + 1) * HV, 0:B_V], a_bank(u % 3).rearrange("p (h e) -> p h e", e=B_V),
                                             ACT.Copy).then_inc(v_read, 1)

                def copies(h, b):
                    if not first(h):
                        act.wait_ge(q_ready, h)
                    for n in range(2):
                        act.wait_ge(q_full, 2 * h + n + 1)
                        nc.scalar.activation(q_raw[:, n * BANK:(n + 1) * BANK], a_bank(n)[0:B_QD, :], ACT.Copy).then_inc(q_copied, 1)
                    for n, (at, size) in enumerate(N_CUTS):
                        act.wait_ge(k_full, 3 * h + n + 1)
                        nc.scalar.activation(kT[b][0:B_NOPE, at:at + size], a_bank((2 + n) % 3)[0:B_NOPE, 0:size],
                                             ACT.Copy).then_inc(k_copied, 1)

                def exps(h, half):
                    for c in range(CH):
                        act.wait_ge(key_scored, CH * (2 * h + half) + c + 1)
                        nc.scalar.activation(probs[half][:, c, :], ps_b[c % 2][:, :], ACT.Exp, scale=B_SCALE).then_inc(exp_done, 1)

                def head(h, b, last):
                    exps(h, 0)
                    if not last:
                        copies(h + 1, 1 - b)
                    exps(h, 1)

                copies(0, 0)
                heads(act, head)

            @block.vector
            def _(dve):
                def rotate(h, b):
                    for n in range(2):
                        dve.wait_ge(rot_full, 2 * h + n + 1)
                        nc.vector.tensor_tensor(q_sin[:, n * BANK:(n + 1) * BANK], a_bank((2 + n) % 3)[0:B_QD, :],
                                                sin[:, n * BANK:(n + 1) * BANK], ALU.mult).then_inc(sin_ready, 1)
                    dve.wait_ge(sin_ready, 2 * h + 2)
                    dve.wait_ge(cos_ready, h + 1)
                    nc.vector.tensor_tensor(qT[b][0:B_QD, :], q_cos[:, :], q_sin[:, :], ALU.add).then_inc(q_ready, 1)

                def maximum(h, u):
                    dve.wait_ge(scored, UN * h + u + 1)
                    nc.vector.tensor_reduce(top[:, u:u + 1], ps_a[:, 0:TALL], AX, ALU.max).then_inc(max_ready, 1)

                def row(h, b, half):
                    dve.wait_ge(row_full, 2 * h + half + 1)
                    nc.vector.tensor_scalar(qT[b][B_QD:B_QD + 1, half * BANK:(half + 1) * BANK], ps_m[0:1, :], -1.0, None,
                                            ALU.mult).then_inc(row_ready, 1)

                def finish(h, half):
                    n = 2 * h + half
                    sums = ps_o[:, 0:4 * VW].rearrange("p (s e) -> p s e", e=VW)
                    dve.wait_ge(pv_full, n + 1)
                    nc.vector.reciprocal(inv[:, :], sums[:, :, B_V]).then_inc(inv_ready, 1)
                    dve.wait_ge(inv_ready, n + 1)
                    nc.vector.tensor_tensor(o_all[:, half * 4:half * 4 + 4, bass.ds(h * B_V, B_V)], sums[:, :, 0:B_V],
                                            bcast_last(inv[:, :], B_V), ALU.mult).then_inc(out_done, 1)

                def head(h, b, last):
                    for u in range(4, 8):
                        maximum(h, u)
                    if not first(h):
                        finish(h - 1, 1)
                    row(h, b, 1)
                    if not last:
                        rotate(h + 1, 1 - b)
                        for u in range(4):
                            maximum(h + 1, u)
                        row(h + 1, 1 - b, 0)
                    finish(h, 0)

                rotate(0, 0)
                for u in range(4):
                    maximum(0, u)
                row(0, 0, 0)
                for b in range(2):
                    head(b, b, False)
                with dve.Fori(1, B_HEADS // 2 - 1) as i:
                    for b in range(2):
                        head(2 * i + b, b, False)
                for b in range(2):
                    head(B_HEADS - 2 + b, b, b == 1)
                finish(B_HEADS - 1, 1)


def load_rows(sp, sem, pairs):
    for tile, row in pairs:
        sp.dma_start(tile, row.partition_broadcast(P)).then_inc(sem, 16)
    return 16 * len(pairs)


def stage_project_out(nc, io, dr, const, layer, w_out, tiles, logits):
    with Stage(nc, f"out{layer}") as st:
        w, wr = st.sb("w", [P, KD, D]), st.sb("wr", [P, KD, ROUTE])
        r_bias = st.sb("r_bias", [P, ROUTE])
        kinds = 2 if tiles > NT_X else 1
        gate, scale, shift = ([st.sb(f"{n}{s}", [P, D]) for s in range(kinds)] for n in ("gate", "scale", "shift"))
        ln_g, ln_b = st.sb("ln_g", [P, D]), st.sb("ln_b", [P, D])
        o, x = ([st.sb(f"{n}{b}", [P, D]) for b in range(2)] for n in ("o", "x"))
        oT, hT = st.sb("oT", [P, KD, P]), st.sb("hT", [P, KD, P])
        gated, res, xn, xg, hs = (st.sb(n, [P, D]) for n in ("gated", "res", "xn", "xg", "hs"))
        xo, h = ([st.sb(f"{n}{b}", [P, D]) for b in range(2)] for n in ("xo", "h"))
        stats, mv, var, rstd, bias = st.sb("stats", [P, 2, 6]), st.sb("mv", [P, 2]), st.sb("var", [P, 1]), st.sb("rstd", [P, 1]), st.sb("bias", [P, 1])
        root = st.sb("root", [P, 1])
        ps_o, ps_y, ps_h = (st.ps(n, [P, 2 * BANK]) for n in ("o", "y", "h"))
        ps_r = st.ps("r", [P, BANK])
        o_in, x_in, x_stored, h_stored = (st.sems(n, 2) for n in ("o_in", "x_in", "x_stored", "h_stored"))
        w_in, wr_in = st.sems("w_in", 2), st.sem("wr_in")
        rows_in, scale_ready, o_turned, o_read, y_full, h_turned, h_read, routed = (
            st.sem(n) for n in ("rows_in", "scale_ready", "o_turned", "o_read", "y_full", "h_turned", "h_read", "routed"))
        chain, rooted, normed, x_ready, hs_ready, h_ready, logit_done = (
            st.sem(n) for n in ("chain", "rooted", "normed", "x_ready", "hs_ready", "h_ready", "logit_done"))
        ident = const("ident")
        STEPS = 9
        mod = lambda s, part: dr["mod"][layer, s, part * D:(part + 1) * D]

        def each(eng, first, second=None):
            pairs = NT_X // 2
            seq = lambda i, b, s: first(i, b, s)
            sec = second or (lambda i, b, s: None)
            seq(0, 0, 0)
            seq(0, 1, 0)
            sec(0, 0, 0)
            with eng.Fori(1, pairs) as i:
                seq(i, 0, 0)
                sec(i - 1, 1, 0)
                seq(i, 1, 0)
                sec(i, 0, 0)
            if kinds == 2:
                seq(pairs, 0, 1)
                sec(pairs - 1, 1, 0)
                seq(pairs, 1, 1)
                sec(pairs, 0, 1)
                sec(pairs, 1, 1)
            else:
                sec(pairs - 1, 1, 0)

        with nc.Block() as block:

            @block.sync
            def _(sp):
                def load(i, b):
                    t = bass.ds((i * 2 + b) * P, P)
                    sp.dma_start(o[b][:, :], dr["o"][t, :]).then_inc(o_in[b], 16)
                    sp.dma_start(x[b][:, :], dr["x"][t, :]).then_inc(x_in[b], 16)

                def store(i, b):
                    t = bass.ds((i * 2 + b) * P, P)
                    sp.wait_ge(x_ready, 2 * i + b + 1)
                    sp.dma_start(dr["x"][t, :], xo[b][:, :]).then_inc(x_stored[b], 16)
                    sp.wait_ge(h_ready, 2 * i + b + 1)
                    sp.dma_start(dr["h"][t, :], h[b][:, :]).then_inc(h_stored[b], 16)

                for b in range(2):
                    sp.sem_inc(x_stored[b], 16)
                    sp.sem_inc(h_stored[b], 16)
                    load(0, b)
                for n in range(2):
                    at = slice(n * BANK, (n + 1) * BANK)
                    sp.dma_start(w[:, :, at], w_out.rearrange("(p k) n -> p k n", k=KD)[:, :, at]).then_inc(w_in[n], 16)
                pairs = [(ln_g[:, :], io["ln_mix_g"][layer]), (ln_b[:, :], io["ln_mix_b"][layer]),
                         (r_bias[:, 0:NG], io["moe_b_grp"][layer]), (r_bias[:, NG:], io["moe_b_rt"][layer])]
                for s in range(kinds):
                    pairs += [(gate[s][:, :], mod(s, 2)), (shift[s][:, :], mod(s, 3)), (scale[s][:, :], mod(s, 4))]
                load_rows(sp, rows_in, pairs)
                sp.dma_start(wr[:, :, 0:NG], io["moe_w_grp"][layer].rearrange("(p k) n -> p k n", k=KD)).then_inc(wr_in, 16)
                sp.dma_start(wr[:, :, NG:], io["moe_w_rt"][layer].rearrange("(p k) n -> p k n", k=KD)).then_inc(wr_in, 16)
                with sp.Fori(1, tiles // 2) as i:
                    for b in range(2):
                        sp.wait_ge(chain, STEPS * (2 * i + b - 2) + 2)
                        load(i, b)
                        store(i - 1, b)
                for b in range(2):
                    store(tiles // 2 - 1, b)
                for b in range(2):
                    sp.wait_ge(x_stored[b], 16 * (tiles // 2) + 16)
                    sp.wait_ge(h_stored[b], 16 * (tiles // 2) + 16)

            ROWS_IN = 16 * (4 + 3 * kinds)

            @block.tensor
            def _(pe):
                pe.sem_inc(y_full, 1)
                pe.sem_inc(routed, 1)

                def project(i, b, s):
                    t = 2 * i + b
                    pe.wait_ge(o_in[b], 16 * i + 16)
                    pe.wait_ge(o_read, t + 1)
                    rows = o[b][:, :].rearrange("t (p k) -> t k p", k=KD)
                    for k in range(KD):
                        last = nc.tensor.transpose(ps_o[:, k * P:(k + 1) * P], rows[:, k, :], ident)
                    last.then_inc(o_turned, 1)
                    pe.wait_ge(o_read, t + 2)
                    if not (isinstance(i, int) and t == 0):
                        pe.wait_ge(chain, STEPS * t - (STEPS - 1))
                    for n in range(2):
                        if isinstance(i, int) and t == 0:
                            pe.wait_ge(w_in[n], 16)
                        for k in range(KD):
                            last = nc.tensor.matmul(ps_y[:, n * BANK:(n + 1) * BANK], oT[:, k, :], w[:, k, n * BANK:(n + 1) * BANK],
                                                    start=(k == 0), stop=(k == KD - 1))
                    last.then_inc(y_full, 1)

                def route(i, b, s):
                    t = 2 * i + b
                    pe.wait_ge(h_ready, t + 1)
                    pe.wait_ge(h_read, t + 1)
                    rows = h[b][:, :].rearrange("t (p k) -> t k p", k=KD)
                    for k in range(KD):
                        last = nc.tensor.transpose(ps_h[:, k * P:(k + 1) * P], rows[:, k, :], ident)
                    last.then_inc(h_turned, 1)
                    pe.wait_ge(h_read, t + 2)
                    pe.wait_ge(logit_done, t + 1)
                    if isinstance(i, int) and t == 0:
                        pe.wait_ge(wr_in, 32)
                    for k in range(KD):
                        last = nc.tensor.matmul(ps_r[:, 0:ROUTE], hT[:, k, :], wr[:, k, :], start=(k == 0), stop=(k == KD - 1))
                    last.then_inc(routed, 1)

                each(pe, project, route)

            @block.scalar
            def _(act):
                act.sem_inc(o_read, 1)
                act.sem_inc(h_read, 1)

                def first(i, b, s):
                    t = 2 * i + b
                    act.wait_ge(o_turned, t + 1)
                    act.wait_ge(y_full, t + 1)
                    nc.scalar.activation(oT[:, :, :].rearrange("p k t -> p (k t)"), ps_o[:, :], ACT.Copy).then_inc(o_read, 1)

                def norm(i, b, s):
                    t = 2 * i + b
                    act.wait_ge(chain, STEPS * t + 6)
                    nc.scalar.activation(root[:, :], var[:, :], ACT.Sqrt).then_inc(rooted, 1)
                    act.wait_ge(chain, STEPS * t + 8)
                    nc.scalar.activation(xn[:, :], res[:, :], ACT.Identity, bias=bias[:, :], scale=rstd[:, :]).then_inc(normed, 1)
                    act.wait_ge(h_turned, t + 1)
                    act.wait_ge(routed, t + 1)
                    nc.scalar.activation(hT[:, :, :].rearrange("p k t -> p (k t)"), ps_h[:, :], ACT.Copy).then_inc(h_read, 1)

                each(act, first, norm)

            @block.vector
            def _(dve):
                dve.sem_inc(logit_done, 1)
                dve.wait_ge(rows_in, ROWS_IN)
                for s in range(kinds):
                    last = nc.vector.tensor_scalar(scale[s][:, :], scale[s][:, :], 1.0, None, ALU.add)
                last.then_inc(scale_ready, 1)
                dve.wait_ge(scale_ready, 1)

                def update(i, b, s):
                    t = 2 * i + b
                    own = Chain(dve, chain, STEPS * t)
                    dve.wait_ge(y_full, t + 2)
                    own.link(nc.vector.tensor_tensor(gated[:, :], ps_y[:, :], gate[s][:, :], ALU.mult))
                    dve.wait_ge(x_in[b], 16 * i + 16)
                    own.link(nc.vector.scalar_tensor_tensor(res[:, :], x[b][:, :], ALPHA, gated[:, :], ALU.mult, ALU.add))
                    for n in range(2):
                        own.inc(nc.vector.bn_stats(stats[:, n, :], res[:, n * BANK:(n + 1) * BANK]))
                    own.wait()
                    st.settle(dve)
                    own.link(nc.vector.bn_aggr(mv[:, :], stats[:, :, :].rearrange("p n s -> p (n s)")))
                    own.link(nc.vector.tensor_scalar(var[:, :], mv[:, 1:2], LN_EPS, None, ALU.add))
                    dve.wait_ge(rooted, t + 1)
                    own.link(nc.vector.reciprocal(rstd[:, :], root[:, :]))
                    own.link(nc.vector.tensor_scalar(bias[:, :], mv[:, 0:1], rstd[:, :], -1.0, ALU.mult, ALU.mult))
                    dve.wait_ge(normed, t + 1)
                    own.link(nc.vector.tensor_tensor(xg[:, :], xn[:, :], ln_g[:, :], ALU.mult))
                    dve.wait_ge(hs_ready, t + 1)
                    dve.wait_ge(h_stored[b], 16 * i + 16)
                    assert own.n == STEPS
                    nc.vector.tensor_tensor(h[b][:, :], hs[:, :], shift[s][:, :], ALU.add).then_inc(h_ready, 1)

                def logit(i, b, s):
                    t = 2 * i + b
                    dve.wait_ge(routed, t + 2)
                    nc.vector.tensor_tensor(logits[:, bass.ds(t * ROUTE, ROUTE)], ps_r[:, 0:ROUTE], r_bias[:, :], ALU.add).then_inc(logit_done, 1)

                each(dve, update, logit)

            @block.gpsimd
            def _(pool):
                pool.wait_ge(rows_in, ROWS_IN)
                pool.wait_ge(scale_ready, 1)

                def shift_norm(i, b, s):
                    t = 2 * i + b
                    pool.wait_ge(chain, STEPS * t + 9)
                    pool.wait_ge(x_stored[b], 16 * i + 16)
                    nc.gpsimd.tensor_tensor(xo[b][:, :], xg[:, :], ln_b[:, :], ALU.add).then_inc(x_ready, 1)
                    pool.wait_ge(x_ready, t + 1)
                    nc.gpsimd.tensor_tensor(hs[:, :], xo[b][:, :], scale[s][:, :], ALU.mult).then_inc(hs_ready, 1)

                each(pool, shift_norm)


def stage_route(nc, dr, const, layer, tiles, logits, weights, slots, block_info, tokens):
    nb = n_blocks(tiles)
    with Stage(nc, f"rt{layer}") as st:
        lg = logits[:, 0:tiles * ROUTE].rearrange("p (t r) -> p t r", r=ROUTE)
        l_grp, l_exp = lg[:, :, 0:NG], lg[:, :, NG:]
        t1 = lambda name, dt=F32: st.sb(name, [P, tiles], dt)
        tg = lambda name: st.sb(name, [P, tiles, NG])
        te = lambda name: st.sb(name, [P, tiles, NE])
        g_max, g_low, g_sum, g_prob = t1("g_max"), t1("g_low"), t1("g_sum"), t1("g_prob")
        g_diff, g_exp, g_hit, g_idx, g_one = tg("g_diff"), tg("g_exp"), tg("g_hit"), tg("g_idx"), tg("g_one")
        e_in, e_hit, e_idx, e_rest = te("e_in"), te("e_hit"), te("e_idx"), te("e_rest")
        e_max, e_low = [t1(f"e_max{k}") for k in range(2)], [t1(f"e_low{k}") for k in range(2)]
        one = [te(f"one{k}") for k in range(2)]
        both, seen = te("both"), st.sb("seen", [P, tiles + 1, NE])
        diff, ratio, denom, w_first = t1("diff"), t1("ratio"), t1("denom"), t1("w_first")
        counts, blocks, ends, starts = (st.sb(n, [P, NE]) for n in ("counts", "blocks", "ends", "starts"))
        over = st.sb("over", [P, NE, tiles])
        ranks, product = te("ranks"), te("product")
        rank, base, above, local, place, block_of = (t1(n) for n in ("rank", "base", "above", "local", "place", "block_of"))
        steps_over = st.sb("steps_over", [P, tiles, tiles])
        where = t1("where")
        table_at = [t1(f"table_at{k}", I32) for k in range(2)]
        passed, owner = st.sb("passed", [P, nb, NE]), st.sb("owner", [P, nb])
        token_id = t1("token_id", I32)
        zeros = st.sb("zeros", [P, nb], I32)
        ps = st.ps("ps", [P, BANK])
        ps_n = st.ps("ps_n", [P, BANK])
        own_sem, exp_ready, exped, both_ready, ranked, routed, zeroed = (
            st.sem(n) for n in ("own", "exp_ready", "exped", "both_ready", "ranked", "routed", "zeroed"))
        zero_in, scattered, read_back = (st.pool_dma_sem(n) for n in ("zero_in", "scattered", "read_back"))
        v = nc.vector
        with nc.Block() as block:

            @block.vector
            def _(dve):
                own = Chain(dve, own_sem)
                link = own.link
                iota_g, iota_e = bcast_mid(const("iota_g"), tiles), bcast_mid(const("iota_e"), tiles)
                link(v.tensor_reduce(g_max[:, :], l_grp, AX, ALU.max))
                v.tensor_tensor(g_diff[:, :, :], l_grp, bcast_last(g_max[:, :], NG), ALU.subtract).then_inc(exp_ready, 1)
                link(v.tensor_tensor(g_hit[:, :, :], l_grp, bcast_last(g_max[:, :], NG), ALU.is_equal))
                link(v.tensor_tensor(g_idx[:, :, :], g_hit[:, :, :], iota_g, ALU.mult))
                link(v.tensor_reduce(g_low[:, :], g_idx[:, :, :], AX, ALU.min))
                link(v.tensor_tensor(g_one[:, :, :], iota_g, bcast_last(g_low[:, :], NG), ALU.is_equal))
                link(v.tensor_scalar(g_idx[:, :, :], g_one[:, :, :], 1.0, BIG, ALU.subtract, ALU.mult))
                for g in range(NG):
                    own.inc(v.tensor_tensor(e_in[:, :, g * EPG:(g + 1) * EPG], l_exp[:, :, g * EPG:(g + 1) * EPG],
                                            g_idx[:, :, g:g + 1].broadcast_to([P, tiles, EPG]), ALU.add))
                own.wait()
                src = e_in
                for k in range(2):
                    link(v.tensor_reduce(e_max[k][:, :], src[:, :, :], AX, ALU.max))
                    link(v.tensor_tensor(e_hit[:, :, :], src[:, :, :], bcast_last(e_max[k][:, :], NE), ALU.is_equal))
                    link(v.tensor_tensor(e_idx[:, :, :], e_hit[:, :, :], iota_e, ALU.mult))
                    link(v.tensor_reduce(e_low[k][:, :], e_idx[:, :, :], AX, ALU.min))
                    link(v.tensor_tensor(one[k][:, :, :], iota_e, bcast_last(e_low[k][:, :], NE), ALU.is_equal))
                    if k == 0:
                        link(v.scalar_tensor_tensor(e_rest[:, :, :], one[0][:, :, :], -BIG, e_in[:, :, :], ALU.mult, ALU.add))
                        src = e_rest
                link(v.tensor_tensor(both[:, :, :], one[0][:, :, :], one[1][:, :, :], ALU.add))
                link(v.memset(seen[:, 0, :], 0.0))
                for t in range(tiles):
                    link(v.tensor_tensor(seen[:, t + 1, :], seen[:, t, :], both[:, t, :], ALU.add))
                dve.sem_inc(both_ready, 1)
                v.tensor_tensor(diff[:, :], e_max[1][:, :], e_max[0][:, :], ALU.subtract).then_inc(exp_ready, 1)
                dve.wait_ge(exped, 1)
                link(v.tensor_reduce(g_sum[:, :], g_exp[:, :, :], AX, ALU.add))
                link(v.reciprocal(g_prob[:, :], g_sum[:, :]))
                dve.wait_ge(exped, 2)
                link(v.tensor_scalar(denom[:, :], ratio[:, :], 1.0, None, ALU.add))
                link(v.reciprocal(w_first[:, :], denom[:, :]))
                link(v.tensor_tensor(weights[:, 0, 0:tiles], w_first[:, :], g_prob[:, :], ALU.mult))
                link(v.tensor_tensor(weights[:, 1, 0:tiles], weights[:, 0, 0:tiles], ratio[:, :], ALU.mult))
                dve.wait_ge(ranked, 1)
                link(v.tensor_copy(counts[:, :], ps_n[:, 0:NE]))
                link(v.tensor_tensor(over[:, :, :], bcast_last(counts[:, :], tiles), bcast_mid(const("steps")[:, 0:tiles], NE), ALU.is_gt))
                link(v.tensor_reduce(blocks[:, :], over[:, :, :], AX, ALU.add))
                link(v.tensor_tensor_scan(ends[:, :], const("ones")[:, 0:NE], blocks[:, :], 0.0, ALU.mult, ALU.add))
                link(v.tensor_tensor(starts[:, :], ends[:, :], blocks[:, :], ALU.subtract))
                link(v.tensor_copy(ranks[:, :, :].rearrange("p t e -> p (t e)"), ps[:, 0:tiles * NE]))
                for k in range(2):
                    link(v.tensor_tensor(product[:, :, :], ranks[:, :, :], one[k][:, :, :], ALU.mult))
                    link(v.tensor_reduce(rank[:, :], product[:, :, :], AX, ALU.add))
                    link(v.tensor_tensor(product[:, :, :], bcast_mid(starts[:, :], tiles), one[k][:, :, :], ALU.mult))
                    link(v.tensor_reduce(base[:, :], product[:, :, :], AX, ALU.add))
                    link(v.tensor_tensor(steps_over[:, :, 1:], bcast_last(rank[:, :], tiles - 1),
                                         bcast_mid(const("steps")[:, 1:tiles], tiles), ALU.is_ge))
                    link(v.tensor_reduce(above[:, :], steps_over[:, :, 1:], AX, ALU.add))
                    link(v.scalar_tensor_tensor(local[:, :], above[:, :], -float(P), rank[:, :], ALU.mult, ALU.add))
                    link(v.tensor_tensor(block_of[:, :], base[:, :], above[:, :], ALU.add))
                    link(v.scalar_tensor_tensor(place[:, :], block_of[:, :], float(P), local[:, :], ALU.mult, ALU.add))
                    link(v.tensor_copy(slots[:, k, 0:tiles], place[:, :]))
                    link(v.scalar_tensor_tensor(where[:, :], local[:, :], float(nb), block_of[:, :], ALU.mult, ALU.add))
                    link(v.tensor_copy(table_at[k][:, :], where[:, :]))
                link(v.tensor_copy(token_id[:, :], const("token")[:, 0:tiles]))
                dve.sem_inc(routed, 1)
                link(v.tensor_tensor(passed[:, :, :], bcast_mid(ends[:, :], nb), bcast_last(const("iota_b")[:, 0:nb], NE), ALU.is_le))
                link(v.tensor_reduce(owner[:, :], passed[:, :, :], AX, ALU.add))
                link(v.tensor_scalar(block_info[:, 0:nb], owner[:, :], float(NE - 1), None, ALU.min))
                link(v.tensor_copy(block_info[:, nb:nb + 1], ends[:, NE - 1:NE]))

            @block.scalar
            def _(act):
                act.wait_ge(exp_ready, 1)
                nc.scalar.activation(g_exp[:, :, :], g_diff[:, :, :], ACT.Exp).then_inc(exped, 1)
                act.wait_ge(exp_ready, 2)
                nc.scalar.activation(ratio[:, :], diff[:, :], ACT.Exp).then_inc(exped, 1)

            @block.tensor
            def _(pe):
                pe.wait_ge(both_ready, 1)
                flat = lambda ap: ap.rearrange("p t e -> p (t e)")
                nc.tensor.matmul(ps[:, 0:tiles * NE], const("before"), flat(both[:, :, :]), start=True, stop=False)
                nc.tensor.matmul(ps[:, 0:tiles * NE], const("ones"), flat(seen[:, 0:tiles, :]), start=False, stop=True)
                nc.tensor.matmul(ps_n[:, 0:NE], const("ones"), seen[:, tiles, :], start=True, stop=True).then_inc(ranked, 1)

            @block.gpsimd
            def _(pool):
                nc.gpsimd.memset(zeros[:, :], 0).then_inc(zeroed, 1)
                pool.wait_ge(zeroed, 1)
                table = dr["table"][0:P * nb, :]
                pool.dma_start(table.rearrange("(p b) one -> p (b one)", p=P), zeros[:, :]).then_inc(zero_in, 16)
                pool.wait_ge(zero_in, 16)
                pool.wait_ge(routed, 1)
                for t in range(tiles):
                    for k in range(2):
                        pool.indirect_dma_start(table, bass.IndirectOffsetOnAxis(table_at[k][:, t:t + 1], 0),
                                                token_id[:, t:t + 1], None).then_inc(scattered, 16)
                pool.wait_ge(scattered, 32 * tiles)
                pool.dma_start(tokens[:, 0:nb], table.rearrange("(p b) one -> p (b one)", p=P)).then_inc(read_back, 16)
                pool.wait_ge(read_back, 16)


def stage_experts(nc, io, dr, const, layer, tiles, block_info, tokens):
    nb = n_blocks(tiles)
    with Stage(nc, f"moe{layer}") as st:
        wg, wu, wd = st.sb("wg", [P, KD, DE]), st.sb("wu", [P, KD, DE]), st.sb("wd", [P, KE, D])
        wg_hi, wg_lo, wu_hi, wu_lo = (st.sb(n, [P, KD, DE], F32R) for n in ("wg_hi", "wg_lo", "wu_hi", "wu_lo"))
        wd_hi, wd_lo = (st.sb(n, [P, KE, D], F32R) for n in ("wd_hi", "wd_lo"))
        index = [st.sb(f"index{b}", [P, 1], I32) for b in range(2)]
        rows = [st.sb(f"rows{b}", [P, D]) for b in range(2)]
        xT_hi, xT_lo = ([st.sb(f"{n}{b}", [P, KD, P], F32R) for b in range(2)] for n in ("xT_hi", "xT_lo"))
        gate, act_up = ([st.sb(f"{n}{b}", [P, DE]) for b in range(2)] for n in ("gate", "act_up"))
        aT_hi, aT_lo = st.sb("aT_hi", [P, KE, P], F32R), st.sb("aT_lo", [P, KE, P], F32R)
        y = [st.sb(f"y{b}", [P, D]) for b in range(2)]
        ps_x = st.ps("x", [P, 2 * BANK])
        ps_g, ps_u, ps_a = (st.ps(n, [P, BANK]) for n in ("g", "u", "a"))
        ps_y = st.ps("y", [P, 2 * BANK])
        g_in, u_in, d_in, g_hi, u_hi, d_hi, g_split, u_split, d_split = (
            st.sem(n) for n in ("g_in", "u_in", "d_in", "g_hi", "u_hi", "d_hi", "g_split", "u_split", "d_split"))
        gathered = [st.pool_dma_sem(f"gathered{b}") for b in range(2)]
        stored = st.sem("stored")
        index_ready, turned, x_hi, x_split, gate_full, up_full, gated, multiplied, a_turned, a_hi, a_split, y_full, y_read_a, y_read_v = (
            st.sem(n) for n in ("index_ready", "turned", "x_hi", "x_split", "gate_full", "up_full", "gated", "multiplied", "a_turned",
                                "a_hi", "a_split", "y_full", "y_read_a", "y_read_v"))
        ident = const("ident")
        experts = lambda name: io[name][layer]
        flat = lambda tile: tile[:, :, :].rearrange("p k n -> p (k n)")

        def in_use(eng):
            return eng.value_load(block_info[0:1, nb:nb + 1], min_val=1, max_val=nb)

        def loads(eng, load):
            used = in_use(eng)
            load(0, 0, 0)
            load(1, 0, 1)
            with eng.Fori(1, nb // 2 + 1) as i:
                for b in range(2):
                    with eng.If(used > 2 * i + b):
                        load(2 * i + b, i, b)

        def steps(eng, start, step):
            used = in_use(eng)
            start()
            with eng.Fori(0, nb // 2) as i:
                for b in (1, 0):
                    n, half = (2 * i + 1, i) if b else (2 * i + 2, i + 1)
                    with eng.If(used > n + 1):
                        step(n, half, b, False)
                    with eng.If(used == n + 1):
                        step(n, half, b, True)
            return used

        with nc.Block() as block:

            @block.sync
            def _(sp):
                def load(n, tile, name, sem, split, k):
                    e = sp.value_load(block_info[0:1, bass.ds(n, 1)], min_val=0, max_val=NE - 1)
                    if not (isinstance(n, int) and n == 0):
                        sp.wait_ge(split, n)
                    sp.dma_start(tile[:, :, :], experts(name)[e].rearrange("(p k) n -> p k n", k=k)).then_inc(sem, 16)

                def load_gu(n):
                    load(n, wg, "moe_w_gate", g_in, g_split, KD)
                    load(n, wu, "moe_w_up", u_in, u_split, KD)

                load_d = lambda n: load(n, wd, "moe_w_down", d_in, d_split, KE)

                def start():
                    load_gu(0)
                    load_gu(1)
                    load_d(0)

                def step(n, i, b, last):
                    if not last:
                        load_gu(n + 1)
                    load_d(n)

                steps(sp, start, step)

            @block.gpsimd
            def _(pool):
                def gather(n, i, b):
                    if not isinstance(i, int):
                        pool.wait_ge(turned, n - 1)
                    nc.gpsimd.tensor_copy(index[b][:, :], tokens[:, bass.ds(n, 1)]).then_inc(index_ready, 1)
                    pool.wait_ge(index_ready, n + 1)
                    st.settle(pool)
                    pool.indirect_dma_start(rows[b][:, :], None, dr["h"], bass.IndirectOffsetOnAxis(index[b][:, :], 0)).then_inc(gathered[b], 16)

                loads(pool, gather)

            @block.tensor
            def _(pe):
                pe.sem_inc(y_full, 1)
                pe.sem_inc(a_turned, 1)

                def passes(out, chunks, hi, lo, w_hi, w_lo, at):
                    for k in range(chunks):
                        nc.tensor.matmul(out, hi[:, k, :], w_hi[:, k, at], start=(k == 0), stop=False)
                        nc.tensor.matmul(out, hi[:, k, :], w_lo[:, k, at], start=False, stop=False)
                        last = nc.tensor.matmul(out, lo[:, k, :], w_hi[:, k, at], start=False, stop=(k == chunks - 1))
                    return last

                def turn_x(n, i, b):
                    pe.wait_ge(gathered[b], 16 * i + 16)
                    pe.wait_ge(x_split, n + 1)
                    xs = rows[b][:, :].rearrange("t (p k) -> t k p", k=KD)
                    for k in range(KD):
                        last = nc.tensor.transpose(ps_x[:, k * P:(k + 1) * P], xs[:, k, :], ident)
                    last.then_inc(turned, 1)

                def gates(n, i, b):
                    pe.wait_ge(x_split, n + 2)
                    pe.wait_ge(g_split, n + 1)
                    pe.wait_ge(gated, n + 1)
                    last = passes(ps_g[:, :], KD, xT_hi[b], xT_lo[b], wg_hi, wg_lo, slice(0, DE))
                    last.then_inc(gate_full, 1)

                def ups(n, i, b):
                    pe.wait_ge(u_split, n + 1)
                    pe.wait_ge(multiplied, n + 1)
                    last = passes(ps_u[:, :], KD, xT_hi[b], xT_lo[b], wu_hi, wu_lo, slice(0, DE))
                    last.then_inc(up_full, 1)

                def turn_a(n, i, b):
                    pe.wait_ge(multiplied, n + 2)
                    pe.wait_ge(a_split, n + 1)
                    cols = act_up[b][:, :].rearrange("t (p k) -> t k p", k=KE)
                    for k in range(KE):
                        last = nc.tensor.transpose(ps_a[:, k * P:(k + 1) * P], cols[:, k, :], ident)
                    last.then_inc(a_turned, 1)

                def downs(n, i, b):
                    pe.wait_ge(a_split, n + 2)
                    pe.wait_ge(d_split, n + 1)
                    pe.wait_ge(y_read_a, n + 1)
                    pe.wait_ge(y_read_v, n + 1)
                    for c in range(2):
                        at = slice(c * BANK, (c + 1) * BANK)
                        last = passes(ps_y[:, at], KE, aT_hi, aT_lo, wd_hi, wd_lo, at)
                    last.then_inc(y_full, 1)

                def start():
                    turn_x(0, 0, 0)
                    gates(0, 0, 0)
                    ups(0, 0, 0)
                    turn_x(1, 0, 1)

                def step(n, i, b, last):
                    before = (n - 1, i if b else i - 1, 1 - b)
                    gates(n, i, b)
                    turn_a(*before)
                    ups(n, i, b)
                    if not last:
                        turn_x(n + 1, i + 1 if b else i, 1 - b)
                    downs(*before)
                    if last:
                        turn_a(n, i, b)
                        downs(n, i, b)

                steps(pe, start, step)

            @block.scalar
            def _(act):
                act.sem_inc(gated, 1)
                act.sem_inc(y_read_a, 1)
                act.sem_inc(stored, 16)

                def round_weight(n, tile, hi, loaded, used, count, ready):
                    if not (isinstance(n, int) and n == 0):
                        act.wait_ge(used, count)
                    act.wait_ge(loaded, 16 * n + 16)
                    nc.scalar.activation(flat(hi), flat(tile), ACT.Copy).then_inc(ready, 1)

                round_g = lambda n: round_weight(n, wg, wg_hi, g_in, gate_full, n, g_hi)
                round_u = lambda n: round_weight(n, wu, wu_hi, u_in, up_full, n, u_hi)
                round_d = lambda n: round_weight(n, wd, wd_hi, d_in, y_full, n + 1, d_hi)

                def round_x(n, b):
                    act.wait_ge(turned, n + 1)
                    if not isinstance(n, int):
                        act.wait_ge(up_full, n - 1)
                    nc.scalar.activation(flat(xT_hi[b]), ps_x[:, :], ACT.Copy).then_inc(x_hi, 1)

                def silu(n, b):
                    act.wait_ge(gate_full, n + 1)
                    if not isinstance(n, int):
                        act.wait_ge(multiplied, n)
                    nc.scalar.activation(gate[b][:, :], ps_g[:, :], ACT.Silu).then_inc(gated, 1)

                def round_a(n):
                    act.wait_ge(a_turned, n + 2)
                    act.wait_ge(y_full, n + 1)
                    nc.scalar.activation(flat(aT_hi), ps_a[:, :], ACT.Copy).then_inc(a_hi, 1)

                def finish(n, b):
                    act.wait_ge(y_full, n + 2)
                    act.wait_ge(stored, 16 * n + 16)
                    nc.scalar.activation(y[b][:, 0:BANK], ps_y[:, 0:BANK], ACT.Copy).then_inc(y_read_a, 1)
                    act.wait_ge(y_read_a, n + 2)
                    act.wait_ge(y_read_v, n + 2)
                    act.dma_start(dr["y"][bass.ds(n * P, P), :], y[b][:, :]).then_inc(stored, 16)

                def start():
                    round_x(0, 0)
                    round_g(0)
                    round_u(0)
                    silu(0, 0)
                    round_g(1)
                    round_x(1, 1)
                    round_u(1)
                    round_d(0)

                def step(n, i, b, last):
                    silu(n, b)
                    round_a(n - 1)
                    if not last:
                        round_g(n + 1)
                        round_x(n + 1, 1 - b)
                        round_u(n + 1)
                    finish(n - 1, 1 - b)
                    round_d(n)
                    if last:
                        round_a(n)
                        finish(n, b)

                used = steps(act, start, step)
                act.wait_ge(stored, 16 * used + 16)
                st.settle(act)

            @block.vector
            def _(dve):
                dve.sem_inc(x_split, 1)
                dve.sem_inc(a_split, 1)
                dve.sem_inc(multiplied, 1)
                dve.sem_inc(y_read_v, 1)

                def rest(n, lo, whole, hi, rounded, split):
                    dve.wait_ge(rounded, n + 1)
                    nc.vector.tensor_tensor(flat(lo), whole, flat(hi), ALU.subtract).then_inc(split, 1)

                rest_g = lambda n: rest(n, wg_lo, flat(wg), wg_hi, g_hi, g_split)
                rest_u = lambda n: rest(n, wu_lo, flat(wu), wu_hi, u_hi, u_split)
                rest_d = lambda n: rest(n, wd_lo, flat(wd), wd_hi, d_hi, d_split)
                rest_x = lambda n, b: rest(n, xT_lo[b], ps_x[:, :], xT_hi[b], x_hi, x_split)
                rest_a = lambda n: rest(n, aT_lo, ps_a[:, :], aT_hi, a_hi, a_split)

                def multiply(n, b):
                    dve.wait_ge(gated, n + 2)
                    dve.wait_ge(up_full, n + 1)
                    if not isinstance(n, int):
                        dve.wait_ge(a_turned, n)
                    nc.vector.tensor_tensor(act_up[b][:, :], gate[b][:, :], ps_u[:, :], ALU.mult).then_inc(multiplied, 1)

                def finish(n, b):
                    dve.wait_ge(y_full, n + 2)
                    dve.wait_ge(stored, 16 * n + 16)
                    nc.vector.tensor_copy(y[b][:, BANK:], ps_y[:, BANK:]).then_inc(y_read_v, 1)

                def start():
                    rest_x(0, 0)
                    rest_g(0)
                    rest_u(0)
                    rest_g(1)
                    multiply(0, 0)
                    rest_x(1, 1)
                    rest_u(1)
                    rest_d(0)

                def step(n, i, b, last):
                    rest_a(n - 1)
                    if not last:
                        rest_g(n + 1)
                    multiply(n, b)
                    if not last:
                        rest_x(n + 1, 1 - b)
                        rest_u(n + 1)
                    finish(n - 1, 1 - b)
                    rest_d(n)
                    if last:
                        rest_a(n)
                        finish(n, b)

                steps(dve, start, step)


def stage_combine(nc, io, dr, const, layer, tiles, weights, slots, out):
    with Stage(nc, f"mix{layer}") as st:
        kinds = 2 if tiles > NT_X else 1
        gate = [st.sb(f"gate{s}", [P, D]) for s in range(kinds)]
        ln_g, ln_b = st.sb("ln_g", [P, D]), st.sb("ln_b", [P, D])
        x, y1, y2, mixed, res, xn, xg, xo = ([st.sb(f"{n}{b}", [P, D]) for b in range(2)]
                                             for n in ("x", "y1_", "y2_", "mixed", "res", "xn", "xg", "xo"))
        both, gated = st.sb("both", [P, D]), st.sb("gated", [P, D])
        stats, mv, var, root, rstd, bias = ([st.sb(f"{n}{b}", shape) for b in range(2)] for n, shape in (
            ("stats", [P, 2, 6]), ("mv", [P, 2]), ("var", [P, 1]), ("root", [P, 1]), ("rstd", [P, 1]), ("bias", [P, 1])))
        x_in, stored = (st.sems(n, 2) for n in ("x_in", "stored"))
        y1_in, y2_in = ([st.pool_dma_sem(f"{n}_in{b}") for b in range(2)] for n in ("first", "second"))
        rows_in, weighed, summing, rooted, scaling, normed, x_ready = (
            st.sem(n) for n in ("rows_in", "weighed", "summing", "rooted", "scaling", "normed", "x_ready"))
        SUM, SCALE = 7, 3
        ROWS_IN = 16 * (2 + kinds)
        with nc.Block() as block:

            @block.sync
            def _(sp):
                load_rows(sp, rows_in, [(gate[s][:, :], dr["mod"][layer, s, 5 * D:6 * D]) for s in range(kinds)]
                          + [(ln_g[:, :], io["ln_ffn_g"][layer]), (ln_b[:, :], io["ln_ffn_b"][layer])])
                for t in range(tiles + 2):
                    if t < tiles:
                        if t >= 2:
                            sp.wait_ge(summing, SUM * (t - 2) + 3)
                        sp.dma_start(x[t % 2][:, :], dr["x"][t * P:(t + 1) * P, :]).then_inc(x_in[t % 2], 16)
                    if t >= 2:
                        sp.wait_ge(x_ready, t - 1)
                        sp.dma_start(out(t - 2), xo[t % 2][:, :]).then_inc(stored[t % 2], 16)
                for b in range(2):
                    sp.wait_ge(stored[b], 16 * (tiles // 2))

            @block.gpsimd
            def _(pool):
                def gather(t):
                    for k, (dst, sem) in enumerate(((y1, y1_in), (y2, y2_in))):
                        if t >= 2:
                            if k == 0:
                                pool.wait_ge(weighed, t - 1)
                            else:
                                pool.wait_ge(summing, SUM * (t - 2) + 1)
                        pool.indirect_dma_start(dst[t % 2][:, :], None, dr["y"],
                                                bass.IndirectOffsetOnAxis(slots[:, k, t:t + 1], 0)).then_inc(sem[t % 2], 16)

                for t in range(3):
                    gather(t)
                pool.wait_ge(rows_in, ROWS_IN)
                for t in range(tiles):
                    if t + 3 < tiles:
                        gather(t + 3)
                    pool.wait_ge(scaling, SCALE * (t + 1))
                    if t >= 2:
                        pool.wait_ge(stored[t % 2], 16 * (t // 2))
                    nc.gpsimd.tensor_tensor(xo[t % 2][:, :], xg[t % 2][:, :], ln_b[:, :], ALU.add).then_inc(x_ready, 1)

            @block.scalar
            def _(act):
                def weigh(t):
                    b = t % 2
                    act.wait_ge(y1_in[b], 16 * (t // 2) + 16)
                    if t >= 2:
                        act.wait_ge(summing, SUM * (t - 2) + 1)
                    nc.scalar.activation(mixed[b][:, :], y1[b][:, :], ACT.Copy, scale=weights[:, 0, t:t + 1]).then_inc(weighed, 1)

                weigh(0)
                for t in range(tiles):
                    b = t % 2
                    if t + 1 < tiles:
                        weigh(t + 1)
                    act.wait_ge(summing, SUM * (t + 1))
                    nc.scalar.activation(root[b][:, :], var[b][:, :], ACT.Sqrt).then_inc(rooted, 1)
                    act.wait_ge(scaling, SCALE * t + 2)
                    nc.scalar.activation(xn[b][:, :], res[b][:, :], ACT.Identity, bias=bias[b][:, :], scale=rstd[b][:, :]).then_inc(normed, 1)

            @block.vector
            def _(dve):
                def scale_and_bias(t):
                    b, own = t % 2, Chain(dve, scaling, SCALE * t)
                    dve.wait_ge(rooted, t + 1)
                    own.link(nc.vector.reciprocal(rstd[b][:, :], root[b][:, :]))
                    own.inc(nc.vector.tensor_scalar(bias[b][:, :], mv[b][:, 0:1], rstd[b][:, :], -1.0, ALU.mult, ALU.mult))

                def gain(t):
                    b = t % 2
                    dve.wait_ge(normed, t + 1)
                    if t >= 2:
                        dve.wait_ge(x_ready, t - 1)
                    nc.vector.tensor_tensor(xg[b][:, :], xn[b][:, :], ln_g[:, :], ALU.mult).then_inc(scaling, 1)

                dve.wait_ge(rows_in, ROWS_IN)
                for t in range(tiles):
                    s, b, n = t // NT_X, t % 2, 16 * (t // 2) + 16
                    own = Chain(dve, summing, SUM * t)
                    dve.wait_ge(weighed, t + 1)
                    dve.wait_ge(y2_in[b], n)
                    own.link(nc.vector.scalar_tensor_tensor(both[:, :], y2[b][:, :], weights[:, 1, t:t + 1], mixed[b][:, :], ALU.mult, ALU.add))
                    if t:
                        scale_and_bias(t - 1)
                    own.link(nc.vector.tensor_tensor(gated[:, :], both[:, :], gate[s][:, :], ALU.mult))
                    dve.wait_ge(x_in[b], n)
                    own.link(nc.vector.scalar_tensor_tensor(res[b][:, :], x[b][:, :], ALPHA, gated[:, :], ALU.mult, ALU.add))
                    for c in range(2):
                        own.inc(nc.vector.bn_stats(stats[b][:, c, :], res[b][:, c * BANK:(c + 1) * BANK]))
                    own.wait()
                    st.settle(dve)
                    own.link(nc.vector.bn_aggr(mv[b][:, :], stats[b][:, :, :].rearrange("p n s -> p (n s)")))
                    own.link(nc.vector.tensor_scalar(var[b][:, :], mv[b][:, 1:2], LN_EPS, None, ALU.add))
                    assert own.n == SUM
                    if t:
                        gain(t - 1)
                scale_and_bias(tiles - 1)
                gain(tiles - 1)


INPUTS = ["x", "c", "ctx", "c_ctx", "ada_w", "ada_b", "ln_mix_g", "ln_mix_b", "ln_ffn_g", "ln_ffn_b",
          "win_w_in", "win_w_out", "win_sink", "mla_w_in", "mla_q_norm", "mla_kv_norm", "mla_w_uq", "mla_w_ukv",
          "mla_w_out", "moe_w_grp", "moe_b_grp", "moe_w_rt", "moe_b_rt", "moe_w_gate", "moe_w_up", "moe_w_down"]


def program(nc, io, const_dram, const_cols, result):
    nb = n_blocks(NT_ALL)
    dr = {name: nc.dram_tensor(f"scratch_{name}", shape, dt, kind="Internal").ap() for name, shape, dt in (
        ("x", (TALL, D), F32), ("mod", (2, 2, 6 * D), F32), ("qkT", (A_QK_CHUNKS * P, TALL), F32), ("o", (TALL, D), F32),
        ("h", (TALL, D), F32), ("table", (P * nb, 1), I32), ("y", ((nb + 2) * P, D), F32))}

    def constants(st, names):
        tiles = {n: st.sb(n, [P, const_cols[n][1]]) for n in names}
        loaded = st.sem("loaded")
        with nc.Block() as block:

            @block.sync
            def _(sp):
                for n in names:
                    at, size = const_cols[n]
                    sp.dma_start(tiles[n][:, :], const_dram[:, at:at + size]).then_inc(loaded, 16)
                sp.wait_ge(loaded, 16 * len(names))

        return tiles

    with Stage(nc, "all") as every:
        Stage.settled = every.sem("settled")
        Stage.pool_dma = every.stack
        fixed = constants(every, ["ident", "ones"])
        const = lambda n: fixed[n][:, :]
        stage_mods(nc, io, dr, const)

        def feed_forward(layer, tiles, w_out, out):
            with Stage(nc, f"ff{layer}") as ff:
                logits = ff.sb("logits", [P, tiles * ROUTE])
                weights = ff.sb("weights", [P, 2, tiles])
                slots = ff.sb("slots", [P, 2, tiles], I32)
                block_info = ff.sb("block_info", [P, n_blocks(tiles) + 4], I32)
                tokens = ff.sb("tokens", [P, n_blocks(tiles) + 4], I32)
                stage_project_out(nc, io, dr, const, layer, w_out, tiles, logits)
                with Stage(nc, f"routing{layer}") as rt:
                    tables = constants(rt, ["before", "iota_e", "iota_g", "steps", "iota_b", "token"])
                    routing = lambda n: (tables[n] if n in tables else fixed[n])[:, :]
                    stage_route(nc, dr, routing, layer, tiles, logits, weights, slots, block_info, tokens)
                stage_experts(nc, io, dr, const, layer, tiles, block_info, tokens)
                stage_combine(nc, io, dr, const, layer, tiles, weights, slots, out)

        with Stage(nc, "layer0") as l0:
            v_all = l0.sb("v_all", [P, NT_ALL, A_KV, A_HD + 1])
            with Stage(nc, "layer0_qkv") as lq:
                hT = lq.sb("hT", [P, KD, TALL])
                stage_transposed(nc, dr, const, hT, 0)
                tables = constants(lq, ["rot_a", "cos_a", "sin_a"])
                stage_window_qkv(nc, io, dr, lambda n: tables[n][:, :], hT, v_all)
            with Stage(nc, "layer0_att") as la:
                tables_m = constants(la, ["mask"])
                window = lambda n: (tables_m[n] if n in tables_m else fixed[n])[:, :]
                stage_window_attention(nc, io, dr, window, v_all)
        feed_forward(0, NT_ALL, io["win_w_out"][0], lambda t: dr["x"][t * P:(t + 1) * P, :])

        with Stage(nc, "layer1") as l1:
            tables_b = constants(l1, ["rot_b", "cos_b", "sin_b", "cos_k", "sin_k"])
            latent = lambda n: (tables_b[n] if n in tables_b else fixed[n])[:, :]
            cqT = l1.sb("cqT", [P, B_QR // P, SEQ])
            ckvT = l1.sb("ckvT", [P, B_KVR // P, TALL])
            kT = [l1.sb(f"kT{b}", [B_QD + 1, TALL]) for b in range(2)]
            stage_latents(nc, io, dr, latent, cqT, ckvT, kT)
            stage_latent_attention(nc, io, dr, latent, cqT, ckvT, kT)
        feed_forward(1, NT_X, io["mla_w_out"][0], lambda t: result[0, t * P:(t + 1) * P, :])


def kernel(**inputs):
    import concourse.bacc as bacc
    from concourse.bass_utils import run_bass_kernel_spmd

    nc = bacc.Bacc("TRN2", target_bir_lowering=False, num_devices=1)
    arrays, io = {}, {}
    for name in INPUTS:
        a = np.ascontiguousarray(inputs[name])
        arrays[f"in_{name}"] = a
        io[name] = nc.dram_tensor(f"in_{name}", a.shape, mybir.dt.from_np(a.dtype), kind="ExternalInput").ap()
    table, cols = constant_arrays()
    arrays["in_tables"] = table
    const_dram = nc.dram_tensor("in_tables", table.shape, F32, kind="ExternalInput").ap()
    result = nc.dram_tensor("out_x", (1, SEQ, D), F32, kind="ExternalOutput").ap()
    program(nc, io, const_dram, cols, result)
    return run_bass_kernel_spmd(nc, [arrays], core_ids=[0]).results[0]["out_x"]
```
